# Optimizing a Trainium2 kernel written in Bass

```python
import jax, jax.numpy as jnp
from jax import lax
import numpy as np

D_MODEL = 1024
BATCH = 1
SEQ = 256
DEPTH = 1
DEC_BATCH = 8
DEC_SEQ = 1
PAST_LEN = 2048
PAGE_SIZE = 128

D_MIX = D_MODEL
D_A = D_MIX // 2
HEAD_DIM_A = 64
N_HEADS_A = D_A // HEAD_DIM_A
D_B = D_MIX - D_A
N_BLOCKS_B = 8
BLOCK_B = D_B // N_BLOCKS_B
CONV_W = 4
LRU_C = 8.0
R_DECAY = 64
R_AAA = 64
R_GATE = 128
N_COLS_A = 3 * D_A + R_DECAY + R_AAA + R_GATE
N_COLS_B = 2 * D_B
N_COLS = N_COLS_A + N_COLS_B
N_EXPERTS = 32
TOP_K = 4
D_FF = D_MODEL
SWIGLU_LIMIT = 7.0
SWIGLU_ALPHA = 1.702
MOE_BLOCK = 128
RMS_EPS = 1e-6
LN_X_EPS = 64e-5
N_MOD = 6

kernel_name = "hymba_rwkv7_rglru_moe_adaln_step"

F32 = jnp.float32

def rmsnorm(x, g):
    xf = x.astype(F32)
    y = xf * lax.rsqrt(jnp.mean(xf * xf, axis=-1, keepdims=True) + RMS_EPS)
    return y * g.astype(F32)

def wkv_scan(S0, r, w, k, v, kk, a):
    xs = tuple(jnp.moveaxis(t, 1, 0) for t in (r, w, k, v, kk, a))

    def step(S, inp):
        r_t, w_t, k_t, v_t, kk_t, a_t = inp
        sa = jnp.einsum('bhij,bhj->bhi', S, -kk_t)
        S = (S * w_t[:, :, None, :] + sa[..., None] * (kk_t * a_t)[:, :, None, :]
             + v_t[..., None] * k_t[:, :, None, :])
        y = jnp.einsum('bhij,bhj->bhi', S, r_t)
        return S, y

    S, ys = lax.scan(step, S0, xs)
    return S, jnp.moveaxis(ys, 0, 1)

def rwkv7_group(pa, shift0, wkv0, p):
    B, T, _ = pa.shape
    paf = pa.astype(F32)
    prev = jnp.concatenate([shift0.astype(F32)[:, None, :], paf[:, :-1]], axis=1)
    z = paf + (prev - paf) * p['rk_mu'].astype(F32)
    new_shift = paf[:, -1]
    idx = [D_A, 2 * D_A, 3 * D_A, 3 * D_A + R_DECAY, 3 * D_A + R_DECAY + R_AAA]
    r, k, v, wd, ad, gd = jnp.split(z, idx, axis=-1)
    w_log = -jax.nn.softplus(-(p['rk_w0'] + jnp.tanh(wd) @ p['rk_w_up'])) - 0.5
    decay = jnp.exp(-jnp.exp(w_log))
    a = jax.nn.sigmoid(p['rk_a0'] + ad @ p['rk_a_up'])
    g = jax.nn.sigmoid(gd) @ p['rk_g_up']
    kk = k * p['rk_k_k']
    hd = lambda t: t.reshape(B, T, N_HEADS_A, HEAD_DIM_A)
    kk_h = hd(kk)
    kk_h = kk_h / jnp.maximum(jnp.sqrt(jnp.sum(kk_h * kk_h, axis=-1, keepdims=True)), 1e-12)
    k = k * (1.0 + (a - 1.0) * p['rk_k_a'])
    r_h, k_h, v_h, w_h, a_h = hd(r), hd(k), hd(v), hd(decay), hd(a)
    S, y = wkv_scan(wkv0.astype(F32), r_h, w_h, k_h, v_h, kk_h, a_h)
    mu = jnp.mean(y, axis=-1, keepdims=True)
    var = jnp.mean((y - mu) ** 2, axis=-1, keepdims=True)
    yn = ((y - mu) * lax.rsqrt(var + LN_X_EPS)).reshape(B, T, D_A) * p['rk_lnx_w'] + p['rk_lnx_b']
    bonus = (jnp.sum(r_h * k_h * p['rk_r_k'], axis=-1, keepdims=True) * v_h).reshape(B, T, D_A)
    out = (yn + bonus) * g
    return out, new_shift, S

def rglru_group(pb, conv0, h0, p):
    B, T, _ = pb.shape
    pbf = pb.astype(F32)
    yb, xb = jnp.split(pbf, 2, axis=-1)
    xpad = jnp.concatenate([conv0.astype(F32), xb], axis=1)
    cw = p['lru_conv_w'].astype(F32)
    xc = p['lru_conv_b'] + sum(cw[j] * xpad[:, j:j + T] for j in range(CONV_W))
    new_conv = xpad[:, -(CONV_W - 1):]
    xblk = xc.reshape(B, T, N_BLOCKS_B, BLOCK_B)
    gate_r = jax.nn.sigmoid(jnp.einsum('btnc,ncd->btnd', xblk, p['lru_w_r']).reshape(B, T, D_B) + p['lru_b_r'])
    gate_i = jax.nn.sigmoid(jnp.einsum('btnc,ncd->btnd', xblk, p['lru_w_i']).reshape(B, T, D_B) + p['lru_b_i'])
    log_a = -LRU_C * gate_r * jax.nn.softplus(-p['lru_lambda'].astype(F32))
    a_t = jnp.exp(log_a)
    b_t = jnp.sqrt(-jnp.expm1(2.0 * log_a)) * (gate_i * xc)
    b_t = b_t.at[:, 0].add(a_t[:, 0] * h0.astype(F32))

    def combine(e1, e2):
        a1, x1 = e1
        a2, x2 = e2
        return a1 * a2, a2 * x1 + x2

    _, h = lax.associative_scan(combine, (a_t, b_t), axis=1)
    out = rmsnorm(h * jax.nn.gelu(yb), p['lru_norm_g'])
    return out, new_conv, h[:, -1]

def moe_ffn(h, p):
    N = h.shape[0]
    logits = h.astype(F32) @ p['router_w'].astype(F32) + p['router_b'].astype(F32)
    top_v, top_i = lax.top_k(logits, TOP_K)
    gates = jax.nn.softmax(top_v, axis=-1)
    NK = N * TOP_K
    flat_e = top_i.reshape(NK)
    flat_tok = jnp.arange(NK, dtype=jnp.int32) // TOP_K
    flat_g = gates.reshape(NK)
    order = jnp.argsort(flat_e)
    e_sorted = flat_e[order]
    counts = jnp.bincount(flat_e, length=N_EXPERTS)
    padded = (counts + MOE_BLOCK - 1) // MOE_BLOCK * MOE_BLOCK
    pad_end = jnp.cumsum(padded)
    pad_start = pad_end - padded
    start = jnp.cumsum(counts) - counts
    dest = pad_start[e_sorted] + (jnp.arange(NK) - start[e_sorted])
    n_blocks = -(-NK // MOE_BLOCK) + N_EXPERTS
    n_rows = n_blocks * MOE_BLOCK
    row_tok = jnp.zeros((n_rows,), jnp.int32).at[dest].set(flat_tok[order])
    row_gate = jnp.zeros((n_rows,), F32).at[dest].set(flat_g[order])
    block_e = jnp.minimum(jnp.searchsorted(pad_end, jnp.arange(n_blocks) * MOE_BLOCK, side='right'),
                          N_EXPERTS - 1)

    def expert_block(args):
        e, toks = args
        xb = h[toks].astype(F32)
        gt = xb @ p['w_gate'][e] + p['b_gate'][e]
        up = xb @ p['w_up'][e] + p['b_up'][e]
        gt = jnp.minimum(gt, SWIGLU_LIMIT)
        up = jnp.clip(up, -SWIGLU_LIMIT, SWIGLU_LIMIT)
        glu = gt * jax.nn.sigmoid(gt * SWIGLU_ALPHA)
        return ((up + 1.0) * glu) @ p['w_down'][e] + p['b_down'][e]

    out = lax.map(expert_block, (block_e, row_tok.reshape(n_blocks, MOE_BLOCK)))
    y = jnp.zeros((N, D_MODEL), F32).at[row_tok].add(out.reshape(n_rows, D_MODEL).astype(F32) * row_gate[:, None])
    return y

def decoder_layer(x, c, st_wkv, st_shift, st_conv, st_lru, p):
    B, T, D = x.shape
    mod = (jax.nn.silu(c.astype(F32)) @ p['w_ada'] + p['b_ada']).reshape(B, N_MOD, D)
    shift1, scale1, gate1, shift2, scale2, gate2 = (mod[:, i, None, :] for i in range(N_MOD))
    h = rmsnorm(x, p['norm1_g']) * (1.0 + scale1) + shift1
    proj = h @ p['w_in']
    ya, new_shift, new_wkv = rwkv7_group(proj[..., :N_COLS_A], st_shift, st_wkv, p)
    yb, new_conv, new_lru = rglru_group(proj[..., N_COLS_A:], st_conv, st_lru, p)
    mixed = jnp.concatenate([ya, yb], axis=-1) @ p['w_out']
    x = (x.astype(F32) + gate1 * mixed).astype(x.dtype)
    h2 = rmsnorm(x, p['norm2_g']) * (1.0 + scale2) + shift2
    ff = moe_ffn(h2.reshape(B * T, D), p).reshape(B, T, D)
    x = (x.astype(F32) + gate2 * ff).astype(x.dtype)
    dt = x.dtype
    return x, (new_wkv.astype(dt), new_shift.astype(dt), new_conv.astype(dt), new_lru.astype(dt))

def setup_inputs(seed: int = 0) -> dict:
    key = jax.random.key(seed)
    ks = iter(jax.random.split(key, 64))

    def nrm(shape, scale):
        return scale * jax.random.normal(next(ks), shape, F32)

    def unif(shape, lo, hi):
        return jax.random.uniform(next(ks), shape, F32, lo, hi)

    L = DEPTH
    u = unif((L, D_B), 0.9, 0.999) ** (1.0 / LRU_C)
    return {
        'x_prompt': nrm((BATCH, SEQ, D_MODEL), 1.0),
        'x_sample': nrm((DEC_BATCH, DEC_SEQ, D_MODEL), 1.0),
        'c_prompt': nrm((BATCH, D_MODEL), 1.0),
        'c_sample': nrm((DEC_BATCH, D_MODEL), 1.0),
        'state_wkv': nrm((L, DEC_BATCH, N_HEADS_A, HEAD_DIM_A, HEAD_DIM_A), 0.3),
        'state_shift': nrm((L, DEC_BATCH, N_COLS_A), 1.0),
        'state_conv': nrm((L, DEC_BATCH, CONV_W - 1, D_B), 1.0),
        'state_lru': nrm((L, DEC_BATCH, D_B), 0.5),
        'w_ada': nrm((L, D_MODEL, N_MOD * D_MODEL), 0.5 * D_MODEL ** -0.5),
        'b_ada': nrm((L, N_MOD * D_MODEL), 0.02),
        'norm1_g': 1.0 + nrm((L, D_MODEL), 0.05),
        'norm2_g': 1.0 + nrm((L, D_MODEL), 0.05),
        'w_in': nrm((L, D_MODEL, N_COLS), D_MODEL ** -0.5),
        'rk_mu': unif((L, N_COLS_A), 0.0, 1.0),
        'rk_w0': unif((L, D_A), -6.0, 1.0),
        'rk_w_up': nrm((L, R_DECAY, D_A), 0.1 * R_DECAY ** -0.5),
        'rk_a0': nrm((L, D_A), 0.1),
        'rk_a_up': nrm((L, R_AAA, D_A), 0.1 * R_AAA ** -0.5),
        'rk_g_up': nrm((L, R_GATE, D_A), R_GATE ** -0.5),
        'rk_k_k': 0.85 + nrm((L, D_A), 0.05),
        'rk_k_a': 1.0 + nrm((L, D_A), 0.05),
        'rk_r_k': nrm((L, N_HEADS_A, HEAD_DIM_A), 0.1),
        'rk_lnx_w': 1.0 + nrm((L, D_A), 0.05),
        'rk_lnx_b': nrm((L, D_A), 0.02),
        'lru_conv_w': nrm((L, CONV_W, D_B), 0.5),
        'lru_conv_b': nrm((L, D_B), 0.02),
        'lru_w_r': nrm((L, N_BLOCKS_B, BLOCK_B, BLOCK_B), BLOCK_B ** -0.5),
        'lru_b_r': nrm((L, D_B), 0.02),
        'lru_w_i': nrm((L, N_BLOCKS_B, BLOCK_B, BLOCK_B), BLOCK_B ** -0.5),
        'lru_b_i': nrm((L, D_B), 0.02),
        'lru_lambda': jnp.log(u) - jnp.log1p(-u),
        'lru_norm_g': 1.0 + nrm((L, D_B), 0.05),
        'w_out': nrm((L, D_MIX, D_MODEL), D_MIX ** -0.5),
        'router_w': nrm((L, D_MODEL, N_EXPERTS), D_MODEL ** -0.5),
        'router_b': nrm((L, N_EXPERTS), 0.01),
        'w_gate': nrm((L, N_EXPERTS, D_MODEL, D_FF), D_MODEL ** -0.5),
        'b_gate': nrm((L, N_EXPERTS, D_FF), 0.02),
        'w_up': nrm((L, N_EXPERTS, D_MODEL, D_FF), D_MODEL ** -0.5),
        'b_up': nrm((L, N_EXPERTS, D_FF), 0.02),
        'w_down': nrm((L, N_EXPERTS, D_FF, D_MODEL), D_FF ** -0.5),
        'b_down': nrm((L, N_EXPERTS, D_MODEL), 0.02),
        'final_g': 1.0 + nrm((D_MODEL,), 0.05),
    }

def reference(x_prompt, x_sample, c_prompt, c_sample, state_wkv, state_shift, state_conv, state_lru,
              w_ada, b_ada, norm1_g, norm2_g, w_in, rk_mu, rk_w0, rk_w_up, rk_a0, rk_a_up, rk_g_up,
              rk_k_k, rk_k_a, rk_r_k, rk_lnx_w, rk_lnx_b, lru_conv_w, lru_conv_b, lru_w_r, lru_b_r,
              lru_w_i, lru_b_i, lru_lambda, lru_norm_g, w_out, router_w, router_b, w_gate, b_gate,
              w_up, b_up, w_down, b_down, final_g):
    yp, ys = x_prompt, x_sample
    Bp = x_prompt.shape[0]
    dt = x_prompt.dtype
    wkv_p, shift_p, conv_p, lru_p = [], [], [], []
    wkv_s, shift_s, conv_s, lru_s = [], [], [], []
    for l in range(DEPTH):
        lp = dict(w_ada=w_ada[l], b_ada=b_ada[l], norm1_g=norm1_g[l], norm2_g=norm2_g[l], w_in=w_in[l],
                  rk_mu=rk_mu[l], rk_w0=rk_w0[l], rk_w_up=rk_w_up[l], rk_a0=rk_a0[l], rk_a_up=rk_a_up[l],
                  rk_g_up=rk_g_up[l], rk_k_k=rk_k_k[l], rk_k_a=rk_k_a[l], rk_r_k=rk_r_k[l],
                  rk_lnx_w=rk_lnx_w[l], rk_lnx_b=rk_lnx_b[l], lru_conv_w=lru_conv_w[l],
                  lru_conv_b=lru_conv_b[l], lru_w_r=lru_w_r[l], lru_b_r=lru_b_r[l], lru_w_i=lru_w_i[l],
                  lru_b_i=lru_b_i[l], lru_lambda=lru_lambda[l], lru_norm_g=lru_norm_g[l], w_out=w_out[l],
                  router_w=router_w[l], router_b=router_b[l], w_gate=w_gate[l], b_gate=b_gate[l],
                  w_up=w_up[l], b_up=b_up[l], w_down=w_down[l], b_down=b_down[l])
        z_wkv = jnp.zeros((Bp, N_HEADS_A, HEAD_DIM_A, HEAD_DIM_A), dt)
        z_shift = jnp.zeros((Bp, N_COLS_A), dt)
        z_conv = jnp.zeros((Bp, CONV_W - 1, D_B), dt)
        z_lru = jnp.zeros((Bp, D_B), dt)
        yp, sp = decoder_layer(yp, c_prompt, z_wkv, z_shift, z_conv, z_lru, lp)
        ys, ss = decoder_layer(ys, c_sample, state_wkv[l], state_shift[l], state_conv[l], state_lru[l], lp)
        wkv_p.append(sp[0]); shift_p.append(sp[1]); conv_p.append(sp[2]); lru_p.append(sp[3])
        wkv_s.append(ss[0]); shift_s.append(ss[1]); conv_s.append(ss[2]); lru_s.append(ss[3])
    y_prompt = rmsnorm(yp, final_g).astype(dt)
    y_sample = rmsnorm(ys, final_g).astype(x_sample.dtype)
    return (y_prompt, y_sample,
            jnp.stack(wkv_p), jnp.stack(shift_p), jnp.stack(conv_p), jnp.stack(lru_p),
            jnp.stack(wkv_s), jnp.stack(shift_s), jnp.stack(conv_s), jnp.stack(lru_s))


_drawn_inputs = setup_inputs


def setup_inputs(seed=0):
    import zlib

    import numpy as np

    out = dict(_drawn_inputs(seed))
    spreads = {}
    factors = {'rk_w_up': 7.177,
     'rk_lnx_w': 6.117,
     'rk_lnx_b': 30.555,
     'lru_b_r': 8.0,
     'lru_b_i': 7.04,
     'lru_norm_g': 2.922,
     'router_b': 14.6,
     'b_gate': 23.947,
     'b_up': 32.2,
     'b_down': 23.594,
     'norm2_g': 2.782}
    for name, (base, spread) in spreads.items():
        noise = np.random.default_rng([zlib.crc32(name.encode()), seed]).standard_normal(out[name].shape)
        drawn = base * np.exp(spread * noise) if base else spread * noise
        out[name] = __import__('jax').numpy.asarray(drawn.astype(out[name].dtype))
    for name, factor in factors.items():
        out[name] = (out[name] * factor).astype(out[name].dtype)
    return out
```

```python
from contextlib import ExitStack

import numpy as np

import concourse.bass as bass
from concourse import mybir
from concourse.alu_op_type import AluOpType as ALU

F32 = mybir.dt.float32
I32 = mybir.dt.int32
ACT = mybir.ActivationFunctionType
AX = mybir.AxisListType.X

P = 128
D = 1024
DC = D // P
T = 256
NB = 8
NT = T + NB
DA = 512
Q = DA // P
HN = 64
H = DA // HN
MA = 14
MP = 22
NROW = NB + 1
EXP_HALF = float(np.exp(-0.5))
CH = 64
LEVELS = CH.bit_length() - 1
CPT = P // CH
NCH = T // CH
E = 32
SLOTS = 64
OVER = 4
NPAR = 94

PARAMS = [("rk_mu", 14), ("rk_w0", 4), ("rk_a0", 4), ("rk_k_k", 4), ("rk_k_a", 4), ("rk_r_k", 4),
          ("rk_lnx_w", 4), ("rk_lnx_b", 4), ("lru_conv_w", 16), ("lru_conv_b", 4), ("lru_b_r", 4),
          ("lru_b_i", 4), ("lru_lambda", 4), ("lru_norm_g", 4), ("norm1_g", 8), ("norm2_g", 8)]
PAT = {}
for _n, _k in PARAMS:
    PAT[_n] = sum(k for _, k in PARAMS[:len(PAT)])

UNITS = ([("ada", 512 * j, 512) for j in range(4)]
         + [("win", 1792, 512), ("win", 2304, 512)]
         + [("win", 0, 512), ("win", 512, 512), ("win", 1024, 512), ("win", 1536, 256)]
         + [("ada", 512 * j, 512) for j in range(4, 12)])
FR = 3


def job_list():
    jobs = [(("t", n), 1) for n in ("c", "prm", "bada", "shift", "conv", "lru")]
    jobs += [(("xT", c), 1) for c in range(DC)]
    for j in range(4):
        jobs += [(("ada", j), 1), (("adaT", j), 1)]
    jobs += [(("proj", m), 1) for m in range(14, 18)]
    jobs += [(("proj", m), 2) for m in range(18, 22)]
    jobs += [(("proj", m), 2) for m in range(0, 4)]
    for c in range(Q):
        jobs += [(("gr", c), 1), (("gi", c), 1)]
    jobs += [(("proj", m), 2) for m in range(4, MA)]
    for j in range(4, 12):
        jobs += [(("ada", j), 1), (("adaT", j), 1)]
    jobs += [(("ssB",), 1)]
    jobs += [((k, q), 1) for k in ("lw", "la", "lg", "kn") for q in range(Q)]
    jobs += [(("smpT", 0), 1), (("smpT", 1), 1), (("smpB",), 1)]
    jobs += [(("bo", q), 1) for q in range(Q)]
    for t in range(2):
        jobs += [(("tk", t, k), 1) for k in range(4)]
        jobs += [((k, t, g), 1) for k in ("U", "L", "Ak", "Rb", "Rk") for g in range(2)]
        for l in range(1, LEVELS):
            jobs += [(("Y", t, g, l), 1) for g in range(2)]
            if l < LEVELS - 1:
                jobs += [(("X", t, g, l), 1) for g in range(2)]
            jobs += [(("XT", t, g, l), 1) for g in range(2)]
        jobs += [((k, t, g), 1) for k in ("LV", "Z", "AH") for g in range(2)]
        for c in range(CPT * t, CPT * (t + 1)):
            jobs += [(("SA", c, 0), 1), (("SA", c, 1), 1), (("SU", c), 1)]
        jobs += [(("Y1", t), 1), (("Y2", t), 1)]
    jobs += [(("syT",), 4)]
    jobs += [(("wkv",), 1)]
    jobs += [((k, q), 1) for k in ("mu", "va") for q in range(Q)]
    jobs += [(("so", n), 1) for n in range(3)]
    for c in range(DC):
        jobs += [(("x2", c), 1), (("mo", c), 2)]
    jobs += [(("ss2",), 1)]
    jobs += [(("lg2", t), 1) for t in range(3)]
    jobs += [(("rank",), 2), (("cnt",), 1)]
    jobs += [(("h2", t, c), 1) for t in range(3) for c in range(2)]
    jobs += [(("g2", c), 1) for c in range(2)]
    return jobs


def build(nc, I, O):
    ctx = ExitStack()
    with ctx:
        mem = ctx.enter_context(nc.sbuf_tensor("mem", [P, 53000], F32))
        cnt_i = ctx.enter_context(nc.sbuf_tensor("cnt_i", [1, (OVER + 1) * E + 32], I32))
        ps = [ctx.enter_context(nc.psum_tensor(f"ps{b}", [P, 512], F32)) for b in range(8)]
        x1_dram = nc.dram_tensor("x1_scratch", (P, DC * NT), F32, kind="Internal").ap()

        def view(at, *dims):
            n = int(np.prod(dims))
            flat = mem[:, at:at + n]
            if len(dims) == 1:
                return flat
            names = "abcd"[:len(dims)]
            return flat.rearrange(f"p ({' '.join(names)}) -> p {' '.join(names)}",
                                  **{k: v for k, v in zip(names[1:], dims[1:])})

        class Region:

            def __init__(self, at, end):
                self.at, self.end = at, end

            def take(self, *dims):
                v = view(self.at, *dims)
                self.at += int(np.prod(dims))
                assert self.at <= self.end, (self.at, self.end)
                return v

        keep = Region(49600, 53000)
        ident = keep.take(128)
        ones = keep.take(128)
        iota = keep.take(128)
        prm = keep.take(96)
        modT = keep.take(6 * DC, NROW)
        gatew = keep.take(3, E)
        rankb = keep.take(3, (OVER + 1) * E)
        sel9 = keep.take(NT)
        gate2 = keep.take(D)
        tri = keep.take(128)
        small = keep.take(64)
        eps1, epsx = (small[:, k:k + 1] for k in range(2))
        ssq, rstd = small[:, 8:11], small[:, 12:15]
        squares = view(20480, D)
        wslot = [view(8192 * s, DC, D) for s in range(4)]
        moe = Region(32768, 49600)
        x1T = moe.take(DC, NT)
        h2T = moe.take(DC, NT)
        y = view(32768, 2, D)
        y_s = view(32768 + 2 * D, 512)
        h2tok = moe.take(3, D)
        xre = h2tok
        Xg, XTg, g_sb, sg_sb, u_sb, a_sb, aT_sb, o_sb = (moe.take(512) for _ in range(8))
        bg, bu = moe.take(D), moe.take(D)
        Psel = [moe.take(3, 128) for _ in range(2)]
        PTz = [moe.take(NT) for _ in range(2)]
        selb = [moe.take(64) for _ in range(2)]
        bd = view(24576, D)
        fslot = [view(4096 * s, DC, 512) for s in range(FR)]
        inv = Region(0, 12288)
        U, X, Y, Ak, XT = (inv.take(8, 128) for _ in range(5))
        Rb, Rk = inv.take(16, 128), inv.take(16, 128)
        Stmp = inv.take(2048)
        sv = inv.take(6, 128)
        wout = view(12288, DC, D)
        dead = Region(12288, 20480)
        z = dead.take(MA, NT)
        sigw, cum, aa, kk = (dead.take(Q, NT) for _ in range(4))
        mid = Region(20480, 32768)
        hT = mid.take(DC, NT)
        mixT = hT
        arp = mid.take(Q, 2, 2, 128)
        bm, kap = mid.take(Q, T), mid.take(Q, T)
        sqy, rsy = view(20480 + 2112, Q, NT), view(20480 + 2112 + 2048, Q, NT)
        W, gg, yT = mid.take(Q, NT), mid.take(Q, NT), mid.take(Q, NT)
        bv = W
        S = mid.take(2048)
        segm = mid.take(NT)
        smp = mid.take(6, Q, NB)
        ar2 = Region(32768, 49600)
        xflat = ar2.take(Q, 292)
        xc, gb, gr, gi, aB = (ar2.take(Q, NT) for _ in range(5))
        xtok = ar2.take(3, D)
        al = Region(32768, ar2.at)
        tok = [al.take(2, DA) for _ in range(4)]
        Z, ahT, SA = al.take(2, DA), al.take(Q, T), al.take(2, DA)
        ST = al.take(NCH + 1, Q, HN)
        LV = ar2.take(8, HN)
        diag = view(ar2.at - 512, 3, 128)
        bones, m_su, m_iu, mU0 = (ar2.take(128) for _ in range(4))
        mL = [ar2.take(128) for _ in range(LEVELS)]
        sel4 = ar2.take(4, 128)
        svb = ar2.take(352)
        lora = ar2.take(2, DA)
        wbd = [ar2.take(Q, 128) for _ in range(2)]
        rows = {n: ar2.take(128) for n in ("c", "prm", "bada", "shift", "conv", "lru")}
        nrows = {"c": 72, "prm": NPAR, "bada": 48, "shift": 112, "conv": 96, "lru": 32}
        cT = ar2.take(DC, 32)
        badaT, shiftT, h0T = ar2.take(48), ar2.take(NB, MA), ar2.take(NB, Q)
        adar = ar2.take(128)
        A1 = ar2.take(DC, NROW)
        omm, omka, sp = ar2.take(MA), ar2.take(Q), ar2.take(8, Q)
        so = [ar2.take(NROW, MA), ar2.take(108), ar2.take(36)]
        nso = [126, 108, 36]
        sorow = [rows["prm"], rows["bada"], rows["shift"]]
        wkvp = rows["conv"]
        late = Region(0, 12288)
        x2 = late.take(DC, NT)
        sq2 = late.take(DC, NT)
        rs2 = late.take(NT)
        A2 = late.take(DC, NROW)
        rw = late.take(DC, E)
        rb = late.take(E)
        lgt, ex, msk, msk2, eq, ce = (late.take(3, E) for _ in range(6))
        top, sc = late.take(3, 8), late.take(3, 8)
        rcp = late.take(3, 8)
        wkvo = late.take(Q, 128)
        lbase = late.take(E)
        fin = Region(0, 8192)
        x1o = fin.take(DC, NT)
        fing = fin.take(D)
        x1t = view(24576, 3, D)
        gt = view(24576 + 3072, 3, D)

        sems = {}

        def sem(name):
            if name not in sems:
                sems[name] = ctx.enter_context(nc.semaphore(name))
            return sems[name]

        bank_full = [sem(f"bank_full{b}") for b in range(8)]
        bank_out = [sem(f"bank_out{b}") for b in range(8)]
        jobs = job_list()
        where, taken = {}, [0] * 8
        for k, (name, n) in enumerate(jobs):
            before = taken[k % 8]
            taken[k % 8] += n
            where[name] = (k % 8, k // 8 + 1, before, taken[k % 8])

        def bank(*name):
            return ps[where[name][0]]

        def wait_full(eng, *name):
            b, n, _, _ = where[name]
            eng.wait_ge(bank_full[b], n)

        def wait_out(eng, *name):
            b, _, _, n = where[name]
            eng.wait_ge(bank_out[b], n)

        count = {}

        def signal(eng, ins, name):
            count[name] = count.get(name, 0) + 1
            ins.then_inc(sem(name), 1)
            eng.wait_ge(sem(name), count[name])

        def ring(n):
            return sem(f"front_loaded{n % FR}"), 16 * (n // FR + 1)

        for n in ("lanes_done", "act_done", "pool_done"):
            sem(n)
        block = ctx.enter_context(nc.Block())

        def vcol(name, k=0):
            return prm[:, PAT[name] + k:PAT[name] + k + 1]

        def mod(i, c, rows_):
            return modT[:, i * DC + c, rows_]

        @block.sync
        def _(sp_):
            def rows_in(dst, src):
                sp_.dma_start(dst, src).then_inc(sem("ld_rows"), 16)

            rows_in(rows["c"][0:8, :], I["c_prompt"].rearrange("a (c p) -> (a c) p", p=P))
            rows_in(rows["c"][8:72, :], I["c_sample"].rearrange("a (c p) -> (a c) p", p=P))
            rows_in(rows["bada"][0:48, :], I["b_ada"].rearrange("a (c p) -> (a c) p", p=P))
            rows_in(rows["shift"][0:112, :], I["state_shift"].rearrange("l b (c p) -> (l b c) p", p=P))
            rows_in(rows["conv"][0:96, :], I["state_conv"].rearrange("l b w (c p) -> (l b w c) p", p=P))
            rows_in(rows["lru"][0:32, :], I["state_lru"].rearrange("l b (c p) -> (l b c) p", p=P))
            sp_.dma_start(xtok[:, 0:2, :], I["x_prompt"].rearrange("a (t p) d -> p (a t) d", p=P))\
               .then_inc(sem("ld_x"), 16)
            sp_.dma_start(xtok[0:NB, 2, :], I["x_sample"].rearrange("b a d -> (b a) d"))\
               .then_inc(sem("ld_x"), 16)

            last_job = {0: ("ada", 0), 1: ("ada", 1), 2: ("ada", 2), 3: ("ada", 3),
                        4: ("proj", 17), 5: ("proj", 21), 6: ("proj", 3), 7: ("proj", 7),
                        8: ("proj", 11), 9: ("proj", 13)}
            last_job.update({10 + j: ("ada", 4 + j) for j in range(8)})
            src = {"ada": I["w_ada"], "win": I["w_in"]}
            for n, (what, c0, w) in enumerate(UNITS):
                if n >= FR:
                    wait_full(sp_, *last_job[n - FR])
                sp_.dma_start(fslot[n % FR][:, :, 0:w],
                              src[what][0, :, c0:c0 + w].rearrange("(c p) n -> p c n", p=P))\
                   .then_inc(sem(f"front_loaded{n % FR}"), 16)
            wait_out(sp_, "tk", 1, 3)
            wait_out(sp_, "bo", 3)
            sp_.wait_ge(sem("vectors_done"), 1)
            sp_.dma_start(wout[:, :, :], I["w_out"][0].rearrange("(c p) n -> p c n", p=P))\
               .then_inc(sem("ld_wout"), 16)
            wait_out(sp_, "Y2", 1)
            sp_.dma_start(xre[:, 0:2, :], I["x_prompt"].rearrange("a (t p) d -> p (a t) d", p=P))\
               .then_inc(sem("ld_xre"), 16)
            sp_.dma_start(xre[0:NB, 2, :], I["x_sample"].rearrange("b a d -> (b a) d"))\
               .then_inc(sem("ld_xre"), 16)
            wait_full(sp_, "Y2", 1)
            sp_.dma_start(rw[:, :, :], I["router_w"][0].rearrange("(c p) n -> p c n", p=P))\
               .then_inc(sem("ld_router"), 16)
            sp_.dma_start(rb[0:1, :], I["router_b"]).then_inc(sem("ld_router"), 16)
            wait_out(sp_, "mo", DC - 1)
            wait_out(sp_, "so", 2)
            sp_.wait_ge(sem("states_out"), 16 * 8)
            sp_.dma_start(bg[0:E, :], I["b_gate"][0]).then_inc(sem("ld_bias"), 16)
            sp_.dma_start(bu[0:E, :], I["b_up"][0]).then_inc(sem("ld_bias"), 16)
            sp_.dma_start(bd[0:E, :], I["b_down"][0]).then_inc(sem("ld_bias"), 16)
            sp_.wait_ge(sem("x1_done"), 1)
            sp_.dma_start(x1_dram, x1T.rearrange("p c t -> p (c t)")).then_inc(sem("x1_out"), 16)

            mats = [I["w_gate"], I["w_up"], I["w_down"]]

            def load(e, t, slot, signal_sem):
                sp_.dma_start(wslot[slot], mats[t][0, bass.ds(e, 1), :, :]
                              .rearrange("a (c p) n -> p (a c) n", p=P)).then_inc(signal_sem, 16)

            def expert_loads(e, r):
                for t in range(3):
                    slot = (3 * r + t) % 4
                    if not isinstance(e, int) or 3 * e + t >= 4:
                        name = ("down_done", "gate_done", "up_done")[t]
                        sp_.wait_ge(sem(name), e - 1 if t == 0 else e)
                    load(e, t, slot, sem(f"w_loaded{slot}"))

            sp_.wait_ge(sem("router_done"), 1)
            wait_full(sp_, "g2", 1)
            for r in range(4):
                if r == 1:
                    sp_.wait_ge(sem("y_ready"), 1)
                expert_loads(r, r)
            with sp_.Fori(1, E // 4) as i:
                for r in range(4):
                    expert_loads(4 * i + r, r)
            n = sp_.alloc_register("sp_block")
            c = sp_.alloc_register("sp_over")
            sp_.reg_load(c, cnt_i[0:1, (OVER + 1) * E:(OVER + 1) * E + 1])
            with sp_.If(sp_.snap(c) > 0):
                sp_.reg_mov(n, E)
                with sp_.Fori(1, OVER + 1) as b:
                    with sp_.Fori(0, E) as e:
                        sp_.reg_load(c, cnt_i[0:1, bass.ds(b * E + e, 1)])
                        with sp_.If(sp_.snap(c) > 0):
                            sp_.wait_ge(sem("down_done"), sp_.snap(n))
                            for t in range(3):
                                load(e, t, t, sem("w_again"))
                            sp_.reg_add(n, n, 1)
                        sp_.nop()
                sp_.nop()
            sp_.nop()
            sp_.wait_ge(sem("experts_done"), 1)
            sp_.wait_ge(sem("x1_out"), 16)
            sp_.dma_start(x1o.rearrange("p c t -> p (c t)"), x1_dram).then_inc(sem("ld_end"), 16)
            sp_.dma_start(fing[:, :], I["final_g"].rearrange("(a d) -> a d", a=1).broadcast_to([P, D]))\
               .then_inc(sem("ld_end"), 16)
            sp_.wait_ge(sem("out_ready"), 3)
            sp_.dma_start(O["y_prompt"].rearrange("a (t p) d -> p (a t) d", p=P), gt[:, 0:2, :])\
               .then_inc(sem("y_out"), 16)
            sp_.dma_start(O["y_sample"].rearrange("b a d -> (b a) d"), gt[0:NB, 2, :])\
               .then_inc(sem("y_out"), 16)
            sp_.wait_ge(sem("y_out"), 32)

        @block.gpsimd
        def _(pool):
            def step(ins, name="pool_done"):
                signal(pool, ins, name)

            def tri_mask(m, cuts):
                step(pool.memset(m, 1.0))
                for v, pattern, base, cm in cuts:
                    step(pool.affine_select(out=v, in_=v, compare_op=ALU.is_ge, fill=0.0, base=base,
                                            pattern=pattern, channel_multiplier=cm))

            step(pool.memset(ident, 0.0))
            step(pool.affine_select(out=ident, in_=ident, compare_op=ALU.not_equal, fill=1.0, base=0,
                                    pattern=[[-1, 128]], channel_multiplier=1), "ident_ready")
            step(pool.memset(ones, 1.0), "consts")
            step(pool.memset(eps1, 1e-6), "consts")
            step(pool.memset(epsx, 64e-5), "consts")
            hb = bones.rearrange("p (h n) -> p h n", n=HN)
            tri_mask(bones, [(hb, [[-HN, 2], [0, HN]], 0, 1), (hb, [[HN, 2], [0, HN]], HN - 1, -1)])
            for m, strict in ((m_su, 1), (m_iu, 0)):
                v = m.rearrange("p (c t) -> p c t", t=CH)
                tri_mask(m, [(v, [[-CH, CPT], [0, CH]], 0, 1), (v, [[CH, CPT], [1, CH]], -strict, -1)])
            for l in range(LEVELS):
                b = 1 << l
                v = mL[l].rearrange("p (g h j) -> p g h j", h=2, j=b)
                n = P // (2 * b)
                tri_mask(mL[l], [(v, [[-2 * b, n], [0, 2], [0, b]], -b, 1),
                                 (v, [[2 * b, n], [0, 2], [0, b]], 2 * b - 1, -1),
                                 (v, [[0, n], [-1, 2], [0, b]], 0, 0)])
            v = mU0.rearrange("p (g h j) -> p g h j", h=2, j=1)
            tri_mask(mU0, [(v, [[-2, 64], [0, 2], [0, 1]], 0, 1), (v, [[2, 64], [0, 2], [0, 1]], 0, -1),
                           (v, [[0, 64], [1, 2], [0, 1]], -1, 0)])
            step(pool.memset(segm[:, :], 1.0))
            step(pool.memset(segm[:, 0:T:CH], 0.0))
            step(pool.memset(segm[:, T:NT], 0.0), "consts2")
            step(pool.memset(sel9[0:NROW, :], 0.0))
            step(pool.memset(sel9[0:1, 0:T], 1.0))
            step(pool.affine_select(out=sel9[0:NROW, T:NT], in_=sel9[0:NROW, T:NT],
                                    compare_op=ALU.not_equal, fill=1.0, base=-1, pattern=[[-1, NB]],
                                    channel_multiplier=1))
            step(pool.memset(sel4[0:32, :, :], 0.0))
            for k in range(4):
                v = sel4[0:32, k, :].rearrange("p (b q k) -> p b q k", q=Q, k=4)[:, :, :, k]
                step(pool.affine_select(out=v, in_=v, compare_op=ALU.not_equal, fill=1.0, base=0,
                                        pattern=[[-1, NB], [-NB, Q]], channel_multiplier=1), "consts2")
            tri_mask(tri, [(tri, [[1, 128]], -1, -1)])
            step(pool.iota(iota.bitcast(I32), [[0, 2], [1, 64]], base=0, channel_multiplier=0))
            step(pool.tensor_copy(iota, iota.bitcast(I32)), "iota_ready")

            for t in range(2):
                for g in range(2):
                    u = slice(4 * g, 4 * g + 4)
                    wait_out(pool, "U", t, g)
                    if t == 1:
                        wait_out(pool, "AH", 0, 1)
                    step(pool.tensor_tensor(XT[:, u, :], U[:, u, :],
                                            mU0.unsqueeze(1).to_broadcast([P, 4, 128]), ALU.mult))
                    step(pool.tensor_tensor(XT[:, u, :], XT[:, u, :],
                                            ident.unsqueeze(1).to_broadcast([P, 4, 128]), ALU.add),
                         "xt_init")
                if t == 0:
                    Sv = S.rearrange("p (i j) -> p i j", j=HN)
                    Tv = Stmp.rearrange("p (i j) -> p i j", j=HN)
                    sh = [P, 32, HN]
                    vec = lambda k: svb[:, 64 * k:64 * k + 64].unsqueeze(1).to_broadcast(sh)
                    vrow = svb[:, 320:352].unsqueeze(2).to_broadcast(sh)
                    red = sv[:, 0, 0:32]
                    yrow = sv[:, 1, 0:32]
                    wait_out(pool, "smpB")
                    pool.wait_ge(sem("ld_S"), 16)
                    step(pool.tensor_tensor(Tv, Sv, vec(3), ALU.mult), "sample_steps")
                    pool.wait_ge(sem("sample_red"), 1)
                    step(pool.tensor_tensor(Sv, Sv, vec(2), ALU.mult))
                    step(pool.tensor_tensor(Tv, vec(4), red.unsqueeze(2).to_broadcast(sh), ALU.mult))
                    step(pool.tensor_tensor(Sv, Sv, Tv, ALU.subtract))
                    step(pool.tensor_tensor(Tv, vec(1), vrow, ALU.mult))
                    step(pool.tensor_tensor(Sv, Sv, Tv, ALU.add), "sample_state")
                    step(pool.tensor_tensor(Tv, Sv, vec(0), ALU.mult), "sample_steps")

        @block.scalar
        def _(act):
            def step(ins, name="act_done"):
                signal(act, ins, name)

            def out(ins, *name):
                ins.then_inc(bank_out[where[name][0]], 1)

            a0 = 0
            for name, k in PARAMS:
                src = I[name]
                flat = {"rk_r_k": "l h n -> (l h n)", "lru_conv_w": "l w d -> (l w d)"}.get(name, "l d -> (l d)")
                act.dma_start(rows["prm"][a0:a0 + k, :], src.rearrange(flat).rearrange("(r p) -> r p", p=P))\
                   .then_inc(sem("ld_prm"), 16)
                a0 += k
            act.dma_start(lora[0:64, 0, :], I["rk_w_up"][0]).then_inc(sem("ld_lora"), 16)
            act.dma_start(lora[64:128, 0, :], I["rk_a_up"][0]).then_inc(sem("ld_lora"), 16)
            act.dma_start(lora[:, 1, :], I["rk_g_up"][0]).then_inc(sem("ld_lora"), 16)
            act.wait_ge(sem("wbd_zero"), 1)
            for k, name in enumerate(("lru_w_r", "lru_w_i")):
                w = I[name][0].rearrange("(q h) c d -> h c q d", h=2)
                act.dma_start(wbd[k][0:64, :, 0:64], w[0]).then_inc(sem("ld_wbd"), 16)
                act.dma_start(wbd[k][64:128, :, 64:128], w[1]).then_inc(sem("ld_wbd"), 16)
            act.dma_start(S[:, :], I["state_wkv"][0].rearrange("b h (s i) j -> (b h s) (i j)", s=2))\
               .then_inc(sem("ld_S"), 16)

            act.wait_ge(sem("ld_x"), 32)
            act.wait_ge(sem("consts"), 3)
            for t in range(3):
                n = P if t < 2 else NB
                step(act.activation(squares[0:n, :], xtok[0:n, t, :], ACT.Square, accum_out=ssq[0:n, t:t + 1]))
            for t in range(3):
                n = P if t < 2 else NB
                step(act.activation(rstd[0:n, t:t + 1], ssq[0:n, t:t + 1], ACT.Sqrt, bias=eps1[0:n, :],
                                    scale=1.0 / D), "x_root")
            act.wait_ge(sem("ct_zero"), 1)
            wait_full(act, "t", "c")
            out(act.activation(cT[:, :, 0:NROW], bank("t", "c")[:, 0:72].rearrange("p (t c) -> p c t", c=DC),
                               ACT.Silu), "t", "c")
            for c in range(DC):
                wait_full(act, "xT", c)
                out(act.activation(hT[:, c, :], bank("xT", c)[:, 0:NT], ACT.Copy), "xT", c)

            def ada(j):
                wait_full(act, "ada", j)
                if j > 0:
                    wait_full(act, "adaT", j - 1)
                out(act.activation(adar[:, :], bank("ada", j)[:, 0:128], ACT.Copy), "ada", j)

            for j in range(4):
                ada(j)
            for m in range(14, 18):
                wait_full(act, "proj", m)
                out(act.activation(gb[:, m - 14, :], bank("proj", m)[:, 0:NT], ACT.Gelu_apprx_tanh),
                    "proj", m)
            act.wait_ge(sem("xflat_zero"), 1)
            for m in range(18, 22):
                c = m - 18
                wait_full(act, "proj", m)
                out(act.activation(xflat[:, c, 3:3 + T], bank("proj", m)[:, 0:T], ACT.Copy), "proj", m)
                out(act.activation(xflat[:, c, 259:291].rearrange("p (b w) -> p b w", w=4)[:, :, 3],
                                   bank("proj", m)[:, T:NT], ACT.Copy), "proj", m)

            def proj_a(m):
                wait_full(act, "proj", m)
                act.wait_ge(sem("derived"), 1)
                out(act.activation(so[0][:, :, m], bank("proj", m)[:, T - 1:NT], ACT.Copy), "proj", m)
                step(act.activation(z[:, m, :], bank("proj", m)[:, 0:NT], ACT.Copy, scale=omm[:, m:m + 1]),
                     "z_part")

            for m in range(0, 4):
                proj_a(m)
            act.wait_ge(sem("sp_one"), 1)
            step(act.activation(sp[:, 1, :], sp[:, 0, :], ACT.Exp, scale=-1.0), "sp_exp")
            for c in range(Q):
                wait_full(act, "gr", c)
                out(act.activation(gr[:, c, :], bank("gr", c)[:, 0:NT], ACT.Sigmoid, bias=vcol("lru_b_r", c)),
                    "gr", c)
                wait_full(act, "gi", c)
                out(act.activation(gi[:, c, :], bank("gi", c)[:, 0:NT], ACT.Sigmoid, bias=vcol("lru_b_i", c)),
                    "gi", c)
            for m in range(4, MA):
                proj_a(m)
            act.wait_ge(sem("sp_done"), 1)
            for c in range(Q):
                wait_out(act, "gr", c)
                step(act.activation(aB[:, c, :], gr[:, c, :], ACT.Exp, scale=sp[:, 3, c:c + 1]), "lru_a")
            for c in range(Q):
                step(act.activation(gr[:, c, :], gr[:, c, :], ACT.Tanh, scale=sp[:, 2, c:c + 1]), "lru_th")
            for j in range(4, 12):
                ada(j)
            act.wait_ge(sem("lru_b2"), 1)
            step(act.activation(gr[:, :, :], gr[:, :, :], ACT.Sqrt), "lru_root")
            wait_full(act, "ssB")
            out(act.activation(gr[:, 0, :], bank("ssB")[:, 0:NT], ACT.Sqrt, bias=eps1, scale=1.0 / DA), "ssB")
            act.wait_ge(sem("z_done"), MA)
            step(act.activation(z[0:64, 12, :], z[0:64, 12, :], ACT.Tanh), "lora_in")
            step(act.activation(z[:, 13, :], z[:, 13, :], ACT.Sigmoid), "lora_in")
            for q in range(Q):
                wait_full(act, "lw", q)
                out(act.activation(sigw[:, q, :], bank("lw", q)[:, 0:NT], ACT.Sigmoid, bias=vcol("rk_w0", q)),
                    "lw", q)
            for q in range(Q):
                wait_full(act, "la", q)
                out(act.activation(aa[:, q, :], bank("la", q)[:, 0:NT], ACT.Sigmoid, bias=vcol("rk_a0", q)),
                    "la", q)
            for q in range(Q):
                wait_full(act, "lg", q)
                out(act.activation(gg[:, q, :], bank("lg", q)[:, 0:NT], ACT.Copy), "lg", q)
            for q in range(Q):
                wait_full(act, "kn", q)
                act.wait_ge(sem("kk2_done"), 1)
                out(act.activation(yT[:, q, :], bank("kn", q)[:, 0:NT], ACT.Sqrt), "kn", q)
            act.wait_ge(sem("cum_done"), 2)
            step(act.activation(W[:, :, :], cum[:, :, :], ACT.Exp, scale=-EXP_HALF), "decays")
            step(act.activation(cum[:, :, :], cum[:, :, :], ACT.Exp, scale=EXP_HALF), "decays")
            step(act.activation(sigw[:, :, :], sigw[:, :, :], ACT.Exp, scale=-EXP_HALF), "decays")
            for k in range(2):
                wait_full(act, "smpT", k)
                out(act.activation(sv[0:32, 3 * k:3 * k + 3, :].rearrange("p k n -> p (k n)"),
                                   bank("smpT", k)[0:32, 0:384], ACT.Copy), "smpT", k)
            wait_full(act, "smpB")
            out(act.activation(svb[:, :], bank("smpB")[:, 0:352], ACT.Copy), "smpB")
            for t in range(2):
                for k in range(4):
                    wait_full(act, "tk", t, k)
                    out(act.activation(tok[k][:, t, :], bank("tk", t, k)[:, :], ACT.Copy), "tk", t, k)
                for g in range(2):
                    wait_full(act, "U", t, g)
                    out(act.activation(U[:, 4 * g:4 * g + 4, :].rearrange("p u n -> p (u n)"),
                                       bank("U", t, g)[:, :], ACT.Copy), "U", t, g)
                for k in ("LV", "Z", "AH"):
                    for g in range(2):
                        wait_full(act, k, t, g)
                        b = bank(k, t, g)
                        if k == "LV":
                            dst, b = LV[:, 4 * g:4 * g + 4, :].rearrange("p u n -> p (u n)"), b[:, 0:256]
                        elif k == "Z":
                            dst, b = Z[:, t, 256 * g:256 * g + 256], b[:, 0:256]
                        else:
                            rows_ = slice(64 * g, 64 * g + 64)
                            dst, b = ahT[rows_, :, P * t:P * t + P], b[rows_, :].rearrange("p (q n) -> p q n", q=Q)
                        out(act.activation(dst, b, ACT.Copy), k, t, g)
                wait_full(act, "Y1", t)
                out(act.activation(yT[:, :, P * t:P * t + P],
                                   bank("Y1", t)[:, :].rearrange("p (q n) -> p q n", q=Q), ACT.Copy), "Y1", t)
            wait_full(act, "wkv")
            out(act.activation(wkvo[0:HN, :, :].rearrange("p q n -> p (q n)"), bank("wkv")[0:HN, :], ACT.Copy),
                "wkv")
            wait_out(act, "wkv")
            act.dma_start(O["wkv_prompt"].rearrange("a b h i j -> i (a b h) j"),
                          wkvo[0:HN, :, :].rearrange("p q (t j) -> p (q t) j", t=2)).then_inc(sem("states_out"), 16)
            for q in range(Q):
                wait_full(act, "va", q)
                out(act.activation(rsy[:, q, :], bank("va", q)[:, 0:NT], ACT.Sqrt, bias=epsx, scale=1.0 / HN),
                    "va", q)
            for n in range(3):
                wait_full(act, "so", n)
                out(act.activation(sorow[n][0:nso[n], :], bank("so", n)[0:nso[n], 0:128], ACT.Copy), "so", n)
            for n in range(3):
                wait_out(act, "so", n)

            def state(dst, src):
                act.dma_start(dst, src).then_inc(sem("states_out"), 16)

            state(O["shift_prompt"].rearrange("a b (m p) -> (a b m) p", p=P), sorow[0][0:14, :])
            state(O["shift_sample"].rearrange("a b (m p) -> (a b m) p", p=P), sorow[0][14:126, :])
            state(O["conv_prompt"].rearrange("a b w (c p) -> (a b w c) p", p=P), sorow[1][0:12, :])
            state(O["conv_sample"].rearrange("a b w (c p) -> (a b w c) p", p=P), sorow[1][12:108, :])
            state(O["lru_prompt"].rearrange("a b (c p) -> (a b c) p", p=P), sorow[2][0:4, :])
            state(O["lru_sample"].rearrange("a b (c p) -> (a b c) p", p=P), sorow[2][4:36, :])
            act.wait_ge(sem("sample_state"), 1)
            state(O["wkv_sample"][0].rearrange("b h (s i) j -> (b h s) (i j)", s=2), S[:, :])
            for c in range(DC):
                wait_full(act, "x2", c)
                out(act.activation(x2[:, c, :], bank("x2", c)[:, 0:NT], ACT.Copy), "x2", c)
            wait_full(act, "ss2")
            out(act.activation(rs2[:, :], bank("ss2")[:, 0:NT], ACT.Sqrt, bias=eps1, scale=1.0 / D), "ss2")
            act.wait_ge(sem("gates_in"), 3)
            for t in range(3):
                n = P if t < 2 else NB
                step(act.activation(ex[0:n, t, :], ex[0:n, t, :], ACT.Exp), "gates_exp")
            act.wait_ge(sem("states_out"), 16 * 8)
            for t in range(3):
                for c in range(2):
                    n = P if t < 2 else NB
                    wait_full(act, "h2", t, c)
                    out(act.activation(h2tok[0:n, t, 512 * c:512 * c + 512], bank("h2", t, c)[0:n, :], ACT.Copy),
                        "h2", t, c)
            for c in range(2):
                wait_full(act, "g2", c)
                out(act.activation(gate2[0:NROW, 512 * c:512 * c + 512], bank("g2", c)[0:NROW, :], ACT.Copy),
                    "g2", c)

            def x_copy(n):
                act.wait_ge(sem("gathered"), n + 1)
                act.activation(Xg[:, :], ps[2][:, :], ACT.Copy).then_inc(sem("x_copied"), 1)

            def xt_copy(n):
                act.wait_ge(sem("x_turned"), n + 1)
                act.activation(XTg[:, :], ps[3][:, :], ACT.Copy).then_inc(sem("xt_copied"), 1)

            def sigmoid(n):
                act.wait_ge(sem("g_read"), n + 1)
                if not isinstance(n, int) or n > 0:
                    act.wait_ge(sem("glu_done"), n)
                act.activation(sg_sb[:, :], g_sb[:, :], ACT.Sigmoid, scale=1.702).then_inc(sem("sig_done"), 1)

            def at_copy(n):
                act.wait_ge(sem("act_turned"), n + 1)
                act.activation(aT_sb[:, :], ps[3][:, :], ACT.Copy).then_inc(sem("at_copied"), 1)

            def pt_copy(n):
                act.wait_ge(sem("pt_turned"), n + 1)
                act.activation(PTz[0][0:64, :], ps[4][0:64, 0:NT], ACT.Copy).then_inc(sem("pt_copied"), 1)
                act.activation(PTz[1][64:128, :], ps[4][64:128, 0:NT], ACT.Copy).then_inc(sem("pt_copied"), 1)

            def out_copy(n):
                act.wait_ge(sem("down_done"), n + 1)
                act.activation(o_sb[:, :], ps[5][:, :], ACT.Copy).then_inc(sem("out_copied"), 1)

            def block_step(n, last=False):
                sigmoid(n)
                if not last:
                    x_copy(n + 1)
                at_copy(n)
                pt_copy(n)
                if not last:
                    xt_copy(n + 1)
                out_copy(n)

            act.wait_ge(sem("ptz_zero"), 2)
            x_copy(0)
            xt_copy(0)
            for r in range(4):
                block_step(r)
            with act.Fori(1, E // 4 - 1) as i:
                for r in range(4):
                    block_step(4 * i + r)
            for r in range(4):
                block_step(E - 4 + r, last=(r == 3))
            n = act.alloc_register("act_block")
            c = act.alloc_register("act_over")
            act.reg_load(c, cnt_i[0:1, (OVER + 1) * E:(OVER + 1) * E + 1])
            with act.If(act.snap(c) > 0):
                act.reg_mov(n, E)
                with act.Fori(1, OVER + 1) as b:
                    with act.Fori(0, E) as e:
                        act.reg_load(c, cnt_i[0:1, bass.ds(b * E + e, 1)])
                        with act.If(act.snap(c) > 0):
                            k = act.snap(n)
                            x_copy(k)
                            xt_copy(k)
                            block_step(k, last=True)
                            act.reg_add(n, n, 1)
                        act.nop()
                act.nop()
            act.nop()
            for t in range(3):
                for c in range(2):
                    k = 2 * t + c
                    n = P if t < 2 else NB
                    act.wait_ge(sem("x1_turned"), k + 1)
                    act.activation(x1t[0:n, t, 512 * c:512 * c + 512], ps[k][0:n, :], ACT.Copy)\
                       .then_inc(sem("x1_copied"), 1)
            act.wait_ge(sem("x3_ready"), 3)
            for t in range(3):
                n = P if t < 2 else NB
                act.activation(x1t[0:n, t, :], gt[0:n, t, :], ACT.Square, accum_out=ssq[0:n, t:t + 1])\
                   .then_inc(sem("ss3_done"), 1)
            act.wait_ge(sem("ss3_done"), 3)
            for t in range(3):
                n = P if t < 2 else NB
                act.activation(rstd[0:n, t:t + 1], ssq[0:n, t:t + 1], ACT.Sqrt, bias=eps1[0:n, :],
                               scale=1.0 / D).then_inc(sem("root3"), 1)
            act.wait_ge(sem("states_out"), 16 * 8)

        @block.vector
        def _(dve):
            def step(ins, name="lanes_done"):
                signal(dve, ins, name)

            def out(ins, *name):
                b, _, before, after = where[name]
                ins.then_inc(bank_out[b], 1)

            def tt(o, a, b, op, name="lanes_done"):
                step(dve.tensor_tensor(o, a, b, op), name)

            def ts(o, a, s1, s2, op0, op1=ALU.bypass, name="lanes_done"):
                step(dve.tensor_scalar(o, a, s1, s2, op0, op1), name)

            def stt(o, a, s, b, op0, op1, name="lanes_done"):
                step(dve.scalar_tensor_tensor(out=o, in0=a, scalar=s, in1=b, op0=op0, op1=op1), name)

            step(dve.memset(cT[:, :, :], 0.0), "ct_zero")
            step(dve.memset(wbd[0][:, :, :], 0.0))
            step(dve.memset(wbd[1][:, :, :], 0.0), "wbd_zero")
            step(dve.memset(xflat[:, :, :], 0.0), "xflat_zero")
            dve.wait_ge(sem("ident_ready"), 1)
            dve.wait_ge(sem("x_root"), 3)
            for t in range(3):
                n = P if t < 2 else NB
                step(dve.reciprocal(rstd[0:n, t:t + 1], rstd[0:n, t:t + 1]))
                ts(diag[0:n, t, 0:n], ident[0:n, 0:n], rstd[0:n, t:t + 1], None, ALU.mult, name="diag_ready")
            for name, dst in (("prm", prm[:, 0:NPAR]), ("bada", badaT[:, :]),
                              ("shift", shiftT.rearrange("p b m -> p (b m)")), ("conv", None),
                              ("lru", h0T.rearrange("p b c -> p (b c)"))):
                wait_full(dve, "t", name)
                src = bank("t", name)[:, 0:nrows[name]]
                if name == "conv":
                    dst = xflat[:, :, 259:291].rearrange("p c (b w) -> p c b w", w=4)
                    src = src.rearrange("p (b w c) -> p c b w", w=3, c=Q)
                    b_ = where[("t", name)][0]
                    for c in range(Q):
                        ins = dve.tensor_copy(dst[:, c, :, 0:3], src[:, c, :, :])
                        if c < Q - 1:
                            step(ins)
                    out(ins, "t", name)
                else:
                    out(dve.tensor_copy(dst, src), "t", name)
                wait_out(dve, "t", name)
            ts(omm[:, :], prm[:, 0:MA], -1.0, 1.0, ALU.mult, ALU.add, name="derived")
            ka = prm[:, PAT["rk_k_a"]:PAT["rk_k_a"] + Q]
            ts(omka[:, :], ka, -1.0, 1.0, ALU.mult, ALU.add)
            lam = prm[:, PAT["lru_lambda"]:PAT["lru_lambda"] + Q]
            ts(sp[:, 4, :], lam, -1.0, None, ALU.mult)
            tt(sp[:, 0, :], sp[:, 4, :], lam, ALU.max, name="sp_one")

            def adaT(j):
                wait_full(dve, "adaT", j)
                out(dve.tensor_tensor(modT[:, 4 * j:4 * j + 4, :],
                                      bank("adaT", j)[:, 0:128].rearrange("p (g r) -> p g r", g=4)[:, :, 0:NROW],
                                      badaT[:, 4 * j:4 * j + 4].unsqueeze(2).to_broadcast([P, 4, NROW]),
                                      ALU.add), "adaT", j)
                wait_out(dve, "adaT", j)

            for j in range(4):
                adaT(j)

            def affine(dst, src, A, shift, c, name="lanes_done"):
                ts(dst[:, c, 0:T], src[:, c, 0:T], A[:, c, 0:1], mod(shift, c, slice(0, 1)), ALU.mult, ALU.add)
                tt(dst[:, c, T:NT], src[:, c, T:NT], A[:, c, 1:NROW], ALU.mult)
                tt(dst[:, c, T:NT], dst[:, c, T:NT], mod(shift, c, slice(1, NROW)), ALU.add, name=name)

            def gains(A, scale, norm):
                ts(A[:, :, :], modT[:, scale * DC:(scale + 1) * DC, :], 1.0, None, ALU.add)
                g_ = prm[:, PAT[norm]:PAT[norm] + DC]
                tt(A[:, :, :], A[:, :, :], g_.unsqueeze(2).to_broadcast([P, DC, NROW]), ALU.mult)

            gains(A1, 1, "norm1_g")
            for c in range(DC):
                wait_out(dve, "xT", c)
                affine(hT, hT, A1, 0, c, name="h_done")

            dve.wait_ge(sem("sp_exp"), 1)
            e_, s_, s2_, q_ = (sp[:, k, :] for k in (1, 5, 6, 7))
            ts(q_, e_, 2.0, None, ALU.add)
            step(dve.reciprocal(q_, q_))
            tt(s_, e_, q_, ALU.mult)
            tt(s2_, s_, s_, ALU.mult)
            ts(q_, s2_, 1.0 / 17, None, ALU.mult)
            for k in (15, 13, 11, 9, 7, 5, 3):
                stt(q_, q_, 1.0 / k, s2_, ALU.add, ALU.mult)
            stt(q_, q_, 1.0, s_, ALU.add, ALU.mult)
            ts(sp[:, 4, :], sp[:, 4, :], 0.0, None, ALU.max)
            stt(q_, q_, 2.0, sp[:, 4, :], ALU.mult, ALU.add)
            ts(sp[:, 2, :], q_, 8.0, None, ALU.mult)
            ts(sp[:, 3, :], q_, -8.0, None, ALU.mult, name="sp_done")

            cw = lambda j, c: vcol("lru_conv_w", 4 * j + c)
            for c in range(Q):
                wait_out(dve, "proj", 18 + c)
                wait_out(dve, "t", "conv")
                tmp = aB.rearrange("p c n -> p (c n)")[:, 0:288]
                ts(tmp, xflat[:, c, 0:288], cw(0, c), vcol("lru_conv_b", c), ALU.mult, ALU.add)
                stt(tmp, xflat[:, c, 1:289], cw(1, c), tmp, ALU.mult, ALU.add)
                stt(tmp, xflat[:, c, 2:290], cw(2, c), tmp, ALU.mult, ALU.add)
                stt(xc[:, c, 0:T], xflat[:, c, 3:259], cw(3, c), tmp[:, 0:T], ALU.mult, ALU.add)
                smp_x = xflat[:, c, 259:291].rearrange("p (b w) -> p b w", w=4)[:, :, 3]
                smp_t = aB.rearrange("p c n -> p (c n)")[:, 259:291].rearrange("p (b w) -> p b w", w=4)[:, :, 0]
                stt(xc[:, c, T:NT], smp_x, cw(3, c), smp_t, ALU.mult, ALU.add, name="conv_done")
            for c in range(Q):
                step(dve.tensor_copy(so[1][:, 0:12].rearrange("p (w c) -> p c w", c=Q)[:, c, :],
                                     xflat[:, c, 256:259]))
                step(dve.tensor_copy(so[1][:, 12:108].rearrange("p (b w c) -> p c b w", c=Q, w=3)[:, c, :, :],
                                     xflat[:, c, 259:291].rearrange("p (b w) -> p b w", w=4)[:, :, 1:4]), "conv_state")

            def mix_shift(m):
                wait_full(dve, "proj", m)
                dve.wait_ge(sem("z_part"), m + 1)
                out(dve.scalar_tensor_tensor(out=z[:, m, 1:T], in0=bank("proj", m)[:, 0:T - 1],
                                             scalar=vcol("rk_mu", m), in1=z[:, m, 1:T],
                                             op0=ALU.mult, op1=ALU.add), "proj", m)
                stt(z[:, m, T:NT], shiftT[:, :, m], vcol("rk_mu", m), z[:, m, T:NT], ALU.mult, ALU.add,
                    name="z_done")

            for m in range(MA):
                mix_shift(m)
            dve.wait_ge(sem("lru_a"), Q)
            dve.wait_ge(sem("lru_th"), Q)
            for c in range(Q):
                wait_out(dve, "gi", c)
            tt(gi[:, :, :], gi[:, :, :], xc[:, :, :], ALU.mult)
            tt(xc[:, :, :], aB[:, :, :], aB[:, :, :], ALU.mult)
            stt(gr[:, :, :], xc[:, :, :], 1.0, gr[:, :, :], ALU.add, ALU.mult, name="lru_b2")
            for j in range(4, 12):
                adaT(j)
            dve.wait_ge(sem("lru_root"), 1)
            tt(gi[:, :, :], gi[:, :, :], gr[:, :, :], ALU.mult)
            for c in range(Q):
                step(dve.tensor_tensor_scan(xc[:, c, 0:T], aB[:, c, 0:T], gi[:, c, 0:T], 0.0, ALU.mult, ALU.add))
            h0 = h0T.rearrange("p b c -> p c b")
            tt(xc[:, :, T:NT], aB[:, :, T:NT], h0, ALU.mult)
            tt(xc[:, :, T:NT], xc[:, :, T:NT], gi[:, :, T:NT], ALU.add)
            step(dve.tensor_copy(so[2][:, 0:4].unsqueeze(2), xc[:, :, T - 1:T]))
            step(dve.tensor_copy(so[2][:, 4:36].rearrange("p (b c) -> p c b", c=Q), xc[:, :, T:NT]), "lru_state")
            for c in range(Q):
                wait_out(dve, "proj", 14 + c)
            tt(xc[:, :, :], xc[:, :, :], gb[:, :, :], ALU.mult)
            tt(gi[:, :, :], xc[:, :, :], xc[:, :, :], ALU.mult, name="sqB_done")
            wait_out(dve, "ssB")
            step(dve.reciprocal(gr[:, 0, :], gr[:, 0, :]))
            for c in range(Q):
                stt(mixT[:, Q + c, :], xc[:, c, :], vcol("lru_norm_g", c), gr[:, 0, :], ALU.mult, ALU.mult,
                    name="mixB_done")

            zk = z[:, 4:8, :]
            for q in range(Q):
                ts(kk[:, q, :], z[:, 4 + q, :], vcol("rk_k_k", q), None, ALU.mult)
            tt(yT[:, :, :], kk[:, :, :], kk[:, :, :], ALU.mult, name="kk2_done")
            dve.wait_ge(sem("consts2"), 1)
            for q in range(Q):
                wait_out(dve, "lw", q)
                step(dve.tensor_tensor_scan(cum[:, q, :], segm[:, :], sigw[:, q, :], 0.0, ALU.mult, ALU.add)) \
                    if q < Q - 1 else \
                    step(dve.tensor_tensor_scan(cum[:, q, :], segm[:, :], sigw[:, q, :], 0.0, ALU.mult, ALU.add),
                         "cum_done")
            tt(sigw[:, :, :], cum[:, :, :], sigw[:, :, :], ALU.subtract, name="cum_done")
            for q in range(Q):
                wait_out(dve, "la", q)
                fq = arp.rearrange("p q t k n -> p (q t k n)")[:, 0:NT] if q % 2 == 0 else \
                    arp.rearrange("p q t k n -> p (q t k n)")[:, 512:512 + NT]
                ts(fq, aa[:, q, :], vcol("rk_k_a", q), omka[:, q:q + 1], ALU.mult, ALU.add)
                tt(z[:, 4 + q, :], z[:, 4 + q, :], fq, ALU.mult)
            for q in range(Q):
                wait_out(dve, "kn", q)
            ts(yT[:, :, :], yT[:, :, :], 1e-12, None, ALU.max)
            step(dve.reciprocal(yT[:, :, :], yT[:, :, :]))
            tt(kk[:, :, :], kk[:, :, :], yT[:, :, :], ALU.mult)
            tt(aa[:, :, :], kk[:, :, :], aa[:, :, :], ALU.mult)
            dve.wait_ge(sem("decays"), 3)
            zr, zv = z[:, 0:4, :], z[:, 8:12, :]
            for k, src in enumerate((zr, zk, W, kk, aa, zv)):
                step(dve.tensor_copy(smp[:, k, :, :], src[:, :, T:NT]), "smp_done")
            for q in range(Q):
                stt(bm[:, q, :], aa[:, q, 0:T], -1.0, cum[:, q, 0:T], ALU.mult, ALU.mult, name="bm_done")
                tt(kap[:, q, :], z[:, 4 + q, 0:T], cum[:, q, 0:T], ALU.mult, name="bm_done")
                two = lambda v: v.rearrange("p (t n) -> p t n", t=2)
                tt(arp[:, q, :, 0, :], two(kk[:, q, 0:T]), two(sigw[:, q, 0:T]), ALU.mult, name="bm_done")
                tt(arp[:, q, :, 1, :], two(z[:, q, 0:T]), two(W[:, q, 0:T]), ALU.mult, name="bm_done")
            wend = sp[:, 0:8, :].rearrange("p a b -> p (a b)")[:, 0:Q * NCH].rearrange("p (q c) -> p q c", q=Q)
            step(dve.tensor_copy(wend, W[:, :, CH - 1:T:CH]))
            for q in range(Q):
                stt(cum[:, q, :], z[:, q, :], vcol("rk_r_k", q), z[:, 4 + q, :], ALU.mult, ALU.mult,
                    name="rk_done")
            for q in range(Q):
                wait_full(dve, "bo", q)
                out(dve.tensor_tensor(bv[:, q, :], bank("bo", q)[:, 0:NT], z[:, 8 + q, :], ALU.mult), "bo", q)
            for q in range(Q):
                wait_out(dve, "bo", q)
            step(dve.memset(ST[:, 0, :, :], 0.0), "vectors_done")

            four = lambda m: m.unsqueeze(1).to_broadcast([P, 4, 128])
            grp = lambda b: b[:, :].rearrange("p (u n) -> p u n", u=4)
            for t in range(2):
                for g in range(2):
                    u = slice(4 * g, 4 * g + 4)
                    wait_full(dve, "L", t, g)
                    out(dve.tensor_tensor(X[:, u, :], grp(bank("L", t, g)), four(mL[0]), ALU.mult), "L", t, g)
                    wait_out(dve, "L", t, g)
                    tt(X[:, u, :], X[:, u, :], four(ident), ALU.add, name="x_init")
                for k, dst, m, n0 in (("Ak", Ak, m_su, 0), ("Rb", Rb, m_iu, 8 * t), ("Rk", Rk, m_iu, 8 * t)):
                    for g in range(2):
                        wait_full(dve, k, t, g)
                        out(dve.tensor_tensor(dst[:, n0 + 4 * g:n0 + 4 * g + 4, :], grp(bank(k, t, g)), four(m),
                                              ALU.mult), k, t, g)
                for l in range(1, LEVELS):
                    for g in range(2):
                        u = slice(4 * g, 4 * g + 4)
                        wait_full(dve, "Y", t, g, l)
                        out(dve.tensor_tensor(Y[:, u, :], grp(bank("Y", t, g, l)), four(mL[l]), ALU.mult),
                            "Y", t, g, l)
                    for k, dst in (("X", X), ("XT", XT)):
                        if k == "X" and l == LEVELS - 1:
                            continue
                        for g in range(2):
                            u = slice(4 * g, 4 * g + 4)
                            wait_full(dve, k, t, g, l)
                            if l > 1:
                                wait_out(dve, k, t, g, l - 1)
                            elif k == "XT":
                                dve.wait_ge(sem("xt_init"), 2 * t + g + 1)
                            out(dve.tensor_tensor(dst[:, u, :], grp(bank(k, t, g, l)), dst[:, u, :], ALU.add),
                                k, t, g, l)
                if t == 0:
                    Tv = Stmp.rearrange("p (i j) -> p i j", j=HN)
                    dve.wait_ge(sem("sample_steps"), 1)
                    step(dve.tensor_reduce(sv[:, 0, 0:32], Tv, AX, ALU.add), "sample_red")
                    dve.wait_ge(sem("sample_steps"), 2)
                    step(dve.tensor_reduce(sv[:, 1, 0:32], Tv, AX, ALU.add), "sample_y")
                for c in range(CPT * t, CPT * (t + 1)):
                    r = slice(CH * (c % CPT), CH * (c % CPT) + CH)
                    for g in range(2):
                        gc = slice(256 * g, 256 * g + 256)
                        wait_full(dve, "SA", c, g)
                        wait_out(dve, "Z", t, g)
                        out(dve.tensor_tensor(SA[r, t, gc], bank("SA", c, g)[r, 0:256], Z[r, t, gc], ALU.add),
                            "SA", c, g)
                    wait_full(dve, "SU", c)
                    b = bank("SU", c)[:, 0:Q * HN].rearrange("p (q n) -> p q n", q=Q)
                    out(dve.tensor_tensor(ST[:, c + 1, :, :], b, ST[:, c, :, :], ALU.add), "SU", c)
                    wait_out(dve, "SU", c)
                    tt(ST[:, c + 1, :, :], ST[:, c + 1, :, :], wend[:, :, c].unsqueeze(2).to_broadcast([P, Q, HN]),
                       ALU.mult, name="state_done")
                wait_full(dve, "Y2", t)
                wait_out(dve, "Y1", t)
                yt = yT[:, :, P * t:P * t + P]
                out(dve.tensor_tensor(yt, bank("Y2", t)[:, :].rearrange("p (q n) -> p q n", q=Q), yt, ALU.add),
                    "Y2", t)
            wait_full(dve, "syT")
            b = bank("syT")[0:32, 0:128].rearrange("p (b q k) -> p k q b", q=Q, k=4)
            for k in range(4):
                out(dve.tensor_copy(yT[32 * k:32 * k + 32, :, T:NT], b[:, k, :, :]), "syT")
            wait_out(dve, "Y2", 0)
            wait_out(dve, "Y2", 1)
            wait_out(dve, "syT")
            for q in range(Q):
                wait_full(dve, "mu", q)
                out(dve.scalar_tensor_tensor(out=yT[:, q, :], in0=bank("mu", q)[:, 0:NT], scalar=-1.0 / HN,
                                             in1=yT[:, q, :], op0=ALU.mult, op1=ALU.add), "mu", q)
                wait_out(dve, "mu", q)
                tt(sqy[:, q, :], yT[:, q, :], yT[:, q, :], ALU.mult, name="sqy_done")
            for q in range(Q):
                wait_out(dve, "va", q)
                step(dve.reciprocal(rsy[:, q, :], rsy[:, q, :]))
                stt(yT[:, q, :], yT[:, q, :], vcol("rk_lnx_w", q), rsy[:, q, :], ALU.mult, ALU.mult)
                stt(yT[:, q, :], yT[:, q, :], vcol("rk_lnx_b", q), bv[:, q, :], ALU.add, ALU.add)
                wait_out(dve, "lg", q)
                tt(mixT[:, q, :], yT[:, q, :], gg[:, q, :], ALU.mult, name="mixA_done")

            for c in range(DC):
                wait_full(dve, "mo", c)
                wait_out(dve, "x2", c)
                b = bank("mo", c)
                out(dve.scalar_tensor_tensor(out=x1T[:, c, 0:T], in0=b[:, 0:T], scalar=mod(2, c, slice(0, 1)),
                                             in1=x2[:, c, 0:T], op0=ALU.mult, op1=ALU.add), "mo", c)
                out(dve.tensor_tensor(x1T[:, c, T:NT], b[:, T:NT], mod(2, c, slice(1, NROW)), ALU.mult), "mo", c)
                wait_out(dve, "mo", c)
                tt(x1T[:, c, T:NT], x1T[:, c, T:NT], x2[:, c, T:NT], ALU.add)
                tt(sq2[:, c, :], x1T[:, c, :], x1T[:, c, :], ALU.mult, name="sq2_done")
            step(dve.memset(lbase[0:1, 0:1], 0.0), "x1_done")
            gains(A2, 4, "norm2_g")
            wait_out(dve, "ss2")
            step(dve.reciprocal(rs2[:, :], rs2[:, :]))
            for c in range(DC):
                tt(h2T[:, c, :], x1T[:, c, :], rs2[:, :], ALU.mult)
                affine(h2T, h2T, A2, 3, c, name="h2_done")

            dve.wait_ge(sem("iota_ready"), 1)
            step(dve.memset(cnt_i[:, :], 0))
            for t in range(3):
                n = P if t < 2 else NB
                wait_full(dve, "lg2", t)
                out(dve.tensor_copy(lgt[0:n, t, :], bank("lg2", t)[0:n, 0:E]), "lg2", t)
                wait_out(dve, "lg2", t)
                L_ = lgt[0:n, t, :]
                step(dve.max(top[0:n, t, :], L_))
                v4 = top[0:n, t, 3:4]
                ts(msk[0:n, t, :], L_, v4, None, ALU.is_gt)
                ts(eq[0:n, t, :], L_, v4, None, ALU.is_equal)
                step(dve.tensor_reduce(sc[0:n, t, 0:1], msk[0:n, t, :], AX, ALU.add))
                step(dve.tensor_tensor_scan(ce[0:n, t, :], ones[0:n, 0:E], eq[0:n, t, :], 0.0, ALU.mult, ALU.add))
                ts(ce[0:n, t, :], ce[0:n, t, :], sc[0:n, t, 0:1], 4.0, ALU.add, ALU.is_le)
                tt(eq[0:n, t, :], eq[0:n, t, :], ce[0:n, t, :], ALU.mult)
                tt(msk[0:n, t, :], msk[0:n, t, :], eq[0:n, t, :], ALU.add, name="mask_done")
                ts(ex[0:n, t, :], L_, top[0:n, t, 0:1], None, ALU.subtract, name="gates_in")
            dve.wait_ge(sem("gates_exp"), 3)
            for t in range(3):
                n = P if t < 2 else NB
                tt(ex[0:n, t, :], ex[0:n, t, :], msk[0:n, t, :], ALU.mult)
                step(dve.tensor_reduce(sc[0:n, t, 1:2], ex[0:n, t, :], AX, ALU.add))
                step(dve.reciprocal(sc[0:n, t, 1:2], sc[0:n, t, 1:2]))
                ts(gatew[0:n, t, :], ex[0:n, t, :], sc[0:n, t, 1:2], None, ALU.mult, name="gatew_done")
            step(dve.tensor_copy(gatew[64:72, 2, :], gatew[0:8, 2, :]), "gatew_done")
            wait_full(dve, "rank")
            b = bank("rank")[:, 0:96].rearrange("p (t e) -> p t e", t=3)
            out(dve.scalar_tensor_tensor(out=lgt[:, 0:2, :], in0=b[:, 0:2, :], scalar=1.0, in1=msk[:, 0:2, :],
                                         op0=ALU.add, op1=ALU.mult), "rank")
            out(dve.scalar_tensor_tensor(out=lgt[0:NB, 2, :], in0=b[0:NB, 2, :], scalar=1.0,
                                         in1=msk[0:NB, 2, :], op0=ALU.add, op1=ALU.mult), "rank")
            wait_out(dve, "rank")
            for k in range(OVER + 1):
                ts(rankb[:, 0:2, E * k:E * k + E], lgt[:, 0:2, :], -1.0 - SLOTS * k, None, ALU.add)
                ts(rankb[0:NB, 2, E * k:E * k + E], lgt[0:NB, 2, :], -1.0 - SLOTS * k, None, ALU.add)
            wait_full(dve, "cnt")
            out(dve.tensor_copy(lbase[0:1, :], bank("cnt")[0:1, 0:E]), "cnt")
            wait_out(dve, "cnt")
            for k in range(OVER + 1):
                ts(cnt_i[0:1, E * k:E * k + E], lbase[0:1, :], float(-SLOTS * k), 0.0, ALU.add, ALU.max)
            step(dve.tensor_reduce(cnt_i[0:1, (OVER + 1) * E:(OVER + 1) * E + 1], cnt_i[0:1, E:2 * E], AX, ALU.max),
                 "router_done")
            dve.wait_ge(sem("states_out"), 16 * 8)
            step(dve.memset(PTz[0][:, :], 0.0), "ptz_zero")
            step(dve.memset(PTz[1][:, :], 0.0), "ptz_zero")

            def select(n, k, e, buf, turned):
                if turned is not None:
                    dve.wait_ge(sem("pt_turned"), turned)
                    dve.wait_ge(sem("up_done"), turned)
                for t in range(3):
                    m = P if t < 2 else NB
                    dve.tensor_scalar(Psel[buf][0:m, t, :], iota[0:m, :], rankb[0:m, t, bass.ds(k, 1)], None,
                                      ALU.is_equal).then_inc(sem("selected"), 1)
                dve.tensor_scalar(selb[buf][0:E, :], ones[0:E, 0:64], ident[0:E, bass.ds(e, 1)], None,
                                  ALU.mult).then_inc(sem("selected"), 1)

            def glu_g(n):
                dve.wait_ge(sem("gate_done"), n + 1)
                if not isinstance(n, int) or n > 0:
                    dve.wait_ge(sem("act_done2"), n)
                dve.tensor_scalar(g_sb[:, :], ps[0][:, :], 7.0, None, ALU.min).then_inc(sem("g_read"), 1)

            def glu_u(n):
                dve.wait_ge(sem("up_done"), n + 1)
                dve.tensor_scalar(u_sb[:, :], ps[1][:, :], 7.0, -7.0, ALU.min, ALU.max).then_inc(sem("u_read"), 1)
                dve.wait_ge(sem("sig_done"), n + 1)
                dve.tensor_tensor(g_sb[:, :], g_sb[:, :], sg_sb[:, :], ALU.mult).then_inc(sem("glu_done"), 1)
                dve.wait_ge(sem("glu_done"), n + 1)
                dve.wait_ge(sem("u_read"), n + 1)
                if not isinstance(n, int) or n > 0:
                    dve.wait_ge(sem("act_turned"), n)
                dve.scalar_tensor_tensor(out=a_sb[:, :], in0=u_sb[:, :], scalar=1.0, in1=g_sb[:, :],
                                         op0=ALU.add, op1=ALU.mult).then_inc(sem("act_done2"), 1)

            def add_out(n, e):
                if not isinstance(n, int) or n > 0:
                    dve.wait_ge(sem("y_added"), 6 * n)
                for k in range(4):
                    t, h = k // 2, k % 2
                    dve.wait_ge(sem("scattered"), 5 * n + k + 1)
                    v = y[:, t, 512 * h:512 * h + 512]
                    dve.scalar_tensor_tensor(out=v, in0=ps[6 + k % 2][:, :], scalar=gatew[:, t, bass.ds(e, 1)],
                                             in1=v, op0=ALU.mult, op1=ALU.add).then_inc(sem("y_added"), 1)
                dve.wait_ge(sem("scattered"), 5 * n + 5)
                for p0 in (0, 64):
                    v = y_s[p0:p0 + NB, :]
                    dve.scalar_tensor_tensor(out=v, in0=ps[6][p0:p0 + NB, :],
                                             scalar=gatew[p0:p0 + NB, 2, bass.ds(e, 1)], in1=v,
                                             op0=ALU.mult, op1=ALU.add).then_inc(sem("y_added"), 1)

            def y_start():
                dve.wait_ge(sem("gt_turned"), 1)
                step(dve.tensor_copy(g_sb[0:E, 0:NT], ps[7][0:E, 0:NT]), "gt_copied")
                dve.wait_ge(sem("x1_out"), 16)
                for k in range(5):
                    dve.wait_ge(sem("y_bias"), k + 1)
                    if k < 4:
                        step(dve.tensor_copy(y[:, k // 2, 512 * (k % 2):512 * (k % 2) + 512], ps[k][:, :]))
                    else:
                        step(dve.tensor_copy(y_s[0:NB, :], ps[4][0:NB, :]))
                        step(dve.tensor_copy(y_s[64:64 + NB, :], ps[4][64:64 + NB, :]), "y_ready")

            select(0, 0, 0, 0, None)
            y_start()
            for n in range(4):
                glu_g(n)
                select(n + 1, n + 1, n + 1, (n + 1) % 2, n if n > 0 else None)
                glu_u(n)
                if n > 0:
                    add_out(n - 1, n - 1)
            with dve.Fori(1, E // 4 - 1) as i:
                for r in range(4):
                    n = 4 * i + r
                    glu_g(n)
                    select(n + 1, n + 1, n + 1, (r + 1) % 2, n)
                    glu_u(n)
                    add_out(n - 1, n - 1)
            for r in range(4):
                n = E - 4 + r
                glu_g(n)
                if r < 3:
                    select(n + 1, n + 1, n + 1, (r + 1) % 2, n)
                glu_u(n)
                add_out(n - 1, n - 1)
            add_out(E - 1, E - 1)
            nreg = dve.alloc_register("dve_block")
            c = dve.alloc_register("dve_over")
            dve.reg_load(c, cnt_i[0:1, (OVER + 1) * E:(OVER + 1) * E + 1])
            with dve.If(dve.snap(c) > 0):
                dve.reg_mov(nreg, E)
                with dve.Fori(1, OVER + 1) as b:
                    with dve.Fori(0, E) as e:
                        dve.reg_load(c, cnt_i[0:1, bass.ds(b * E + e, 1)])
                        with dve.If(dve.snap(c) > 0):
                            n = dve.snap(nreg)
                            select(n, b * E + e, e, 0, n)
                            glu_g(n)
                            glu_u(n)
                            add_out(n, e)
                            dve.reg_add(nreg, nreg, 1)
                        dve.nop()
                dve.nop()
            dve.nop()
            step(dve.memset(small[:, 40:41], 0.0), "experts_done")
            for t in range(2):
                for h in range(2):
                    k = 2 * t + h
                    cs = slice(512 * h, 512 * h + 512)
                    dve.wait_ge(sem("x1_copied"), 6)
                    dve.wait_ge(sem("g2_done"), k + 1)
                    tt(gt[:, t, cs], ps[6 + k % 2][:, :], y[:, t, cs], ALU.mult, name="g2_used")
                    tt(gt[:, t, cs], gt[:, t, cs], x1t[:, t, cs], ALU.add, name="lanes_done")
                step(dve.memset(small[:, 41:42], 0.0), "x3_ready")
            dve.wait_ge(sem("g2_done"), 5)
            for h in range(2):
                p0, cs = 64 * h, slice(512 * h, 512 * h + 512)
                tt(g_sb[p0:p0 + NB, :], ps[6][p0:p0 + NB, :], y_s[p0:p0 + NB, :], ALU.mult)
                if h:
                    step(dve.tensor_copy(u_sb[0:NB, :], g_sb[64:64 + NB, :]))
                tt(gt[0:NB, 2, cs], (u_sb if h else g_sb)[0:NB, :], x1t[0:NB, 2, cs], ALU.add)
            step(dve.memset(small[:, 41:42], 0.0), "x3_ready")
            dve.wait_ge(sem("root3"), 3)
            dve.wait_ge(sem("ld_end"), 32)
            for t in range(3):
                n = P if t < 2 else NB
                step(dve.reciprocal(rstd[0:n, t:t + 1], rstd[0:n, t:t + 1]))
                stt(gt[0:n, t, :], gt[0:n, t, :], rstd[0:n, t:t + 1], fing[0:n, :], ALU.mult, ALU.mult,
                    name="out_ready")

        @block.tensor
        def _(pe):
            order = [n for n, _ in jobs]
            pos = [0]

            def start(*name):
                assert order[pos[0]] == name, (order[pos[0]], name)
                pos[0] += 1
                b, _, before, _ = where[name]
                if before:
                    pe.wait_ge(bank_out[b], before)
                return ps[b]

            def done(ins, *name):
                ins.then_inc(bank_full[where[name][0]], 1)

            def turn(dst, src):
                return pe.transpose(dst, src, ident[0:src.shape[0], 0:src.shape[0]])

            pe.wait_ge(sem("ident_ready"), 1)
            pe.wait_ge(sem("ld_rows"), 16 * 6)
            pe.wait_ge(sem("ld_prm"), 16 * len(PARAMS))
            for name in ("c", "prm", "bada", "shift", "conv", "lru"):
                o = start("t", name)
                done(turn(o[:, 0:nrows[name]], rows[name][0:nrows[name], :]), "t", name)
            pe.wait_ge(sem("diag_ready"), 3)
            for c in range(DC):
                o = start("xT", c)
                for t in range(3):
                    n = P if t < 2 else NB
                    mm = pe.matmul(o[:, P * t:P * t + n], xtok[0:n, t, P * c:P * c + P], diag[0:n, t, 0:n],
                                   start=True, stop=True)
                done(mm, "xT", c)

            def ada(j):
                n = j if j < 4 else 6 + j
                w = fslot[n % FR]
                o = start("ada", j)
                pe.wait_ge(*ring(n))
                wait_out(pe, "t", "c")
                for c in range(DC):
                    for g in range(4):
                        mm = pe.matmul(o[32 * g:32 * g + 32, 0:128], cT[:, c, :], w[:, c, P * g:P * g + P],
                                       start=(c == 0), stop=(c == DC - 1))
                done(mm, "ada", j)
                o = start("adaT", j)
                wait_out(pe, "ada", j)
                done(turn(o[:, 0:128], adar[:, :]), "adaT", j)

            def proj(m, n, c0):
                o = start("proj", m)
                pe.wait_ge(*ring(n))
                w = fslot[n % FR]
                for c in range(DC):
                    mm = pe.matmul(o[:, 0:NT], w[:, c, c0:c0 + P], hT[:, c, :], start=(c == 0), stop=(c == DC - 1))
                done(mm, "proj", m)

            for j in range(4):
                ada(j)
            pe.wait_ge(sem("h_done"), DC)
            for m in range(14, 22):
                proj(m, 4 + (m - 14) // 4, P * ((m - 14) % 4))
            for m in range(0, 4):
                proj(m, 6, P * m)
            pe.wait_ge(sem("ld_wbd"), 64)
            for c in range(Q):
                pe.wait_ge(sem("conv_done"), c + 1)
                for k, name in enumerate(("gr", "gi")):
                    o = start(name, c)
                    done(pe.matmul(o[:, 0:NT], wbd[k][:, c, :], xc[:, c, :], start=True, stop=True), name, c)
            for m in range(4, MA):
                proj(m, 6 + m // 4, P * (m % 4))
            for j in range(4, 12):
                ada(j)
            pe.wait_ge(sem("consts"), 3)
            pe.wait_ge(sem("consts2"), 5)
            o = start("ssB")
            pe.wait_ge(sem("sqB_done"), 1)
            for c in range(Q):
                mm = pe.matmul(o[:, 0:NT], ones, gi[:, c, :], start=(c == 0), stop=(c == Q - 1))
            done(mm, "ssB")
            pe.wait_ge(sem("ld_lora"), 48)
            pe.wait_ge(sem("z_done"), MA)
            pe.wait_ge(sem("lora_in"), 2)
            for name, w, m, p0, p1 in (("lw", 0, 12, 0, 64), ("la", 0, 12, 64, 128), ("lg", 1, 13, 0, 128)):
                for q in range(Q):
                    o = start(name, q)
                    done(pe.matmul(o[:, 0:NT], lora[p0:p1, w, P * q:P * q + P], z[p0:p1, m, :],
                                   start=True, stop=True), name, q)
            pe.wait_ge(sem("kk2_done"), 1)
            for q in range(Q):
                o = start("kn", q)
                done(pe.matmul(o[:, 0:NT], bones, yT[:, q, :], start=True, stop=True), "kn", q)
            pe.wait_ge(sem("smp_done"), 6)
            for k in range(2):
                o = start("smpT", k)
                for j in range(3):
                    mm = turn(o[0:32, P * j:P * j + P], smp[:, 3 * k + j, :, :].rearrange("p q b -> p (q b)"))
                done(mm, "smpT", k)
            o = start("smpB")
            pe.wait_ge(sem("consts2"), 5)
            wait_out(pe, "smpT", 0)
            wait_out(pe, "smpT", 1)
            for k in range(4):
                h = k // 2
                pe.matmul(o[:, 0:320].rearrange("p (v n) -> p v n", v=5), sel4[0:32, k, :],
                          sv[0:32, 0:5, 64 * h:64 * h + 64], start=(k == 0), stop=(k == 3))
            for k in range(4):
                mm = pe.matmul(o[:, 320:352], sel4[0:32, k, :], sv[0:32, 5, 32 * k:32 * k + 32],
                               start=(k == 0), stop=(k == 3))
            done(mm, "smpB")
            pe.wait_ge(sem("rk_done"), Q)
            for q in range(Q):
                o = start("bo", q)
                done(pe.matmul(o[:, 0:NT], bones, cum[:, q, :], start=True, stop=True), "bo", q)

            pe.wait_ge(sem("bm_done"), 4 * Q)
            for t in range(2):
                tc = slice(P * t, P * t + P)
                srcs = [lambda q: bm[:, q, tc], lambda q: kap[:, q, tc], lambda q: z[:, 8 + q, tc],
                        lambda q: arp[:, q, t, 0, :]]
                for k in range(4):
                    o = start("tk", t, k)
                    for q in range(Q):
                        mm = turn(o[:, P * q:P * q + P], srcs[k](q))
                    done(mm, "tk", t, k)

                def head(h):
                    return slice(64 * (h % 2), 64 * (h % 2) + 64), h // 2

                def unit(h):
                    return 4 * (h % 2) + h // 2

                pairs = {"U": (bm, 0), "L": (None, 0), "Ak": (kap, 0), "Rb": (bm, 1), "Rk": (kap, 1)}
                for k in ("U", "L", "Ak", "Rb", "Rk"):
                    for g in range(2):
                        o = start(k, t, g)
                        for j in range(4):
                            rows_, q = head(2 * j + g)
                            a, kind = pairs[k]
                            lhs = arp[rows_, q, t, 0, :] if a is None else a[rows_, q, tc]
                            rhs = bm[rows_, q, tc] if a is None else arp[rows_, q, t, kind, :]
                            mm = pe.matmul(o[:, P * j:P * j + P], lhs, rhs, start=True, stop=True)
                        done(mm, k, t, g)
                for l in range(1, LEVELS):
                    for g in range(2):
                        o = start("Y", t, g, l)
                        if l == 1:
                            wait_out(pe, "U", t, g)
                            pe.wait_ge(sem("x_init"), 2 * t + g + 1)
                        else:
                            wait_out(pe, "X", t, g, l - 1)
                        for j in range(4):
                            mm = pe.matmul(o[:, P * j:P * j + P], U[:, 4 * g + j, :], X[:, 4 * g + j, :],
                                           start=True, stop=True)
                        done(mm, "Y", t, g, l)
                    if l < LEVELS - 1:
                        for g in range(2):
                            o = start("X", t, g, l)
                            wait_out(pe, "Y", t, g, l)
                            if l == 1:
                                pe.wait_ge(sem("xt_init"), 2 * t + g + 1)
                            else:
                                wait_out(pe, "XT", t, g, l - 1)
                            for j in range(4):
                                mm = pe.matmul(o[:, P * j:P * j + P], XT[:, 4 * g + j, :], Y[:, 4 * g + j, :],
                                               start=True, stop=True)
                            done(mm, "X", t, g, l)
                    for g in range(2):
                        o = start("XT", t, g, l)
                        wait_out(pe, "Y", t, g, l)
                        if l > 1:
                            wait_out(pe, "XT", t, g, l - 1)
                        for j in range(4):
                            mm = pe.matmul(o[:, P * j:P * j + P], Y[:, 4 * g + j, :], XT[:, 4 * g + j, :],
                                           start=True, stop=True)
                        done(mm, "XT", t, g, l)
                for g in range(2):
                    o = start("LV", t, g)
                    wait_out(pe, "Ak", t, g)
                    wait_out(pe, "tk", t, 2)
                    for j in range(4):
                        h = 2 * j + g
                        mm = pe.matmul(o[:, 64 * j:64 * j + 64], Ak[:, 4 * g + j, :], tok[2][:, t, 64 * h:64 * h + 64],
                                       start=True, stop=True)
                    done(mm, "LV", t, g)
                for g in range(2):
                    o = start("Z", t, g)
                    wait_out(pe, "LV", t, g)
                    wait_out(pe, "XT", t, g, LEVELS - 1)
                    for j in range(4):
                        u = 4 * g + j
                        mm = pe.matmul(o[:, 64 * j:64 * j + 64], XT[:, u, :], LV[:, u, :], start=True, stop=True)
                    done(mm, "Z", t, g)
                for g in range(2):
                    o = start("AH", t, g)
                    wait_out(pe, "tk", t, 3)
                    for j in range(4):
                        h = 2 * j + g
                        rows_, q = head(h)
                        mm = pe.matmul(o[rows_, P * q:P * q + P], tok[3][:, t, 64 * h:64 * h + 64],
                                       XT[:, 4 * g + j, :], start=True, stop=True)
                    done(mm, "AH", t, g)
                for c in range(CPT * t, CPT * (t + 1)):
                    r0 = CH * (c % CPT)
                    r = slice(r0, r0 + CH)
                    cc = slice(CH * c, CH * c + CH)
                    for g in range(2):
                        o = start("SA", c, g)
                        wait_out(pe, "AH", t, g)
                        if c == 0:
                            pe.wait_ge(sem("vectors_done"), 1)
                        else:
                            pe.wait_ge(sem("state_done"), c)
                        for j in range(4):
                            rows_, q = head(2 * j + g)
                            mm = pe.matmul(o[r, 64 * j:64 * j + 64], ahT[rows_, q, cc], ST[rows_, c, q, :],
                                           start=True, stop=True)
                        done(mm, "SA", c, g)
                    o = start("SU", c)
                    wait_out(pe, "SA", c, 0)
                    wait_out(pe, "SA", c, 1)
                    wait_out(pe, "tk", t, 0)
                    wait_out(pe, "tk", t, 1)
                    for h in range(H):
                        rows_, q = head(h)
                        hc = slice(64 * h, 64 * h + 64)
                        uc = slice(64 * unit(h), 64 * unit(h) + 64)
                        pe.matmul(o[rows_, 64 * q:64 * q + 64], tok[1][r, t, hc], tok[2][r, t, hc],
                                  start=True, stop=False)
                        mm = pe.matmul(o[rows_, 64 * q:64 * q + 64], tok[0][r, t, hc], SA[r, t, uc],
                                       start=False, stop=True)
                    done(mm, "SU", c)
                o = start("Y1", t)
                for h in range(H):
                    rows_, q = head(h)
                    for c in range(CPT):
                        r0 = CH * c
                        mm = pe.matmul(o[rows_, P * q + r0:P * q + r0 + CH], ST[rows_, CPT * t + c, q, :],
                                       arp[rows_, q, t, 1, r0:r0 + CH], start=True, stop=True)
                done(mm, "Y1", t)
                o = start("Y2", t)
                for k in ("Rb", "Rk"):
                    for g in range(2):
                        wait_out(pe, k, t, g)
                for h in range(H):
                    rows_, q = head(h)
                    u = unit(h)
                    v = o[rows_, P * q:P * q + P]
                    pe.matmul(v, SA[:, t, 64 * u:64 * u + 64], Rb[:, 8 * t + u, :], start=True, stop=False)
                    mm = pe.matmul(v, tok[2][:, t, 64 * h:64 * h + 64], Rk[:, 8 * t + u, :],
                                   start=False, stop=True)
                done(mm, "Y2", t)
            o = start("syT")
            pe.wait_ge(sem("sample_y"), 1)
            done(turn(o[0:32, 0:128], sv[:, 1, 0:32]), "syT")
            o = start("wkv")
            pe.wait_ge(sem("state_done"), NCH)
            for q in range(Q):
                mm = turn(o[0:HN, P * q:P * q + P], ST[:, NCH, q, :])
            done(mm, "wkv")
            wait_out(pe, "Y2", 0)
            wait_out(pe, "Y2", 1)
            wait_out(pe, "syT")
            for q in range(Q):
                o = start("mu", q)
                done(pe.matmul(o[:, 0:NT], bones, yT[:, q, :], start=True, stop=True), "mu", q)
            for q in range(Q):
                o = start("va", q)
                pe.wait_ge(sem("sqy_done"), q + 1)
                done(pe.matmul(o[:, 0:NT], bones, sqy[:, q, :], start=True, stop=True), "va", q)
            for n in range(3):
                o = start("so", n)
                if n == 0:
                    for m in range(MA):
                        wait_out(pe, "proj", m)
                else:
                    pe.wait_ge(sem("conv_state" if n == 1 else "lru_state"), Q if n == 1 else 1)
                src = so[0].rearrange("p b m -> p (b m)") if n == 0 else so[n]
                done(turn(o[0:nso[n], 0:128], src), "so", n)
            pe.wait_ge(sem("ld_xre"), 32)
            pe.wait_ge(sem("ld_wout"), 16)
            pe.wait_ge(sem("mixA_done"), Q)
            pe.wait_ge(sem("mixB_done"), Q)
            for c in range(DC):
                o = start("x2", c)
                for t in range(3):
                    n = P if t < 2 else NB
                    mm = turn(o[:, P * t:P * t + n], xre[0:n, t, P * c:P * c + P])
                done(mm, "x2", c)
                o = start("mo", c)
                for k in range(DC):
                    mm = pe.matmul(o[:, 0:NT], wout[:, k, P * c:P * c + P], mixT[:, k, :],
                                   start=(k == 0), stop=(k == DC - 1))
                done(mm, "mo", c)
            o = start("ss2")
            for c in range(DC):
                pe.wait_ge(sem("sq2_done"), c + 1)
                mm = pe.matmul(o[:, 0:NT], ones, sq2[:, c, :], start=(c == 0), stop=(c == DC - 1))
            done(mm, "ss2")
            pe.wait_ge(sem("ld_router"), 32)
            pe.wait_ge(sem("h2_done"), DC)
            for t in range(3):
                n = P if t < 2 else NB
                o = start("lg2", t)
                pe.matmul(o[0:n, 0:E], ones[0:1, 0:n], rb[0:1, :], start=True, stop=False)
                for c in range(DC):
                    mm = pe.matmul(o[0:n, 0:E], h2T[:, c, P * t:P * t + n], rw[:, c, :], start=False,
                                   stop=(c == DC - 1))
                done(mm, "lg2", t)
            o = start("rank")
            pe.wait_ge(sem("mask_done"), 3)
            pe.wait_ge(sem("iota_ready"), 1)
            pe.matmul(o[:, 0:E], tri[:, :], msk[:, 0, :], start=True, stop=True)
            pe.matmul(o[:, E:2 * E], ones, msk[:, 0, :], start=True, stop=False)
            pe.matmul(o[:, E:2 * E], tri[:, :], msk[:, 1, :], start=False, stop=True)
            pe.matmul(o[0:NB, 2 * E:3 * E], ones[:, 0:NB], msk[:, 0, :], start=True, stop=False)
            pe.matmul(o[0:NB, 2 * E:3 * E], ones[:, 0:NB], msk[:, 1, :], start=False, stop=False)
            mm = pe.matmul(o[0:NB, 2 * E:3 * E], tri[0:NB, 0:NB], msk[0:NB, 2, :], start=False, stop=True)
            done(mm, "rank")
            o = start("cnt")
            pe.matmul(o[0:1, 0:E], ones[:, 0:1], msk[:, 0, :], start=True, stop=False)
            pe.matmul(o[0:1, 0:E], ones[:, 0:1], msk[:, 1, :], start=False, stop=False)
            done(pe.matmul(o[0:1, 0:E], ones[0:NB, 0:1], msk[0:NB, 2, :], start=False, stop=True), "cnt")
            for t in range(3):
                n = P if t < 2 else NB
                for c in range(2):
                    o = start("h2", t, c)
                    for j in range(4):
                        mm = turn(o[0:n, P * j:P * j + P], h2T[:, 4 * c + j, P * t:P * t + n])
                    done(mm, "h2", t, c)
            for c in range(2):
                o = start("g2", c)
                for j in range(4):
                    mm = turn(o[0:NROW, P * j:P * j + P], modT[:, 40 + 4 * c + j, :])
                done(mm, "g2", c)
            assert pos[0] == len(order)

            for b in range(8):
                pe.wait_ge(bank_out[b], taken[b])
            pe.wait_ge(sem("gatew_done"), 4)
            pe.wait_ge(sem("ld_bias"), 48)
            turn(ps[7][0:E, 0:128], gatew[:, 0, :])
            turn(ps[7][0:E, 128:256], gatew[:, 1, :])
            turn(ps[7][0:E, 256:NT], gatew[0:NB, 2, :]).then_inc(sem("gt_turned"), 1)
            pe.wait_ge(sem("gt_copied"), 1)
            for k in range(4):
                t, h = k // 2, k % 2
                pe.matmul(ps[k][:, :], g_sb[0:E, P * t:P * t + P], bd[0:E, 512 * h:512 * h + 512],
                          start=True, stop=True).then_inc(sem("y_bias"), 1)
            for h in range(2):
                mm = pe.matmul(ps[4][64 * h:64 * h + NB, :], g_sb[0:E, T:NT], bd[0:E, 512 * h:512 * h + 512],
                               start=True, stop=True)
            mm.then_inc(sem("y_bias"), 1)

            def gather(n, buf):
                pe.wait_ge(sem("selected"), 4 * n + 4)
                if not isinstance(n, int) or n > 0:
                    pe.wait_ge(sem("x_copied"), n)
                for t in range(3):
                    m = P if t < 2 else NB
                    for h in range(2):
                        mm = pe.matmul(ps[2][64 * h:64 * h + 64, :], Psel[buf][0:m, t, 0:64],
                                       h2tok[0:m, t, 512 * h:512 * h + 512], start=(t == 0), stop=(t == 2))
                mm.then_inc(sem("gathered"), 1)

            def turn_rows(n):
                pe.wait_ge(sem("x_copied"), n + 1)
                if not isinstance(n, int) or n > 0:
                    pe.wait_ge(sem("at_copied"), n)
                for j in range(4):
                    mm = turn(ps[3][:, P * j:P * j + P], Xg[:, P * j:P * j + P])
                mm.then_inc(sem("x_turned"), 1)

            def product(bank_, lhsT, w, bias, buf):
                if bias is not None:
                    for h in range(2):
                        pe.matmul(bank_[64 * h:64 * h + 64, :], selb[buf][0:E, :],
                                  bias[0:E, 512 * h:512 * h + 512], start=True, stop=False)
                for k in range(DC):
                    s0 = P * (k % 4) + 64 * (k // 4)
                    for h in range(2):
                        mm = pe.matmul(bank_[64 * h:64 * h + 64, :], lhsT[:, s0:s0 + 64],
                                       w[:, k, 512 * h:512 * h + 512],
                                       start=(bias is None and k == 0), stop=(k == DC - 1))
                return mm

            def gate_up(n, buf, slot, loaded):
                pe.wait_ge(sem("xt_copied"), n + 1)
                if not isinstance(n, int) or n > 0:
                    pe.wait_ge(sem("g_read"), n)
                loaded(0)
                product(ps[0], XTg, wslot[slot[0]], bg, buf).then_inc(sem("gate_done"), 1)
                if not isinstance(n, int) or n > 0:
                    pe.wait_ge(sem("u_read"), n)
                loaded(1)
                product(ps[1], XTg, wslot[slot[1]], bu, buf).then_inc(sem("up_done"), 1)

            def turn_act(n):
                pe.wait_ge(sem("act_done2"), n + 1)
                pe.wait_ge(sem("xt_copied"), n + 1)
                for j in range(4):
                    mm = turn(ps[3][:, P * j:P * j + P], a_sb[:, P * j:P * j + P])
                mm.then_inc(sem("act_turned"), 1)

            def turn_places(n, buf):
                if not isinstance(n, int) or n > 0:
                    pe.wait_ge(sem("pt_copied"), 2 * n)
                for t in range(3):
                    m = P if t < 2 else NB
                    mm = turn(ps[4][:, P * t:P * t + m], Psel[buf][0:m, t, :])
                mm.then_inc(sem("pt_turned"), 1)

            def down(n, slot, loaded):
                pe.wait_ge(sem("at_copied"), n + 1)
                if not isinstance(n, int) or n > 0:
                    pe.wait_ge(sem("out_copied"), n)
                loaded(2)
                product(ps[5], aT_sb, wslot[slot[2]], None, 0).then_inc(sem("down_done"), 1)

            def scatter(n):
                pe.wait_ge(sem("out_copied"), n + 1)
                pe.wait_ge(sem("pt_copied"), 2 * n + 2)
                for k in range(4):
                    t, h = k // 2, k % 2
                    if k < 2:
                        if not isinstance(n, int) or n > 0:
                            pe.wait_ge(sem("y_added"), 6 * n)
                    else:
                        pe.wait_ge(sem("y_added"), 6 * n + k - 1)
                    pe.matmul(ps[6 + k % 2][:, :], PTz[h][:, P * t:P * t + P], o_sb[:, :], start=True, stop=True)\
                      .then_inc(sem("scattered"), 1)
                pe.wait_ge(sem("y_added"), 6 * n + 3)
                for h in range(2):
                    mm = pe.matmul(ps[6][64 * h:64 * h + NB, :], PTz[h][:, T:NT], o_sb[:, :], start=True, stop=True)
                mm.then_inc(sem("scattered"), 1)

            def slots_of(r):
                return [(3 * r + t) % 4 for t in range(3)]

            def loaded_of(rounds, r):
                def loaded(t):
                    pe.wait_ge(sem(f"w_loaded{(3 * r + t) % 4}"), 48 * rounds + 16 * ((3 * r + t) // 4 + 1))
                return loaded

            def block_step(n, rounds, r, first=False, last=False):
                gate_up(n, r % 2, slots_of(r), loaded_of(rounds, r))
                if not first:
                    scatter(n - 1)
                if not last:
                    gather(n + 1, (r + 1) % 2)
                turn_act(n)
                turn_places(n, r % 2)
                if not last:
                    turn_rows(n + 1)
                down(n, slots_of(r), loaded_of(rounds, r))

            pe.wait_ge(sem("y_ready"), 1)
            gather(0, 0)
            turn_rows(0)
            for r in range(4):
                block_step(r, 0, r, first=(r == 0))
            with pe.Fori(1, E // 4 - 1) as i:
                for r in range(4):
                    block_step(4 * i + r, i, r)
            for r in range(4):
                block_step(E - 4 + r, E // 4 - 1, r, last=(r == 3))
            scatter(E - 1)
            nreg = pe.alloc_register("pe_block")
            c = pe.alloc_register("pe_over")
            pe.reg_load(c, cnt_i[0:1, (OVER + 1) * E:(OVER + 1) * E + 1])
            with pe.If(pe.snap(c) > 0):
                pe.reg_mov(nreg, E)
                with pe.Fori(1, OVER + 1) as b:
                    with pe.Fori(0, E) as e:
                        pe.reg_load(c, cnt_i[0:1, bass.ds(b * E + e, 1)])
                        with pe.If(pe.snap(c) > 0):
                            n = pe.snap(nreg)

                            def again(t):
                                pe.wait_ge(sem("w_again"), 48 * (n - E) + 48)

                            gather(n, 0)
                            turn_rows(n)
                            gate_up(n, 0, [0, 1, 2], again)
                            turn_act(n)
                            turn_places(n, 0)
                            down(n, [0, 1, 2], again)
                            scatter(n)
                            pe.reg_add(nreg, nreg, 1)
                        pe.nop()
                pe.nop()
            pe.nop()
            pe.wait_ge(sem("experts_done"), 1)
            pe.wait_ge(sem("ld_end"), 32)
            for t in range(3):
                n = P if t < 2 else NB
                for c in range(2):
                    for j in range(4):
                        mm = turn(ps[2 * t + c][0:n, P * j:P * j + P], x1o[:, 4 * c + j, P * t:P * t + n])
                    mm.then_inc(sem("x1_turned"), 1)
            for k in range(4):
                t, h = k // 2, k % 2
                if k >= 2:
                    pe.wait_ge(sem("g2_used"), k - 1)
                pe.matmul(ps[6 + k % 2][:, :], sel9[0:NROW, P * t:P * t + P],
                          gate2[0:NROW, 512 * h:512 * h + 512], start=True, stop=True).then_inc(sem("g2_done"), 1)
            pe.wait_ge(sem("g2_used"), 3)
            for h in range(2):
                mm = pe.matmul(ps[6][64 * h:64 * h + NB, :], sel9[0:NROW, T:NT],
                               gate2[0:NROW, 512 * h:512 * h + 512], start=True, stop=True)
            mm.then_inc(sem("g2_done"), 1)


INPUTS = ["x_prompt", "x_sample", "c_prompt", "c_sample", "state_wkv", "state_shift", "state_conv", "state_lru",
          "w_ada", "b_ada", "norm1_g", "norm2_g", "w_in", "rk_mu", "rk_w0", "rk_w_up", "rk_a0", "rk_a_up",
          "rk_g_up", "rk_k_k", "rk_k_a", "rk_r_k", "rk_lnx_w", "rk_lnx_b", "lru_conv_w", "lru_conv_b",
          "lru_w_r", "lru_b_r", "lru_w_i", "lru_b_i", "lru_lambda", "lru_norm_g", "w_out", "router_w",
          "router_b", "w_gate", "b_gate", "w_up", "b_up", "w_down", "b_down", "final_g"]
OUTPUTS = [("y_prompt", (1, T, D)), ("y_sample", (NB, 1, D)), ("wkv_prompt", (1, 1, H, HN, HN)),
           ("shift_prompt", (1, 1, MA * P)), ("conv_prompt", (1, 1, 3, DA)), ("lru_prompt", (1, 1, DA)),
           ("wkv_sample", (1, NB, H, HN, HN)), ("shift_sample", (1, NB, MA * P)),
           ("conv_sample", (1, NB, 3, DA)), ("lru_sample", (1, NB, DA))]


def kernel(**inputs):
    import numpy as _np
    import concourse.bacc as _bacc
    from concourse import mybir as _mybir
    from concourse.bass_utils import run_bass_kernel_spmd as _run

    nc = _bacc.Bacc("TRN2", target_bir_lowering=False, num_devices=1)
    arrays, ins, outs = {}, {}, {}
    for name in INPUTS:
        a = _np.ascontiguousarray(inputs[name])
        arrays[f"in_{name}_dram"] = a
        ins[name] = nc.dram_tensor(f"in_{name}_dram", a.shape, _mybir.dt.from_np(a.dtype), kind="ExternalInput").ap()
    for name, shape in OUTPUTS:
        outs[name] = nc.dram_tensor(f"out_{name}_dram", shape, _mybir.dt.float32, kind="ExternalOutput").ap()
    build(nc, ins, outs)
    r = _run(nc, [arrays], core_ids=[0])
    return tuple(r.results[0][f"out_{name}_dram"] for name, _ in OUTPUTS)
```

```python
from contextlib import ExitStack

import numpy as np

import concourse.bass as bass
from concourse import mybir
from concourse.alu_op_type import AluOpType as ALU

F32 = mybir.dt.float32
I32 = mybir.dt.int32
ACT = mybir.ActivationFunctionType
AX = mybir.AxisListType.X

P = 128
D = 1024
DC = D // P
T = 256
NB = 8
NT = T + NB
DA = 512
Q = DA // P
HN = 64
H = DA // HN
MA = 14
MP = 22
NROW = NB + 1
EXP_HALF = float(np.exp(-0.5))
CH = 64
LEVELS = CH.bit_length() - 1
CPT = P // CH
NCH = T // CH
E = 32
SLOTS = 64
OVER = 4
NPAR = 94

PARAMS = [("rk_mu", 14), ("rk_w0", 4), ("rk_a0", 4), ("rk_k_k", 4), ("rk_k_a", 4), ("rk_r_k", 4),
          ("rk_lnx_w", 4), ("rk_lnx_b", 4), ("lru_conv_w", 16), ("lru_conv_b", 4), ("lru_b_r", 4),
          ("lru_b_i", 4), ("lru_lambda", 4), ("lru_norm_g", 4), ("norm1_g", 8), ("norm2_g", 8)]
PAT = {}
for _n, _k in PARAMS:
    PAT[_n] = sum(k for _, k in PARAMS[:len(PAT)])

UNITS = [("ada", 512 * j, 512) for j in (0, 2, 1, 3)]
UNITS += [("win", 2304, 512), ("win", 1792, 512), ("ada", 2048, 512), ("win", 1536, 256),
          ("ada", 2560, 512), ("win", 512, 512), ("ada", 3072, 512), ("ada", 3584, 512),
          ("win", 0, 512), ("ada", 4096, 512), ("win", 1024, 512)]
UNITS += [("ada", 512 * j, 512) for j in (9, 10, 11)]
FR = 3


def job_list():
    def ada(*units):
        return [x for j in units for x in ((("ada", j), 1), (("adaT", j), 1))]

    def proj_a(*ms):
        return [(("proj", m), 2) for m in ms]

    jobs = [(("t", "c"), 1)] + [(("xT", c), 1) for c in range(DC)]
    jobs += [(("ada", 0), 1), (("ada", 2), 1), (("t", "prm"), 1), (("t", "bada"), 1), (("adaT", 0), 1),
             (("adaT", 2), 1)]
    jobs += ada(1, 3) + proj_a(18, 19, 20, 21)
    jobs += [(("t", n), 1) for n in ("shift", "conv", "lru")]
    jobs += [(("proj", m), 1) for m in range(14, 18)] + [(("ada", 4), 1)]
    for c in range(Q):
        jobs += [(("gr", c), 1), (("gi", c), 1)]
    jobs += [(("adaT", 4), 1)] + proj_a(12, 13) + [(("ada", 5), 1)] + proj_a(4) + [(("adaT", 5), 1)] + proj_a(5)
    jobs += [((k, q), 1) for k in ("lw", "la", "lg") for q in range(Q)]
    jobs += proj_a(6, 7) + [(("ada", 6), 1), (("ada", 7), 1), (("adaT", 6), 1), (("adaT", 7), 1)]
    jobs += proj_a(0, 1, 2, 3)
    jobs += [(("kn", q), 1) for q in range(Q)] + [(("ada", 8), 1)] + proj_a(8) + [(("adaT", 8), 1)]
    jobs += proj_a(9, 10, 11) + [(("ada", 9), 1), (("ssB",), 1), (("ada", 10), 1), (("adaT", 9), 1)]
    jobs += [(("ada", 11), 1), (("adaT", 10), 1), (("adaT", 11), 1)]
    jobs += [(("smpT", 0), 1), (("smpT", 1), 1), (("smpB",), 1)]
    jobs += [(("bo", q), 1) for q in range(Q)]
    def systems(t):
        jobs = []
        for l in range(1, LEVELS):
            jobs += [(("Y", t, g, l), 1) for g in range(2)]
            if l < LEVELS - 1:
                jobs += [(("X", t, g, l), 1) for g in range(2)]
            jobs += [(("XT", t, g, l), 1) for g in range(2)]
        return jobs + [((k, t, g), 1) for k in ("LV", "Z", "AH") for g in range(2)]

    def pairs(t, *ks):
        return [((k, t, g), 1) for k in ks for g in range(2)]

    def sa(c):
        return [(("SA", c, 0), 1), (("SA", c, 1), 1)]

    jobs += [(("tk", 0, k), 1) for k in range(4)] + pairs(0, "U", "L", "Ak", "Rb", "Rk") + systems(0)
    jobs += [(("so", n), 1) for n in range(3)]
    jobs += sa(0) + [(("tk", 1, 0), 1), (("tk", 1, 1), 1), (("SU", 0), 1), (("tk", 1, 2), 1), (("tk", 1, 3), 1)]
    jobs += pairs(1, "U") + sa(1) + pairs(1, "L") + [(("SU", 1), 1)] + pairs(1, "Ak", "Rb", "Rk")
    jobs += systems(1)
    jobs += sa(2) + [(("Y1", 0), 1), (("SU", 2), 1), (("Y2", 0), 1)] + sa(3)
    jobs += [(("syT",), 4), (("mu", 0), 1)] + [(("x2", c), 1) for c in range(4)] + [(("SU", 3), 1)]
    jobs += [(("mu", 2), 1), (("x2", 4), 1), (("x2", 5), 1), (("mB", 0), 2), (("va", 0), 1), (("va", 2), 1)]
    jobs += [(("wkv",), 1), (("Y1", 1), 1), (("Y2", 1), 1), (("x2", 6), 1), (("x2", 7), 1), (("mB", 1), 2)]
    jobs += [(("mu", 1), 1), (("mB", 2), 2), (("mB", 3), 2), (("va", 1), 1)]
    jobs += [(("mB", c), 2) for c in range(4, DC)] + [(("mA", 0), 2), (("ss2",), 1)]
    jobs += [(("mA", c), 2) for c in range(1, DC)]
    jobs += [(("lg2",), 2)]
    jobs += [(("h2", t, c), 1) for t in range(3) for c in range(2)]
    jobs += [(("rank",), 2), (("cnt",), 1)]
    jobs += [(("g2", c), 1) for c in range(2)]
    return jobs


def build(nc, I, O):
    ctx = ExitStack()
    with ctx:
        mem = ctx.enter_context(nc.sbuf_tensor("mem", [P, 53000], F32))
        cnt_i = ctx.enter_context(nc.sbuf_tensor("cnt_i", [1, (OVER + 1) * E + 32], I32))
        ps = [ctx.enter_context(nc.psum_tensor(f"ps{b}", [P, 512], F32)) for b in range(8)]
        x1_dram = nc.dram_tensor("x1_scratch", (P, DC * NT), F32, kind="Internal").ap()

        def view(at, *dims):
            n = int(np.prod(dims))
            flat = mem[:, at:at + n]
            if len(dims) == 1:
                return flat
            names = "abcd"[:len(dims)]
            return flat.rearrange(f"p ({' '.join(names)}) -> p {' '.join(names)}",
                                  **{k: v for k, v in zip(names[1:], dims[1:])})

        class Region:

            def __init__(self, at, end):
                self.at, self.end = at, end

            def take(self, *dims):
                v = view(self.at, *dims)
                self.at += int(np.prod(dims))
                assert self.at <= self.end, (self.at, self.end)
                return v

        keep = Region(49600, 53000)
        ident = keep.take(128)
        ones = keep.take(128)
        iota = keep.take(128)
        prm = keep.take(96)
        modT = keep.take(6 * DC, NROW)
        gatew = keep.take(3, E)
        rankb = keep.take(3, (OVER + 1) * E)
        sel9 = keep.take(NT)
        gate2 = keep.take(D)
        tri = keep.take(128)
        small = keep.take(64)
        eps1, epsx = (small[:, k:k + 1] for k in range(2))
        ssq, rstd = small[:, 8:11], small[:, 12:15]
        squares = view(12288, 3, D)
        wslot = [view(8192 * s, DC, D) for s in range(4)]
        moe = Region(32768, 49600)
        x1T = moe.take(DC, NT)
        h2T = moe.take(DC, NT)
        y = view(32768, 2, D)
        y_s = view(32768 + 2 * D, 512)
        h2tok = moe.take(3, D)
        xre = h2tok
        Xg, XTg, g_sb, sg_sb, u_sb, a_sb, aT_sb, o_sb = (moe.take(512) for _ in range(8))
        bg, bu = moe.take(D), moe.take(D)
        Psel = [moe.take(3, 128) for _ in range(2)]
        PTz = [moe.take(NT) for _ in range(2)]
        selb = [moe.take(64) for _ in range(2)]
        bd = view(32768 + 2 * D + 512, D)
        fslot = [view(4096 * s, DC, 512) for s in range(FR)]
        inv = Region(0, 12288)
        U, X, Y, Ak, XT = (inv.take(8, 128) for _ in range(5))
        Rb, Rk = inv.take(16, 128), inv.take(16, 128)
        Stmp = inv.take(2048)
        sv = inv.take(6, 128)
        wout = view(24576, DC, D)
        dead = Region(24576, 32768)
        z = dead.take(MA, NT)
        sigw, cum, aa, kk = (dead.take(Q, NT) for _ in range(4))
        mid = Region(12288, 24576)
        arp = mid.take(Q, 2, 2, 128)
        bm, kap = mid.take(Q, T), mid.take(Q, T)
        hT = mid.take(DC, NT)
        mixT = hT
        W, gg, yT = mid.take(Q, NT), mid.take(Q, NT), mid.take(Q, NT)
        bv = W
        S = mid.take(2048)
        segm = mid.take(NT)
        smp = mid.take(6, Q, NB)
        ar2 = Region(32768, 49600)
        xflat = ar2.take(Q, 292)
        xc, gb, gr, gi, aB = (ar2.take(Q, NT) for _ in range(5))
        xtok = ar2.take(3, D)
        al = Region(32768, 39216)
        tok = [al.take(2, DA) for _ in range(4)]
        ahT = al.take(Q, T)
        ST = al.take(NCH + 1, Q, HN)
        LV = ar2.take(8, HN)
        diag = view(ar2.at - 512, 3, 128)
        bones = ar2.take(128)
        x2 = view(ar2.at, DC, NT)
        m_su, m_iu, mU0 = (ar2.take(128) for _ in range(3))
        mL = [ar2.take(128) for _ in range(LEVELS)]
        sel4 = ar2.take(4, 128)
        svb = ar2.take(352)
        cT = ar2.take(DC, 32)
        assert ar2.at >= 42928 + DC * NT
        SA = view(ar2.at, 2, DA)
        wbd = [ar2.take(Q, 128) for _ in range(2)]
        so = [ar2.take(NROW, MA), ar2.take(108), ar2.take(36)]
        nso = [126, 108, 36]
        badaT, shiftT, h0T = keep.take(48), keep.take(NB, MA), keep.take(NB, Q)
        A1 = ar2.take(DC, NROW)
        omm, omka, sp = ar2.take(MA), ar2.take(Q), ar2.take(8, Q)
        rows = {n: ar2.take(128) for n in ("c", "prm", "bada", "shift", "conv", "lru")}
        nrows = {"c": 72, "prm": NPAR, "bada": 48, "shift": 112, "conv": 96, "lru": 32}
        sorow = [rows["prm"], rows["bada"], rows["shift"]]
        ar2.at = 49600 - 2048
        Z = view(ar2.at, 2, DA)
        lora = ar2.take(2, DA)
        adar = [ar2.take(512) for _ in range(2)]
        fold = small[:, 16:32]
        gn_sq = [bm.rearrange("p q n -> p (q n)")[:, 512 * k:512 * k + 512].rearrange("p (q n) -> p q n", q=Q)
                 for k in range(2)] + [smp[:, 0, :, :]]
        gn_rs = [kap.rearrange("p q n -> p (q n)")[:, 512 * k:512 * k + 512].rearrange("p (q n) -> p q n", q=Q)
                 for k in range(2)] + [smp[:, 1, :, :]]
        gn_cols = [slice(0, P), slice(P, T), slice(T, NT)]
        late = Region(49600 - 2048, 49600)
        sq2 = x2
        A2 = late.take(DC, NROW)
        rs2 = late.take(NT)
        rw = late.take(DC, E)
        rb = late.take(E)
        lgt = late.take(3, E)
        lbase = late.take(E)
        x1tmp = [late.take(NB) for _ in range(2)]
        late.at = max(late.at, 49600 - 1024)
        wkvo = late.take(Q, 128)
        ex, msk, eq, ce = (late.take(3, E) for _ in range(4))
        top, sc = late.take(3, 8), late.take(3, 8)
        seg = keep.take(3, E)
        gtT = rs2
        fin = Region(0, 8192)
        x1o = fin.take(DC, NT)
        fing = fin.take(D)
        x1t = fin.take(3, D)
        g2b, g2s = fin.take(D), fin.take(512)
        gt, fsq = view(8192, 3, D), view(8192 + 3 * D, 3, D)
        sems = {}

        def sem(name):
            if name not in sems:
                sems[name] = ctx.enter_context(nc.semaphore(name))
            return sems[name]

        bank_full = [sem(f"bank_full{b}") for b in range(8)]
        bank_out = [sem(f"bank_out{b}") for b in range(8)]
        jobs = job_list()
        where, taken = {}, [0] * 8
        for k, (name, n) in enumerate(jobs):
            before = taken[k % 8]
            taken[k % 8] += n
            where[name] = (k % 8, k // 8 + 1, before, taken[k % 8])

        def bank(*name):
            return ps[where[name][0]]

        def wait_full(eng, *name):
            b, n, _, _ = where[name]
            eng.wait_ge(bank_full[b], n)

        def wait_out(eng, *name):
            b, _, _, n = where[name]
            eng.wait_ge(bank_out[b], n)

        count = {}

        def signal(eng, ins, name):
            count[name] = count.get(name, 0) + 1
            ins.then_inc(sem(name), 1)
            eng.wait_ge(sem(name), count[name])

        def mark(ins, name):
            count[name] = count.get(name, 0) + 1
            ins.then_inc(sem(name), 1)

        def settle(eng, name):
            eng.wait_ge(sem(name), count[name])

        def ring(n):
            return sem(f"front_loaded{n % FR}"), 16 * (n // FR + 1)

        unit_of = {("ada", c0 // 512): n for n, (what, c0, _) in enumerate(UNITS) if what == "ada"}
        for n, (what, c0, w) in enumerate(UNITS):
            if what == "win":
                unit_of.update({("win", m): n for m in range(c0 // P, (c0 + w) // P)})
        last_job = {}
        for name, _ in jobs:
            if name[0] in ("ada", "proj"):
                last_job[unit_of[("ada" if name[0] == "ada" else "win", name[1])]] = name

        for n in ("lanes_done", "act_done", "pool_done"):
            sem(n)
        block = ctx.enter_context(nc.Block())

        def vcol(name, k=0):
            return prm[:, PAT[name] + k:PAT[name] + k + 1]

        def mod(i, c, rows_):
            return modT[:, i * DC + c, rows_]

        a_order = [n[1] for n, _ in jobs if n[0] == "proj" and n[1] < MA]

        @block.sync
        def _(sp_):
            def rows_in(dst, src, name):
                sp_.dma_start(dst, src).then_inc(sem(name), 16)

            src = {"ada": I["w_ada"], "win": I["w_in"]}

            def unit_in(n):
                what, c0, w = UNITS[n]
                if n >= FR:
                    wait_full(sp_, *last_job[n - FR])
                sp_.dma_start(fslot[n % FR][:, :, 0:w],
                              src[what][0, :, c0:c0 + w].rearrange("(c p) n -> p c n", p=P))\
                   .then_inc(sem(f"front_loaded{n % FR}"), 16)

            rows_in(rows["c"][0:8, :], I["c_prompt"].rearrange("a (c p) -> (a c) p", p=P), "ld_c")
            rows_in(rows["c"][8:72, :], I["c_sample"].rearrange("a (c p) -> (a c) p", p=P), "ld_c")
            sp_.dma_start(xtok[:, 0:2, :], I["x_prompt"].rearrange("a (t p) d -> p (a t) d", p=P))\
               .then_inc(sem("ld_x"), 16)
            sp_.dma_start(xtok[0:NB, 2, :], I["x_sample"].rearrange("b a d -> (b a) d"))\
               .then_inc(sem("ld_x"), 16)
            unit_in(0)
            rows_in(rows["bada"][0:48, :], I["b_ada"].rearrange("a (c p) -> (a c) p", p=P), "ld_bada")
            unit_in(1)
            unit_in(2)
            for n in range(FR, len(UNITS)):
                unit_in(n)
            wait_out(sp_, "tk", 1, 3)
            wait_out(sp_, "bo", 3)
            sp_.wait_ge(sem("vectors_done"), 1)
            sp_.dma_start(wout[:, :, :], I["w_out"][0].rearrange("(c p) n -> p c n", p=P))\
               .then_inc(sem("ld_wout"), 16)

            mats = [I["w_gate"], I["w_up"], I["w_down"]]

            def load(e, t, slot, signal_sem):
                sp_.dma_start(wslot[slot], mats[t][0, bass.ds(e, 1), :, :]
                              .rearrange("a (c p) n -> p (a c) n", p=P)).then_inc(signal_sem, 16)

            wait_full(sp_, "SU", 3)
            sp_.dma_start(rw[:, :, :], I["router_w"][0].rearrange("(c p) n -> p c n", p=P))\
               .then_inc(sem("ld_router"), 16)
            sp_.dma_start(rb[0:1, :], I["router_b"]).then_inc(sem("ld_router"), 16)
            wait_out(sp_, "Y2", 1)
            sp_.wait_ge(sem("sample_y"), 2)
            load(0, 0, 0, sem("w_loaded0"))
            sp_.wait_ge(sem("mixA_done"), 3)
            load(0, 1, 1, sem("w_loaded1"))
            wait_full(sp_, "mA", DC - 1)
            sp_.wait_ge(sem("states_out"), 16 * 8)
            load(0, 2, 2, sem("w_loaded2"))
            load(1, 0, 3, sem("w_loaded3"))
            sp_.wait_ge(sem("x1_done"), 1)
            sp_.dma_start(x1_dram, x1T.rearrange("p c t -> p (c t)")).then_inc(sem("x1_out"), 16)
            wait_full(sp_, "ss2")
            sp_.dma_start(bg[0:E, :], I["b_gate"][0]).then_inc(sem("ld_bias"), 16)
            sp_.dma_start(bu[0:E, :], I["b_up"][0]).then_inc(sem("ld_bias"), 16)
            for c in range(2):
                wait_full(sp_, "h2", 2, c)
            sp_.dma_start(bd[0:E, :], I["b_down"][0]).then_inc(sem("ld_bdown"), 16)

            def expert_loads(e, r, first=0):
                for t in range(first, 3):
                    slot = (3 * r + t) % 4
                    sp_.wait_ge(sem(("down_done", "gate_done", "up_done")[t]), e - 1 if t == 0 else e)
                    load(e, t, slot, sem(f"w_loaded{slot}"))

            expert_loads(1, 1, first=1)
            expert_loads(2, 2)
            expert_loads(3, 3)
            with sp_.Fori(1, E // 4) as i:
                for r in range(4):
                    expert_loads(4 * i + r, r)
            sp_.wait_ge(sem("down_done"), E - 1)
            sp_.wait_ge(sem("x1_out"), 16)
            sp_.dma_start(x1o.rearrange("p c t -> p (c t)"), x1_dram).then_inc(sem("ld_end"), 16)
            sp_.dma_start(fing[:, :], I["final_g"].rearrange("(a d) -> a d", a=1).broadcast_to([P, D]))\
               .then_inc(sem("ld_end"), 16)
            sp_.wait_ge(sem("router_done"), 1)
            n = sp_.alloc_register("sp_block")
            c = sp_.alloc_register("sp_over")
            sp_.reg_load(c, cnt_i[0:1, (OVER + 1) * E:(OVER + 1) * E + 1])
            with sp_.If(sp_.snap(c) > 0):
                sp_.reg_mov(n, E)
                with sp_.Fori(1, OVER + 1) as b:
                    with sp_.Fori(0, E) as e:
                        sp_.reg_load(c, cnt_i[0:1, bass.ds(b * E + e, 1)])
                        with sp_.If(sp_.snap(c) > 0):
                            sp_.wait_ge(sem("down_done"), sp_.snap(n))
                            for t in range(3):
                                load(e, t, t + 1, sem("w_again"))
                            sp_.reg_add(n, n, 1)
                        sp_.nop()
                sp_.nop()
            sp_.nop()
            for t in range(2):
                sp_.wait_ge(sem("out_ready"), t + 1)
                sp_.dma_start(O["y_prompt"][0, P * t:P * t + P, :], gt[:, t, :]).then_inc(sem("y_out"), 16)
            sp_.wait_ge(sem("out_ready"), 3)
            sp_.dma_start(O["y_sample"].rearrange("b a d -> (b a) d"), gt[0:NB, 2, :])\
               .then_inc(sem("y_out"), 16)
            sp_.wait_ge(sem("y_out"), 48)

        @block.gpsimd
        def _(pool):
            def step(ins, name="pool_done"):
                signal(pool, ins, name)

            def tri_mask(m, cuts):
                step(pool.memset(m, 1.0))
                for v, pattern, base, cm in cuts:
                    step(pool.affine_select(out=v, in_=v, compare_op=ALU.is_ge, fill=0.0, base=base,
                                            pattern=pattern, channel_multiplier=cm))

            step(pool.memset(ident, 0.0))
            step(pool.affine_select(out=ident, in_=ident, compare_op=ALU.not_equal, fill=1.0, base=0,
                                    pattern=[[-1, 128]], channel_multiplier=1), "ident_ready")
            step(pool.memset(ones, 1.0), "consts")
            step(pool.memset(eps1, 1e-6), "consts")
            step(pool.memset(epsx, 64e-5), "consts")
            step(pool.tensor_tensor(fold, ident[:, 0:16], ident[:, 32:48], ALU.add))
            step(pool.tensor_tensor(fold, fold, ident[:, 64:80], ALU.add))
            step(pool.tensor_tensor(fold, fold, ident[:, 96:112], ALU.add), "fold_ready")
            hb = bones.rearrange("p (h n) -> p h n", n=HN)
            tri_mask(bones, [(hb, [[-HN, 2], [0, HN]], 0, 1), (hb, [[HN, 2], [0, HN]], HN - 1, -1)])
            for m, strict in ((m_su, 1), (m_iu, 0)):
                v = m.rearrange("p (c t) -> p c t", t=CH)
                tri_mask(m, [(v, [[-CH, CPT], [0, CH]], 0, 1), (v, [[CH, CPT], [1, CH]], -strict, -1)])
            for l in range(LEVELS):
                b = 1 << l
                v = mL[l].rearrange("p (g h j) -> p g h j", h=2, j=b)
                n = P // (2 * b)
                tri_mask(mL[l], [(v, [[-2 * b, n], [0, 2], [0, b]], -b, 1),
                                 (v, [[2 * b, n], [0, 2], [0, b]], 2 * b - 1, -1),
                                 (v, [[0, n], [-1, 2], [0, b]], 0, 0)])
            v = mU0.rearrange("p (g h j) -> p g h j", h=2, j=1)
            tri_mask(mU0, [(v, [[-2, 64], [0, 2], [0, 1]], 0, 1), (v, [[2, 64], [0, 2], [0, 1]], 0, -1),
                           (v, [[0, 64], [1, 2], [0, 1]], -1, 0)])
            step(pool.memset(segm[:, :], 1.0))
            step(pool.memset(segm[:, 0:T:CH], 0.0))
            step(pool.memset(segm[:, T:NT], 0.0), "consts2")
            step(pool.memset(sel9[0:NROW, :], 0.0))
            step(pool.memset(sel9[0:1, 0:T], 1.0))
            step(pool.affine_select(out=sel9[0:NROW, T:NT], in_=sel9[0:NROW, T:NT],
                                    compare_op=ALU.not_equal, fill=1.0, base=-1, pattern=[[-1, NB]],
                                    channel_multiplier=1))
            step(pool.memset(sel4[0:32, :, :], 0.0))
            for k in range(4):
                v = sel4[0:32, k, :].rearrange("p (b q k) -> p b q k", q=Q, k=4)[:, :, :, k]
                step(pool.affine_select(out=v, in_=v, compare_op=ALU.not_equal, fill=1.0, base=0,
                                        pattern=[[-1, NB], [-NB, Q]], channel_multiplier=1), "consts2")
            tri_mask(tri, [(tri, [[1, 128]], -1, -1)])
            step(pool.iota(iota.bitcast(I32), [[0, 2], [1, 64]], base=0, channel_multiplier=0))
            step(pool.tensor_copy(iota, iota.bitcast(I32)), "iota_ready")

            for t in range(2):
                for g in range(2):
                    u = slice(4 * g, 4 * g + 4)
                    wait_out(pool, "U", t, g)
                    if t == 1:
                        wait_full(pool, "AH", 0, 1)
                    step(pool.tensor_tensor(XT[:, u, :], U[:, u, :],
                                            mU0.unsqueeze(1).to_broadcast([P, 4, 128]), ALU.mult))
                    step(pool.tensor_tensor(XT[:, u, :], XT[:, u, :],
                                            ident.unsqueeze(1).to_broadcast([P, 4, 128]), ALU.add),
                         "xt_init")
                if t == 0:
                    Sv = S.rearrange("p (i j) -> p i j", j=HN)
                    Tv = Stmp.rearrange("p (i j) -> p i j", j=HN)
                    sh = [P, 32, HN]
                    vec = lambda k: svb[:, 64 * k:64 * k + 64].unsqueeze(1).to_broadcast(sh)
                    vrow = svb[:, 320:352].unsqueeze(2).to_broadcast(sh)
                    red = sv[:, 0, 0:32]
                    yrow = sv[:, 1, 0:32]
                    wait_out(pool, "smpB")
                    pool.wait_ge(sem("ld_S"), 16)
                    step(pool.tensor_tensor(Tv, Sv, vec(3), ALU.mult), "sample_steps")
                    pool.wait_ge(sem("sample_red"), 2)
                    step(pool.tensor_tensor(Sv, Sv, vec(2), ALU.mult))
                    step(pool.tensor_tensor(Tv, vec(4), red.unsqueeze(2).to_broadcast(sh), ALU.mult))
                    step(pool.tensor_tensor(Sv, Sv, Tv, ALU.subtract))
                    step(pool.tensor_tensor(Tv, vec(1), vrow, ALU.mult))
                    step(pool.tensor_tensor(Sv, Sv, Tv, ALU.add), "sample_state")
                    step(pool.tensor_tensor(Tv, Sv, vec(0), ALU.mult), "sample_steps")
            pool.wait_ge(sem("vectors_done"), 1)
            for q in range(Q):
                wait_out(pool, "lg", q)
                step(pool.tensor_scalar(bv[:, q, :], bv[:, q, :], vcol("rk_lnx_b", q), None, ALU.add))
                step(pool.tensor_tensor(bv[:, q, :], bv[:, q, :], gg[:, q, :], ALU.mult))
                step(pool.tensor_scalar(gg[:, q, :], gg[:, q, :], vcol("rk_lnx_w", q), None, ALU.mult), "gates_ready")
            pool.wait_ge(sem("states_out"), 16 * 8)
            step(pool.memset(PTz[0][:, :], 0.0), "ptz_zero")
            step(pool.memset(PTz[1][:, :], 0.0), "ptz_zero")
            for g in range(2):
                wait_out(pool, "SA", NCH - 1, g)
            step(pool.memset(seg[:, :, :], 1.0))
            step(pool.memset(seg[:, :, 0:1], 0.0))
            step(pool.memset(lgt[:, 2, :], 0.0), "router_zero")

        @block.scalar
        def _(act):
            def step(ins, name="act_done"):
                signal(act, ins, name)

            def out(ins, *name):
                ins.then_inc(bank_out[where[name][0]], 1)

            act.wait_ge(sem("ld_x"), 32)
            act.wait_ge(sem("consts"), 3)
            for t in range(3):
                n = P if t < 2 else NB
                mark(act.activation(squares[0:n, t, :], xtok[0:n, t, :], ACT.Square, accum_out=ssq[0:n, t:t + 1]),
                     "x_squared")
            settle(act, "x_squared")
            for t in range(3):
                n = P if t < 2 else NB
                mark(act.activation(rstd[0:n, t:t + 1], ssq[0:n, t:t + 1], ACT.Sqrt, bias=eps1[0:n, :],
                                    scale=1.0 / D), "x_root")
            act.wait_ge(sem("ct_zero"), 1)
            wait_full(act, "t", "c")
            out(act.activation(cT[:, :, 0:NROW], bank("t", "c")[:, 0:72].rearrange("p (t c) -> p c t", c=DC),
                               ACT.Silu), "t", "c")
            a0 = 0
            for name, k in PARAMS:
                src = I[name]
                flat = {"rk_r_k": "l h n -> (l h n)", "lru_conv_w": "l w d -> (l w d)"}.get(name, "l d -> (l d)")
                act.dma_start(rows["prm"][a0:a0 + k, :], src.rearrange(flat).rearrange("(r p) -> r p", p=P))\
                   .then_inc(sem("ld_prm"), 16)
                a0 += k
            for c in range(DC):
                wait_full(act, "xT", c)
                out(act.activation(hT[:, c, :], bank("xT", c)[:, 0:NT], ACT.Copy), "xT", c)

            adas = [n[1] for n, _ in jobs if n[0] == "ada"]

            def ada(j):
                k = adas.index(j)
                wait_full(act, "ada", j)
                if k > 1:
                    wait_full(act, "adaT", adas[k - 2])
                out(act.activation(adar[k % 2][:, :], bank("ada", j)[:, :], ACT.Copy), "ada", j)

            def proj_a(*ms):
                for m in ms:
                    wait_full(act, "proj", m)
                    act.wait_ge(sem("derived"), 1)
                    out(act.activation(so[0][:, :, m], bank("proj", m)[:, T - 1:NT], ACT.Copy), "proj", m)
                    mark(act.activation(z[:, m, :], bank("proj", m)[:, 0:NT], ACT.Copy, scale=omm[:, m:m + 1]),
                         "z_part")

            for j in (0, 2, 1, 3):
                ada(j)
            for name, pat in (("shift", "l b (c p) -> (l b c) p"), ("conv", "l b w (c p) -> (l b w c) p"),
                              ("lru", "l b (c p) -> (l b c) p")):
                act.dma_start(rows[name][0:nrows[name], :], I["state_" + name].rearrange(pat, p=P))\
                   .then_inc(sem("ld_rows"), 16)
            act.dma_start(lora[0:64, 0, :], I["rk_w_up"][0]).then_inc(sem("ld_lora"), 16)
            act.dma_start(lora[64:128, 0, :], I["rk_a_up"][0]).then_inc(sem("ld_lora"), 16)
            act.dma_start(lora[:, 1, :], I["rk_g_up"][0]).then_inc(sem("ld_lora"), 16)
            act.wait_ge(sem("wbd_zero"), 1)
            for k, name in enumerate(("lru_w_r", "lru_w_i")):
                w = I[name][0].rearrange("(q h) c d -> h c q d", h=2)
                act.dma_start(wbd[k][0:64, :, 0:64], w[0]).then_inc(sem("ld_wbd"), 16)
                act.dma_start(wbd[k][64:128, :, 64:128], w[1]).then_inc(sem("ld_wbd"), 16)
            act.dma_start(S[:, :], I["state_wkv"][0].rearrange("b h (s i) j -> (b h s) (i j)", s=2))\
               .then_inc(sem("ld_S"), 16)

            act.wait_ge(sem("xflat_zero"), 1)
            for m in range(18, 22):
                c = m - 18
                wait_full(act, "proj", m)
                out(act.activation(xflat[:, c, 3:3 + T], bank("proj", m)[:, 0:T], ACT.Copy), "proj", m)
                out(act.activation(xflat[:, c, 259:291].rearrange("p (b w) -> p b w", w=4)[:, :, 3],
                                   bank("proj", m)[:, T:NT], ACT.Copy), "proj", m)
            act.wait_ge(sem("sp_one"), 1)
            step(act.activation(sp[:, 1, :], sp[:, 0, :], ACT.Exp, scale=-1.0), "sp_exp")
            for m in range(14, 18):
                wait_full(act, "proj", m)
                out(act.activation(gb[:, m - 14, :], bank("proj", m)[:, 0:NT], ACT.Gelu_apprx_tanh),
                    "proj", m)
            ada(4)
            for c in range(Q):
                wait_full(act, "gr", c)
                out(act.activation(gr[:, c, :], bank("gr", c)[:, 0:NT], ACT.Sigmoid, bias=vcol("lru_b_r", c)),
                    "gr", c)
                wait_full(act, "gi", c)
                out(act.activation(gi[:, c, :], bank("gi", c)[:, 0:NT], ACT.Sigmoid, bias=vcol("lru_b_i", c)),
                    "gi", c)
            proj_a(12, 13)
            act.wait_ge(sem("sp_done"), 1)
            for c in range(Q):
                wait_out(act, "gr", c)
                mark(act.activation(aB[:, c, :], gr[:, c, :], ACT.Exp, scale=sp[:, 3, c:c + 1]), "lru_a")
            settle(act, "lru_a")
            ada(5)
            for c in range(Q):
                mark(act.activation(gr[:, c, :], gr[:, c, :], ACT.Tanh, scale=sp[:, 2, c:c + 1]), "lru_th")
            act.wait_ge(sem("z_done"), 2)
            mark(act.activation(z[0:64, 12, :], z[0:64, 12, :], ACT.Tanh), "lora_in")
            mark(act.activation(z[:, 13, :], z[:, 13, :], ACT.Sigmoid), "lora_in")
            proj_a(4, 5)
            for q in range(Q):
                wait_full(act, "lw", q)
                out(act.activation(sigw[:, q, :], bank("lw", q)[:, 0:NT], ACT.Sigmoid, bias=vcol("rk_w0", q)),
                    "lw", q)
            for q in range(Q):
                wait_full(act, "la", q)
                out(act.activation(aa[:, q, :], bank("la", q)[:, 0:NT], ACT.Sigmoid, bias=vcol("rk_a0", q)),
                    "la", q)
            for q in range(Q):
                wait_full(act, "lg", q)
                out(act.activation(gg[:, q, :], bank("lg", q)[:, 0:NT], ACT.Copy), "lg", q)
            proj_a(6, 7)
            act.wait_ge(sem("lru_b2"), 1)
            step(act.activation(gr[:, :, :], gr[:, :, :], ACT.Sqrt), "lru_root")
            ada(6)
            ada(7)
            proj_a(0, 1, 2, 3)
            act.wait_ge(sem("cum_done"), Q + 1)
            step(act.activation(W[:, :, :], cum[:, :, :], ACT.Exp, scale=-EXP_HALF), "decays")
            mark(act.activation(cum[:, :, :], cum[:, :, :], ACT.Exp, scale=EXP_HALF), "decays")
            mark(act.activation(sigw[:, :, :], sigw[:, :, :], ACT.Exp, scale=-EXP_HALF), "decays")
            for q in range(Q):
                wait_full(act, "kn", q)
                act.wait_ge(sem("kk2_done"), 1)
                out(act.activation(yT[:, q, :], bank("kn", q)[:, 0:NT], ACT.Sqrt), "kn", q)
            ada(8)
            proj_a(8, 9, 10, 11)
            ada(9)
            wait_full(act, "ssB")
            out(act.activation(gr[:, 0, :], bank("ssB")[:, 0:NT], ACT.Sqrt, bias=eps1, scale=1.0 / DA), "ssB")
            ada(10)
            ada(11)
            for k in range(2):
                wait_full(act, "smpT", k)
                out(act.activation(sv[0:32, 3 * k:3 * k + 3, :].rearrange("p k n -> p (k n)"),
                                   bank("smpT", k)[0:32, 0:384], ACT.Copy), "smpT", k)
            wait_full(act, "smpB")
            out(act.activation(svb[:, :], bank("smpB")[:, 0:352], ACT.Copy), "smpB")
            def tk_copies(t, ks):
                for k in ks:
                    wait_full(act, "tk", t, k)
                    out(act.activation(tok[k][:, t, :], bank("tk", t, k)[:, :], ACT.Copy), "tk", t, k)

            def u_copies(t):
                for g in range(2):
                    wait_full(act, "U", t, g)
                    out(act.activation(U[:, 4 * g:4 * g + 4, :].rearrange("p u n -> p (u n)"),
                                       bank("U", t, g)[:, :], ACT.Copy), "U", t, g)

            def system_copies(t):
                for k in ("LV", "Z", "AH"):
                    for g in range(2):
                        wait_full(act, k, t, g)
                        b = bank(k, t, g)
                        if k == "LV":
                            dst, b = LV[:, 4 * g:4 * g + 4, :].rearrange("p u n -> p (u n)"), b[:, 0:256]
                        elif k == "Z":
                            dst, b = Z[:, t, 256 * g:256 * g + 256], b[:, 0:256]
                        else:
                            rows_ = slice(64 * g, 64 * g + 64)
                            dst, b = ahT[rows_, :, P * t:P * t + P], b[rows_, :].rearrange("p (q n) -> p q n", q=Q)
                        out(act.activation(dst, b, ACT.Copy), k, t, g)

            def y1_copy(t):
                wait_full(act, "Y1", t)
                out(act.activation(yT[:, :, P * t:P * t + P],
                                   bank("Y1", t)[:, :].rearrange("p (q n) -> p q n", q=Q), ACT.Copy), "Y1", t)

            def x2_copies(cs):
                for c in cs:
                    wait_full(act, "x2", c)
                    out(act.activation(x2[:, c, :], bank("x2", c)[:, 0:NT], ACT.Copy), "x2", c)

            def root(k):
                wait_full(act, "va", k)
                n = gn_cols[k].stop - gn_cols[k].start
                out(act.activation(gn_rs[k], bank("va", k)[:, 0:Q * n].rearrange("p (q n) -> p q n", q=Q),
                                   ACT.Sqrt, bias=epsx, scale=1.0 / HN), "va", k)

            def state(dst, src):
                act.dma_start(dst, src).then_inc(sem("states_out"), 16)

            tk_copies(0, range(4))
            u_copies(0)
            system_copies(0)
            for n in range(3):
                wait_full(act, "so", n)
                out(act.activation(sorow[n][0:nso[n], :], bank("so", n)[0:nso[n], 0:128], ACT.Copy), "so", n)
            tk_copies(1, range(4))
            u_copies(1)
            for n in range(3):
                wait_out(act, "so", n)
            state(O["shift_prompt"].rearrange("a b (m p) -> (a b m) p", p=P), sorow[0][0:14, :])
            state(O["shift_sample"].rearrange("a b (m p) -> (a b m) p", p=P), sorow[0][14:126, :])
            state(O["conv_prompt"].rearrange("a b w (c p) -> (a b w c) p", p=P), sorow[1][0:12, :])
            state(O["conv_sample"].rearrange("a b w (c p) -> (a b w c) p", p=P), sorow[1][12:108, :])
            state(O["lru_prompt"].rearrange("a b (c p) -> (a b c) p", p=P), sorow[2][0:4, :])
            state(O["lru_sample"].rearrange("a b (c p) -> (a b c) p", p=P), sorow[2][4:36, :])
            act.wait_ge(sem("sample_state"), 1)
            state(O["wkv_sample"][0].rearrange("b h (s i) j -> (b h s) (i j)", s=2), S[:, :])
            system_copies(1)
            y1_copy(0)
            act.wait_ge(sem("sample_y"), 2)
            for g in range(2):
                wait_out(act, "XT", 1, g, LEVELS - 1)
            x2_copies(range(0, 6))
            root(0)
            root(2)
            wait_full(act, "wkv")
            out(act.activation(wkvo[0:HN, :, :].rearrange("p q n -> p (q n)"), bank("wkv")[0:HN, :], ACT.Copy),
                "wkv")
            y1_copy(1)
            x2_copies(range(6, DC))
            wait_out(act, "wkv")
            state(O["wkv_prompt"].rearrange("a b h i j -> i (a b h) j"),
                  wkvo[0:HN, :, :].rearrange("p q (t j) -> p (q t) j", t=2))
            root(1)
            wait_full(act, "ss2")
            out(act.activation(rs2[:, :], bank("ss2")[:, 0:NT], ACT.Sqrt, bias=eps1, scale=1.0 / D), "ss2")
            for c in range(DC):
                act.wait_ge(sem("h2_scaled"), c + 1)
                mark(act.activation(h2T[:, c, 0:T], h2T[:, c, 0:T], ACT.Identity, bias=mod(3, c, slice(0, 1))),
                     "h2_done")
            for t in range(3):
                for c in range(2):
                    n = P if t < 2 else NB
                    if (t, c) == (1, 0):
                        act.wait_ge(sem("gates_in"), 1)
                        mark(act.activation(ex[:, :, :], ex[:, :, :], ACT.Exp), "gates_exp")
                    wait_full(act, "h2", t, c)
                    out(act.activation(h2tok[0:n, t, 512 * c:512 * c + 512], bank("h2", t, c)[0:n, :], ACT.Copy),
                        "h2", t, c)
            for c in range(2):
                wait_full(act, "g2", c)
                out(act.activation(gate2[0:NROW, 512 * c:512 * c + 512], bank("g2", c)[0:NROW, :], ACT.Copy),
                    "g2", c)

            def x_copy(n):
                act.wait_ge(sem("gathered"), n + 1)
                act.activation(Xg[:, :], ps[2][:, :], ACT.Copy).then_inc(sem("x_copied"), 1)

            def xt_copy(n):
                act.wait_ge(sem("x_turned"), n + 1)
                act.activation(XTg[:, :], ps[3][:, :], ACT.Copy).then_inc(sem("xt_copied"), 1)

            def sigmoid(n):
                act.wait_ge(sem("g_read"), n + 1)
                if not isinstance(n, int) or n > 0:
                    act.wait_ge(sem("glu_done"), n)
                act.activation(sg_sb[:, :], g_sb[:, :], ACT.Sigmoid, scale=1.702).then_inc(sem("sig_done"), 1)

            def at_copy(n):
                act.wait_ge(sem("act_turned"), n + 1)
                act.activation(aT_sb[:, :], ps[3][:, :], ACT.Copy).then_inc(sem("at_copied"), 1)

            def pt_copy(n):
                act.wait_ge(sem("pt_turned"), n + 1)
                act.activation(PTz[0][0:64, :], ps[4][0:64, 0:NT], ACT.Copy).then_inc(sem("pt_copied"), 1)
                act.activation(PTz[1][64:128, :], ps[4][64:128, 0:NT], ACT.Copy).then_inc(sem("pt_copied"), 1)

            def out_copy(n):
                act.wait_ge(sem("down_done"), n + 1)
                act.activation(o_sb[:, :], ps[5][:, :], ACT.Copy).then_inc(sem("out_copied"), 1)

            def block_step(n, last=False):
                sigmoid(n)
                if not last:
                    x_copy(n + 1)
                at_copy(n)
                pt_copy(n)
                if not last:
                    xt_copy(n + 1)
                out_copy(n)

            act.wait_ge(sem("ptz_zero"), 2)
            x_copy(0)
            xt_copy(0)
            for r in range(4):
                block_step(r)
            with act.Fori(1, E // 4 - 1) as i:
                for r in range(4):
                    block_step(4 * i + r)
            for r in range(4):
                block_step(E - 4 + r, last=(r == 3))
            for t in range(3):
                n = P if t < 2 else NB
                for c in range(2):
                    act.wait_ge(sem("x1_turned"), 2 * t + c + 1)
                    act.activation(x1t[0:n, t, 512 * c:512 * c + 512], ps[(2 * t + c) % 5][0:n, :], ACT.Copy)\
                       .then_inc(sem("x1_copied"), 1)
            for k in range(3):
                act.wait_ge(sem("g2_done"), k + 1)
                dst = g2b[:, 512 * k:512 * k + 512] if k < 2 else g2s[:, :]
                act.activation(dst, ps[1 + k][:, :], ACT.Copy).then_inc(sem("g2_copied"), 1)
            n = act.alloc_register("act_block")
            c = act.alloc_register("act_over")
            act.reg_load(c, cnt_i[0:1, (OVER + 1) * E:(OVER + 1) * E + 1])
            with act.If(act.snap(c) > 0):
                act.reg_mov(n, E)
                with act.Fori(1, OVER + 1) as b:
                    with act.Fori(0, E) as e:
                        act.reg_load(c, cnt_i[0:1, bass.ds(b * E + e, 1)])
                        with act.If(act.snap(c) > 0):
                            k = act.snap(n)
                            x_copy(k)
                            xt_copy(k)
                            block_step(k, last=True)
                            act.reg_add(n, n, 1)
                        act.nop()
                act.nop()
            act.nop()
            for t in range(3):
                n = P if t < 2 else NB
                act.wait_ge(sem("x3_ready"), t + 1)
                act.activation(fsq[0:n, t, :], gt[0:n, t, :], ACT.Square, accum_out=ssq[0:n, t:t + 1])\
                   .then_inc(sem("ss3_done"), 1)
                act.wait_ge(sem("ss3_done"), t + 1)
                act.activation(rstd[0:n, t:t + 1], ssq[0:n, t:t + 1], ACT.Sqrt, bias=eps1[0:n, :],
                               scale=1.0 / D).then_inc(sem("root3"), 1)
            act.wait_ge(sem("states_out"), 16 * 8)

        @block.vector
        def _(dve):
            def step(ins, name="lanes_done"):
                signal(dve, ins, name)

            def out(ins, *name):
                b, _, before, after = where[name]
                ins.then_inc(bank_out[b], 1)

            def tt(o, a, b, op, name="lanes_done"):
                step(dve.tensor_tensor(o, a, b, op), name)

            def ts(o, a, s1, s2, op0, op1=ALU.bypass, name="lanes_done"):
                step(dve.tensor_scalar(o, a, s1, s2, op0, op1), name)

            def stt(o, a, s, b, op0, op1, name="lanes_done"):
                step(dve.scalar_tensor_tensor(out=o, in0=a, scalar=s, in1=b, op0=op0, op1=op1), name)

            step(dve.memset(cT[:, :, :], 0.0), "ct_zero")
            step(dve.memset(wbd[0][:, :, :], 0.0))
            step(dve.memset(wbd[1][:, :, :], 0.0), "wbd_zero")
            step(dve.memset(xflat[:, :, :], 0.0), "xflat_zero")
            step(dve.memset(cnt_i[:, :], 0), "count_zero")
            dve.wait_ge(sem("ident_ready"), 1)
            dve.wait_ge(sem("x_root"), 3)
            for t in range(3):
                n = P if t < 2 else NB
                step(dve.reciprocal(rstd[0:n, t:t + 1], rstd[0:n, t:t + 1]))
                ts(diag[0:n, t, 0:n], ident[0:n, 0:n], rstd[0:n, t:t + 1], None, ALU.mult, name="diag_ready")

            def column_vectors(name, dst):
                wait_full(dve, "t", name)
                src = bank("t", name)[:, 0:nrows[name]]
                if name == "conv":
                    dst = xflat[:, :, 259:291].rearrange("p c (b w) -> p c b w", w=4)
                    src = src.rearrange("p (b w c) -> p c b w", w=3, c=Q)
                    for c in range(Q):
                        ins = dve.tensor_copy(dst[:, c, :, 0:3], src[:, c, :, :])
                        if c < Q - 1:
                            step(ins)
                    out(ins, "t", name)
                else:
                    out(dve.tensor_copy(dst, src), "t", name)
                wait_out(dve, "t", name)

            column_vectors("prm", prm[:, 0:NPAR])
            column_vectors("bada", badaT[:, :])

            def adaT(j):
                wait_full(dve, "adaT", j)
                out(dve.tensor_tensor(modT[:, 4 * j:4 * j + 4, :],
                                      bank("adaT", j)[:, 0:64].rearrange("p (g r) -> p g r", g=4)[:, :, 0:NROW],
                                      badaT[:, 4 * j:4 * j + 4].unsqueeze(2).to_broadcast([P, 4, NROW]),
                                      ALU.add), "adaT", j)
                wait_out(dve, "adaT", j)

            def gains(A, scale, norm, cs):
                ts(A[:, cs, :], modT[:, scale * DC + cs.start:scale * DC + cs.stop, :], 1.0, None, ALU.add)
                g_ = prm[:, PAT[norm] + cs.start:PAT[norm] + cs.stop]
                tt(A[:, cs, :], A[:, cs, :], g_.unsqueeze(2).to_broadcast([P, cs.stop - cs.start, NROW]), ALU.mult)

            def affine(v, A, shift, cs, name):
                tt(v[:, cs, T:NT], v[:, cs, T:NT], A[:, cs, 1:NROW], ALU.mult)
                tt(v[:, cs, T:NT], v[:, cs, T:NT], modT[:, shift * DC + cs.start:shift * DC + cs.stop, 1:NROW],
                   ALU.add)
                for c in range(cs.start, cs.stop):
                    mark(dve.tensor_scalar(v[:, c, 0:T], v[:, c, 0:T], A[:, c, 0:1], mod(shift, c, slice(0, 1)),
                                           ALU.mult, ALU.add), name)

            for c0, js in ((0, (0, 2)), (4, (1, 3))):
                cs = slice(c0, c0 + 4)
                for j in js:
                    adaT(j)
                for c in range(c0, c0 + 4):
                    wait_out(dve, "xT", c)
                gains(A1, 1, "norm1_g", cs)
                affine(hT, A1, 0, cs, "h_done")
            ts(omm[:, :], prm[:, 0:MA], -1.0, 1.0, ALU.mult, ALU.add, name="derived")
            ka = prm[:, PAT["rk_k_a"]:PAT["rk_k_a"] + Q]
            ts(omka[:, :], ka, -1.0, 1.0, ALU.mult, ALU.add)
            lam = prm[:, PAT["lru_lambda"]:PAT["lru_lambda"] + Q]
            ts(sp[:, 4, :], lam, -1.0, None, ALU.mult)
            tt(sp[:, 0, :], sp[:, 4, :], lam, ALU.max, name="sp_one")
            column_vectors("shift", shiftT.rearrange("p b m -> p (b m)"))
            column_vectors("conv", None)
            column_vectors("lru", h0T.rearrange("p b c -> p (b c)"))

            dve.wait_ge(sem("sp_exp"), 1)
            e_, s_, s2_, q_ = (sp[:, k, :] for k in (1, 5, 6, 7))
            ts(q_, e_, 2.0, None, ALU.add)
            step(dve.reciprocal(q_, q_))
            tt(s_, e_, q_, ALU.mult)
            tt(s2_, s_, s_, ALU.mult)
            ts(q_, s2_, 1.0 / 17, None, ALU.mult)
            for k in (15, 13, 11, 9, 7, 5, 3):
                stt(q_, q_, 1.0 / k, s2_, ALU.add, ALU.mult)
            stt(q_, q_, 1.0, s_, ALU.add, ALU.mult)
            ts(sp[:, 4, :], sp[:, 4, :], 0.0, None, ALU.max)
            stt(q_, q_, 2.0, sp[:, 4, :], ALU.mult, ALU.add)
            ts(sp[:, 2, :], q_, 8.0, None, ALU.mult)
            ts(sp[:, 3, :], q_, -8.0, None, ALU.mult, name="sp_done")

            cw = lambda j, c: vcol("lru_conv_w", 4 * j + c)
            for c in range(Q):
                wait_out(dve, "proj", 18 + c)
                wait_out(dve, "t", "conv")
                tmp = aB.rearrange("p c n -> p (c n)")[:, 0:288]
                ts(tmp, xflat[:, c, 0:288], cw(0, c), vcol("lru_conv_b", c), ALU.mult, ALU.add)
                stt(tmp, xflat[:, c, 1:289], cw(1, c), tmp, ALU.mult, ALU.add)
                stt(tmp, xflat[:, c, 2:290], cw(2, c), tmp, ALU.mult, ALU.add)
                stt(xc[:, c, 0:T], xflat[:, c, 3:259], cw(3, c), tmp[:, 0:T], ALU.mult, ALU.add)
                smp_x = xflat[:, c, 259:291].rearrange("p (b w) -> p b w", w=4)[:, :, 3]
                smp_t = aB.rearrange("p c n -> p (c n)")[:, 259:291].rearrange("p (b w) -> p b w", w=4)[:, :, 0]
                stt(xc[:, c, T:NT], smp_x, cw(3, c), smp_t, ALU.mult, ALU.add, name="conv_done")
            adaT(4)
            for c in range(Q):
                step(dve.tensor_copy(so[1][:, 0:12].rearrange("p (w c) -> p c w", c=Q)[:, c, :],
                                     xflat[:, c, 256:259]))
                step(dve.tensor_copy(so[1][:, 12:108].rearrange("p (b w c) -> p c b w", c=Q, w=3)[:, c, :, :],
                                     xflat[:, c, 259:291].rearrange("p (b w) -> p b w", w=4)[:, :, 1:4]), "conv_state")

            def mix_shift(*ms):
                for m in ms:
                    wait_full(dve, "proj", m)
                    dve.wait_ge(sem("z_part"), a_order.index(m) + 1)
                    out(dve.scalar_tensor_tensor(out=z[:, m, 1:T], in0=bank("proj", m)[:, 0:T - 1],
                                                 scalar=vcol("rk_mu", m), in1=z[:, m, 1:T],
                                                 op0=ALU.mult, op1=ALU.add), "proj", m)
                    mark(dve.scalar_tensor_tensor(out=z[:, m, T:NT], in0=shiftT[:, :, m], scalar=vcol("rk_mu", m),
                                                  in1=z[:, m, T:NT], op0=ALU.mult, op1=ALU.add), "z_done")

            def z_ready(*ms):
                for m in ms:
                    wait_out(dve, "proj", m)
                dve.wait_ge(sem("z_done"), max(a_order.index(m) for m in ms) + 1)

            mix_shift(12, 13)
            adaT(5)
            mix_shift(4, 5)
            dve.wait_ge(sem("lru_a"), Q)
            dve.wait_ge(sem("lru_th"), Q)
            for c in range(Q):
                wait_out(dve, "gi", c)
            tt(gi[:, :, :], gi[:, :, :], xc[:, :, :], ALU.mult)
            tt(xc[:, :, :], aB[:, :, :], aB[:, :, :], ALU.mult)
            stt(gr[:, :, :], xc[:, :, :], 1.0, gr[:, :, :], ALU.add, ALU.mult, name="lru_b2")
            dve.wait_ge(sem("consts2"), 1)
            for q in range(Q):
                wait_out(dve, "lw", q)
                mark(dve.tensor_tensor_scan(cum[:, q, :], segm[:, :], sigw[:, q, :], 0.0, ALU.mult, ALU.add),
                     "cum_done")
            settle(dve, "cum_done")
            tt(sigw[:, :, :], cum[:, :, :], sigw[:, :, :], ALU.subtract, name="cum_done")
            mix_shift(6, 7)
            z_ready(4, 5, 6, 7)
            for q in range(Q):
                mark(dve.tensor_scalar(kk[:, q, :], z[:, 4 + q, :], vcol("rk_k_k", q), None, ALU.mult), "kk_done")
            settle(dve, "kk_done")
            tt(yT[:, :, :], kk[:, :, :], kk[:, :, :], ALU.mult, name="kk2_done")
            adaT(6)
            adaT(7)
            dve.wait_ge(sem("lru_root"), 1)
            tt(gi[:, :, :], gi[:, :, :], gr[:, :, :], ALU.mult)
            for c in range(Q):
                mark(dve.tensor_tensor_scan(xc[:, c, 0:T], aB[:, c, 0:T], gi[:, c, 0:T], 0.0, ALU.mult, ALU.add),
                     "lanes_done")
            h0 = h0T.rearrange("p b c -> p c b")
            tt(xc[:, :, T:NT], aB[:, :, T:NT], h0, ALU.mult)
            tt(xc[:, :, T:NT], xc[:, :, T:NT], gi[:, :, T:NT], ALU.add)
            mix_shift(0, 1)
            step(dve.tensor_copy(so[2][:, 0:4].unsqueeze(2), xc[:, :, T - 1:T]))
            step(dve.tensor_copy(so[2][:, 4:36].rearrange("p (b c) -> p c b", c=Q), xc[:, :, T:NT]), "lru_state")
            for c in range(Q):
                wait_out(dve, "proj", 14 + c)
            tt(xc[:, :, :], xc[:, :, :], gb[:, :, :], ALU.mult)
            tt(gi[:, :, :], xc[:, :, :], xc[:, :, :], ALU.mult, name="sqB_done")
            mix_shift(2, 3)

            zk = z[:, 4:8, :]
            for q in range(Q):
                wait_out(dve, "la", q)
            arp_flat = arp.rearrange("p q t k n -> p (q t k n)")
            fq = [arp_flat[:, 512 * q:512 * q + NT] for q in range(Q)]
            for q in range(Q):
                mark(dve.tensor_scalar(fq[q], aa[:, q, :], vcol("rk_k_a", q), omka[:, q:q + 1], ALU.mult, ALU.add),
                     "lanes_done")
            settle(dve, "lanes_done")
            for q in range(Q):
                mark(dve.tensor_tensor(z[:, 4 + q, :], z[:, 4 + q, :], fq[q], ALU.mult), "lanes_done")
            for q in range(Q):
                wait_out(dve, "kn", q)
            ts(yT[:, :, :], yT[:, :, :], 1e-12, None, ALU.max)
            step(dve.reciprocal(yT[:, :, :], yT[:, :, :]))
            tt(kk[:, :, :], kk[:, :, :], yT[:, :, :], ALU.mult)
            tt(aa[:, :, :], kk[:, :, :], aa[:, :, :], ALU.mult)
            adaT(8)
            dve.wait_ge(sem("decays"), 3)
            z_ready(0, 1, 2, 3)
            zr, zv = z[:, 0:4, :], z[:, 8:12, :]
            two = lambda v: v.rearrange("p (t n) -> p t n", t=2)
            for q in range(Q):
                if q % 2 == 0:
                    mix_shift(8 + q // 2)
                for ins in (
                        dve.scalar_tensor_tensor(out=bm[:, q, :], in0=aa[:, q, 0:T], scalar=-1.0,
                                                 in1=cum[:, q, 0:T], op0=ALU.mult, op1=ALU.mult),
                        dve.tensor_tensor(kap[:, q, :], z[:, 4 + q, 0:T], cum[:, q, 0:T], ALU.mult),
                        dve.tensor_tensor(arp[:, q, :, 0, :], two(kk[:, q, 0:T]), two(sigw[:, q, 0:T]), ALU.mult),
                        dve.tensor_tensor(arp[:, q, :, 1, :], two(z[:, q, 0:T]), two(W[:, q, 0:T]), ALU.mult)):
                    mark(ins, "bm_done")
            settle(dve, "bm_done")
            for q in range(Q):
                mark(dve.scalar_tensor_tensor(out=cum[:, q, :], in0=z[:, q, :], scalar=vcol("rk_r_k", q),
                                              in1=z[:, 4 + q, :], op0=ALU.mult, op1=ALU.mult), "rk_done")
            mix_shift(10, 11)
            z_ready(8, 9, 10, 11)
            for k, src in enumerate((zr, zk, W, kk, aa, zv)):
                mark(dve.tensor_copy(smp[:, k, :, :], src[:, :, T:NT]), "smp_done")
            wait_out(dve, "ssB")
            step(dve.reciprocal(gr[:, 0, :], gr[:, 0, :]))
            for c in range(Q):
                mark(dve.scalar_tensor_tensor(out=mixT[:, Q + c, :], in0=xc[:, c, :], scalar=vcol("lru_norm_g", c),
                                              in1=gr[:, 0, :], op0=ALU.mult, op1=ALU.mult), "mixB_done")
            for j in (9, 10, 11):
                adaT(j)
            wend = sp[:, 0:8, :].rearrange("p a b -> p (a b)")[:, 0:Q * NCH].rearrange("p (q c) -> p q c", q=Q)
            step(dve.tensor_copy(wend, W[:, :, CH - 1:T:CH]))
            for q in range(Q):
                wait_full(dve, "bo", q)
                out(dve.tensor_tensor(bv[:, q, :], bank("bo", q)[:, 0:NT], z[:, 8 + q, :], ALU.mult), "bo", q)
            for q in range(Q):
                wait_out(dve, "bo", q)
            step(dve.memset(ST[:, 0, :, :], 0.0), "vectors_done")

            four = lambda m: m.unsqueeze(1).to_broadcast([P, 4, 128])
            grp = lambda b: b[:, :].rearrange("p (u n) -> p u n", u=4)

            def l_masks(t):
                for g in range(2):
                    u = slice(4 * g, 4 * g + 4)
                    wait_full(dve, "L", t, g)
                    out(dve.tensor_tensor(X[:, u, :], grp(bank("L", t, g)), four(mL[0]), ALU.mult), "L", t, g)
                for g in range(2):
                    u = slice(4 * g, 4 * g + 4)
                    wait_out(dve, "L", t, g)
                    tt(X[:, u, :], X[:, u, :], four(ident), ALU.add, name="x_init")

            def pair_masks(t):
                for k, dst, m, n0 in (("Ak", Ak, m_su, 0), ("Rb", Rb, m_iu, 8 * t), ("Rk", Rk, m_iu, 8 * t)):
                    for g in range(2):
                        wait_full(dve, k, t, g)
                        out(dve.tensor_tensor(dst[:, n0 + 4 * g:n0 + 4 * g + 4, :], grp(bank(k, t, g)), four(m),
                                              ALU.mult), k, t, g)

            def level(t, l):
                for g in range(2):
                    u = slice(4 * g, 4 * g + 4)
                    wait_full(dve, "Y", t, g, l)
                    out(dve.tensor_tensor(Y[:, u, :], grp(bank("Y", t, g, l)), four(mL[l]), ALU.mult),
                        "Y", t, g, l)
                for k, dst in (("X", X), ("XT", XT)):
                    if k == "X" and l == LEVELS - 1:
                        continue
                    for g in range(2):
                        u = slice(4 * g, 4 * g + 4)
                        wait_full(dve, k, t, g, l)
                        if l > 1:
                            wait_out(dve, k, t, g, l - 1)
                        elif k == "XT":
                            dve.wait_ge(sem("xt_init"), 2 * t + g + 1)
                        out(dve.tensor_tensor(dst[:, u, :], grp(bank(k, t, g, l)), dst[:, u, :], ALU.add),
                            k, t, g, l)

            def sa_sum(c):
                t, r = c // CPT, slice(CH * (c % CPT), CH * (c % CPT) + CH)
                for g in range(2):
                    gc = slice(256 * g, 256 * g + 256)
                    wait_full(dve, "SA", c, g)
                    wait_out(dve, "Z", t, g)
                    out(dve.tensor_tensor(SA[r, t, gc], bank("SA", c, g)[r, 0:256], Z[r, t, gc], ALU.add),
                        "SA", c, g)

            def state_sum(c):
                wait_full(dve, "SU", c)
                b = bank("SU", c)[:, 0:Q * HN].rearrange("p (q n) -> p q n", q=Q)
                out(dve.tensor_tensor(ST[:, c + 1, :, :], b, ST[:, c, :, :], ALU.add), "SU", c)
                wait_out(dve, "SU", c)
                tt(ST[:, c + 1, :, :], ST[:, c + 1, :, :], wend[:, :, c].unsqueeze(2).to_broadcast([P, Q, HN]),
                   ALU.mult, name="state_done")

            def y_sum(t):
                wait_full(dve, "Y2", t)
                wait_out(dve, "Y1", t)
                yt = yT[:, :, P * t:P * t + P]
                out(dve.tensor_tensor(yt, bank("Y2", t)[:, :].rearrange("p (q n) -> p q n", q=Q), yt, ALU.add),
                    "Y2", t)

            def centre(k):
                n = gn_cols[k].stop - gn_cols[k].start
                wait_full(dve, "mu", k)
                v = yT[:, :, gn_cols[k]]
                out(dve.scalar_tensor_tensor(out=v, in0=bank("mu", k)[:, 0:Q * n].rearrange("p (q n) -> p q n", q=Q),
                                             scalar=-1.0 / HN, in1=v, op0=ALU.mult, op1=ALU.add), "mu", k)
                wait_out(dve, "mu", k)
                tt(gn_sq[k], v, v, ALU.mult, name=f"squares{k}")

            def gated(k):
                wait_out(dve, "va", k)
                v = yT[:, :, gn_cols[k]]
                step(dve.reciprocal(gn_rs[k], gn_rs[k]))
                tt(v, v, gn_rs[k], ALU.mult)
                dve.wait_ge(sem("gates_ready"), Q)
                tt(v, v, gg[:, :, gn_cols[k]], ALU.mult)
                tt(mixT[:, 0:Q, gn_cols[k]], v, bv[:, :, gn_cols[k]], ALU.add, name="mixA_done")

            def mixing(k, cs, dst, base):
                for c in cs:
                    wait_full(dve, k, c)
                    if k == "mB":
                        wait_out(dve, "x2", c)
                    b = bank(k, c)
                    out(dve.scalar_tensor_tensor(out=dst[:, c, 0:T], in0=b[:, 0:T], scalar=mod(2, c, slice(0, 1)),
                                                 in1=base[:, c, 0:T], op0=ALU.mult, op1=ALU.add), k, c)
                    tmp = x1tmp[c % 2]
                    out(dve.tensor_tensor(tmp, b[:, T:NT], mod(2, c, slice(1, NROW)), ALU.mult), k, c)
                    wait_out(dve, k, c)
                    tt(dst[:, c, T:NT], base[:, c, T:NT], tmp, ALU.add, name=k + "_added")

            def key_sums(row, half, name):
                Tv = Stmp.rearrange("p (i j) -> p i j", j=HN)
                hs = slice(16 * half, 16 * half + 16)
                mark(dve.tensor_reduce(sv[:, row, hs], Tv[:, hs, :], AX, ALU.add), name)

            l_masks(0)
            pair_masks(0)
            for l in range(1, LEVELS):
                level(0, l)
                if l in (3, 4):
                    dve.wait_ge(sem("sample_steps"), 1)
                    key_sums(0, l - 3, "sample_red")
            sa_sum(0)
            state_sum(0)
            sa_sum(1)
            l_masks(1)
            state_sum(1)
            pair_masks(1)
            for l in range(1, LEVELS):
                level(1, l)
                if l in (3, 4):
                    dve.wait_ge(sem("sample_steps"), 2)
                    key_sums(1, l - 3, "sample_y")
            sa_sum(2)
            state_sum(2)
            y_sum(0)
            sa_sum(3)
            wait_full(dve, "syT")
            b = bank("syT")[0:32, 0:128].rearrange("p (b q k) -> p k q b", q=Q, k=4)
            for k in range(4):
                out(dve.tensor_copy(yT[32 * k:32 * k + 32, :, T:NT], b[:, k, :, :]), "syT")
            state_sum(3)
            wait_out(dve, "syT")
            wait_out(dve, "Y2", 0)
            centre(0)
            centre(2)
            mixing("mB", [0], x2, x2)
            y_sum(1)
            wait_out(dve, "Y2", 1)
            mixing("mB", [1], x2, x2)
            centre(1)
            gated(0)
            mixing("mB", [2, 3], x2, x2)
            gated(2)
            gated(1)
            mixing("mB", range(4, DC), x2, x2)
            gains(A2, 4, "norm2_g", slice(0, DC))
            for c in range(DC):
                mixing("mA", [c], x1T, x2)
                mark(dve.tensor_tensor(sq2[:, c, :], x1T[:, c, :], x1T[:, c, :], ALU.mult), "sq2_done")
                mark(dve.tensor_scalar(h2T[:, c, 0:T], x1T[:, c, 0:T], A2[:, c, 0:1], None, ALU.mult), "x1_gained")
            step(dve.memset(lbase[0:1, 0:1], 0.0), "x1_done")
            tt(h2T[:, :, T:NT], x1T[:, :, T:NT], A2[:, :, 1:NROW], ALU.mult, name="x1_gained")
            wait_out(dve, "ss2")
            step(dve.reciprocal(rs2[:, :], rs2[:, :]))
            for c in range(DC):
                mark(dve.tensor_tensor(h2T[:, c, :], h2T[:, c, :], rs2[:, :], ALU.mult), "h2_scaled")
            settle(dve, "h2_scaled")
            tt(h2T[:, :, T:NT], h2T[:, :, T:NT], modT[:, 3 * DC:4 * DC, 1:NROW], ALU.add, name="h2_samples")

            dve.wait_ge(sem("iota_ready"), 1)
            dve.wait_ge(sem("router_zero"), 1)
            wait_full(dve, "lg2")
            b = bank("lg2")[:, 0:96].rearrange("p (t e) -> p t e", t=3)
            out(dve.tensor_copy(lgt[:, 0:2, :], b[:, 0:2, :]), "lg2")
            out(dve.tensor_copy(lgt[0:NB, 2, :], b[0:NB, 2, :]), "lg2")
            wait_out(dve, "lg2")
            for t in range(3):
                mark(dve.max(top[:, t, :], lgt[:, t, :]), "top_done")
            settle(dve, "top_done")
            over = lambda v: v.to_broadcast([P, 3, E])
            mark(dve.tensor_tensor(ex[:, :, :], lgt[:, :, :], over(top[:, :, 0:1]), ALU.subtract), "gates_in")
            mark(dve.tensor_tensor(eq[:, :, :], lgt[:, :, :], over(top[:, :, 3:4]), ALU.is_equal), "lanes_done")
            tt(msk[:, :, :], lgt[:, :, :], over(top[:, :, 3:4]), ALU.is_gt)
            mark(dve.tensor_reduce(sc[:, :, 0:1], msk[:, :, :], AX, ALU.add), "lanes_done")
            flat = lambda v: v.rearrange("p t e -> p (t e)")
            step(dve.tensor_tensor_scan(flat(ce), flat(seg), flat(eq), 0.0, ALU.mult, ALU.add))
            tt(ce[:, :, :], ce[:, :, :], over(sc[:, :, 0:1]), ALU.add)
            stt(ce[:, :, :], ce[:, :, :], 4.0, eq[:, :, :], ALU.is_le, ALU.mult)
            tt(msk[:, :, :], msk[:, :, :], ce[:, :, :], ALU.add, name="mask_done")
            dve.wait_ge(sem("gates_exp"), 1)
            tt(ex[:, :, :], ex[:, :, :], msk[:, :, :], ALU.mult)
            step(dve.tensor_reduce(sc[:, :, 1:2], ex[:, :, :], AX, ALU.add))
            step(dve.reciprocal(sc[:, :, 1:2], sc[:, :, 1:2]))
            tt(gatew[:, :, :], ex[:, :, :], over(sc[:, :, 1:2]), ALU.mult, name="gatew_done")
            wait_full(dve, "rank")
            b = bank("rank")[:, 0:96].rearrange("p (t e) -> p t e", t=3)
            out(dve.scalar_tensor_tensor(out=lgt[:, 0:2, :], in0=b[:, 0:2, :], scalar=1.0, in1=msk[:, 0:2, :],
                                         op0=ALU.add, op1=ALU.mult), "rank")
            out(dve.scalar_tensor_tensor(out=lgt[0:NB, 2, :], in0=b[0:NB, 2, :], scalar=1.0,
                                         in1=msk[0:NB, 2, :], op0=ALU.add, op1=ALU.mult), "rank")
            wait_out(dve, "rank")

            def places(k):
                mark(dve.tensor_scalar(rankb[:, :, E * k:E * k + E], lgt[:, :, :], -1.0 - SLOTS * k, None, ALU.add),
                     "places_done")

            def counts():
                step(dve.tensor_copy(gatew[64:72, 2, :], gatew[0:8, 2, :]), "gatew_done")
                for k in range(1, OVER + 1):
                    places(k)
                for k in range(OVER + 1):
                    ts(cnt_i[0:1, E * k:E * k + E], lbase[0:1, :], float(-SLOTS * k), 0.0, ALU.add, ALU.max)
                step(dve.tensor_reduce(cnt_i[0:1, (OVER + 1) * E:(OVER + 1) * E + 1], cnt_i[0:1, E:2 * E], AX,
                                       ALU.max), "router_done")

            places(0)
            wait_full(dve, "cnt")
            out(dve.tensor_copy(lbase[0:1, :], bank("cnt")[0:1, 0:E]), "cnt")
            wait_out(dve, "cnt")
            settle(dve, "places_done")

            def select(n, k, e, buf, turned):
                if turned is not None:
                    dve.wait_ge(sem("pt_turned"), turned)
                    dve.wait_ge(sem("up_done"), turned)
                for t in range(3):
                    m = P if t < 2 else NB
                    dve.tensor_scalar(Psel[buf][0:m, t, :], iota[0:m, :], rankb[0:m, t, bass.ds(k, 1)], None,
                                      ALU.is_equal).then_inc(sem("selected"), 1)
                dve.tensor_scalar(selb[buf][0:E, :], ones[0:E, 0:64], ident[0:E, bass.ds(e, 1)], None,
                                  ALU.mult).then_inc(sem("selected"), 1)

            def glu_g(n):
                dve.wait_ge(sem("gate_done"), n + 1)
                if not isinstance(n, int) or n > 0:
                    dve.wait_ge(sem("act_done2"), n)
                dve.tensor_scalar(g_sb[:, :], ps[0][:, :], 7.0, None, ALU.min).then_inc(sem("g_read"), 1)

            def glu_u(n):
                dve.wait_ge(sem("up_done"), n + 1)
                dve.tensor_scalar(u_sb[:, :], ps[1][:, :], 7.0, -7.0, ALU.min, ALU.max).then_inc(sem("u_read"), 1)
                dve.wait_ge(sem("sig_done"), n + 1)
                dve.tensor_tensor(g_sb[:, :], g_sb[:, :], sg_sb[:, :], ALU.mult).then_inc(sem("glu_done"), 1)
                dve.wait_ge(sem("glu_done"), n + 1)
                dve.wait_ge(sem("u_read"), n + 1)
                if not isinstance(n, int) or n > 0:
                    dve.wait_ge(sem("act_turned"), n)
                dve.scalar_tensor_tensor(out=a_sb[:, :], in0=u_sb[:, :], scalar=1.0, in1=g_sb[:, :],
                                         op0=ALU.add, op1=ALU.mult).then_inc(sem("act_done2"), 1)

            def add_out(n, e):
                if not isinstance(n, int) or n > 0:
                    dve.wait_ge(sem("y_added"), 6 * n)
                for k in range(4):
                    t, h = k // 2, k % 2
                    dve.wait_ge(sem("scattered"), 5 * n + k + 1)
                    v = y[:, t, 512 * h:512 * h + 512]
                    dve.scalar_tensor_tensor(out=v, in0=ps[6 + k % 2][:, :], scalar=gatew[:, t, bass.ds(e, 1)],
                                             in1=v, op0=ALU.mult, op1=ALU.add).then_inc(sem("y_added"), 1)
                dve.wait_ge(sem("scattered"), 5 * n + 5)
                for p0 in (0, 64):
                    v = y_s[p0:p0 + NB, :]
                    dve.scalar_tensor_tensor(out=v, in0=ps[6][p0:p0 + NB, :],
                                             scalar=gatew[p0:p0 + NB, 2, bass.ds(e, 1)], in1=v,
                                             op0=ALU.mult, op1=ALU.add).then_inc(sem("y_added"), 1)

            def y_start():
                dve.wait_ge(sem("gt_turned"), 1)
                step(dve.tensor_copy(gtT[0:E, :], ps[7][0:E, 0:NT]), "gt_copied")
                dve.wait_ge(sem("x1_out"), 16)
                for k in range(5):
                    dve.wait_ge(sem("y_bias"), k + 1)
                    if k < 4:
                        step(dve.tensor_copy(y[:, k // 2, 512 * (k % 2):512 * (k % 2) + 512], ps[6 + k % 2][:, :]),
                             "y_started")
                    else:
                        step(dve.tensor_copy(y_s[0:NB, :], ps[6][0:NB, :]))
                        step(dve.tensor_copy(y_s[64:64 + NB, :], ps[6][64:64 + NB, :]), "y_started")

            select(0, 0, 0, 0, None)
            counts()
            for n in range(4):
                glu_g(n)
                select(n + 1, n + 1, n + 1, (n + 1) % 2, n if n > 0 else None)
                glu_u(n)
                if n > 0:
                    add_out(n - 1, n - 1)
                else:
                    y_start()
            with dve.Fori(1, E // 4 - 1) as i:
                for r in range(4):
                    n = 4 * i + r
                    glu_g(n)
                    select(n + 1, n + 1, n + 1, (r + 1) % 2, n)
                    glu_u(n)
                    add_out(n - 1, n - 1)
            for r in range(4):
                n = E - 4 + r
                glu_g(n)
                if r < 3:
                    select(n + 1, n + 1, n + 1, (r + 1) % 2, n)
                glu_u(n)
                add_out(n - 1, n - 1)
            add_out(E - 1, E - 1)
            nreg = dve.alloc_register("dve_block")
            c = dve.alloc_register("dve_over")
            dve.reg_mov(nreg, E)
            dve.reg_load(c, cnt_i[0:1, (OVER + 1) * E:(OVER + 1) * E + 1])
            with dve.If(dve.snap(c) > 0):
                with dve.Fori(1, OVER + 1) as b:
                    with dve.Fori(0, E) as e:
                        dve.reg_load(c, cnt_i[0:1, bass.ds(b * E + e, 1)])
                        with dve.If(dve.snap(c) > 0):
                            n = dve.snap(nreg)
                            select(n, b * E + e, e, 0, n)
                            glu_g(n)
                            glu_u(n)
                            add_out(n, e)
                            dve.reg_add(nreg, nreg, 1)
                        dve.nop()
                dve.nop()
            dve.nop()
            dve.wait_ge(sem("x1_copied"), 6)
            dve.wait_ge(sem("g2_copied"), 3)
            dve.wait_ge(sem("y_added"), dve.snap(nreg) * 6)
            for t in range(2):
                tt(gt[:, t, :], g2b[:, :], y[:, t, :], ALU.mult)
                tt(gt[:, t, :], gt[:, t, :], x1t[:, t, :], ALU.add, name="x3_ready")
            for h in range(2):
                p0, cs = 64 * h, slice(512 * h, 512 * h + 512)
                tt(g_sb[p0:p0 + NB, :], g2s[p0:p0 + NB, :], y_s[p0:p0 + NB, :], ALU.mult)
            step(dve.tensor_copy(u_sb[0:NB, :], g_sb[64:64 + NB, :]))
            for h in range(2):
                cs = slice(512 * h, 512 * h + 512)
                mark(dve.tensor_tensor(gt[0:NB, 2, cs], (u_sb if h else g_sb)[0:NB, :], x1t[0:NB, 2, cs], ALU.add),
                     "x3_samples")
            settle(dve, "x3_samples")
            step(dve.memset(small[:, 41:42], 0.0), "x3_ready")
            dve.wait_ge(sem("ld_end"), 32)
            for t in range(3):
                n = P if t < 2 else NB
                dve.wait_ge(sem("root3"), t + 1)
                step(dve.reciprocal(rstd[0:n, t:t + 1], rstd[0:n, t:t + 1]))
                stt(gt[0:n, t, :], gt[0:n, t, :], rstd[0:n, t:t + 1], fing[0:n, :], ALU.mult, ALU.mult,
                    name="out_ready")

        @block.tensor
        def _(pe):
            order = [n for n, _ in jobs]
            pos = [0]

            def start(*name):
                assert order[pos[0]] == name, (order[pos[0]], name)
                pos[0] += 1
                b, _, before, _ = where[name]
                if before:
                    pe.wait_ge(bank_out[b], before)
                return ps[b]

            def done(ins, *name):
                ins.then_inc(bank_full[where[name][0]], 1)

            def turn(dst, src):
                return pe.transpose(dst, src, ident[0:src.shape[0], 0:src.shape[0]])

            def rows_turned(name):
                o = start("t", name)
                done(turn(o[:, 0:nrows[name]], rows[name][0:nrows[name], :]), "t", name)

            pe.wait_ge(sem("ident_ready"), 1)
            pe.wait_ge(sem("ld_c"), 32)
            rows_turned("c")
            pe.wait_ge(sem("diag_ready"), 3)
            for c in range(DC):
                o = start("xT", c)
                for t in range(3):
                    n = P if t < 2 else NB
                    mm = pe.matmul(o[:, P * t:P * t + n], xtok[0:n, t, P * c:P * c + P], diag[0:n, t, 0:n],
                                   start=True, stop=True)
                done(mm, "xT", c)

            adas = [n[1] for n, _ in jobs if n[0] == "ada"]

            def ada_part(j):
                n = unit_of[("ada", j)]
                w = fslot[n % FR]
                o = start("ada", j)
                pe.wait_ge(*ring(n))
                wait_out(pe, "t", "c")
                for c in range(2):
                    for g in range(4):
                        mm = pe.matmul(o[32 * g:32 * g + 32, :], cT[:, 2 * g + c, :], w[:, 2 * g + c, :],
                                       start=(c == 0), stop=(c == 1))
                done(mm, "ada", j)

            def ada_turned(j):
                o = start("adaT", j)
                wait_out(pe, "ada", j)
                pe.wait_ge(sem("fold_ready"), 1)
                for g in range(4):
                    mm = pe.matmul(o[:, 16 * g:16 * g + 16], adar[adas.index(j) % 2][:, P * g:P * g + P], fold,
                                   start=True, stop=True)
                done(mm, "adaT", j)

            def ada(*js):
                for j in js:
                    ada_part(j)
                    ada_turned(j)

            def proj(*ms):
                for m in ms:
                    o = start("proj", m)
                    n = unit_of[("win", m)]
                    pe.wait_ge(*ring(n))
                    w = fslot[n % FR]
                    c0 = P * m - UNITS[n][1]
                    for c in range(DC):
                        if m == 18:
                            pe.wait_ge(sem("h_done"), c + 1)
                        mm = pe.matmul(o[:, 0:NT], w[:, c, c0:c0 + P], hT[:, c, :], start=(c == 0),
                                       stop=(c == DC - 1))
                    done(mm, "proj", m)

            ada_part(0)
            ada_part(2)
            pe.wait_ge(sem("ld_prm"), 16 * len(PARAMS))
            rows_turned("prm")
            pe.wait_ge(sem("ld_bada"), 16)
            rows_turned("bada")
            ada_turned(0)
            ada_turned(2)
            ada(1, 3)
            proj(18, 19, 20, 21)
            pe.wait_ge(sem("ld_rows"), 16 * 3)
            for name in ("shift", "conv", "lru"):
                rows_turned(name)
            proj(14, 15, 16, 17)
            ada_part(4)
            pe.wait_ge(sem("ld_wbd"), 64)
            for c in range(Q):
                pe.wait_ge(sem("conv_done"), c + 1)
                for k, name in enumerate(("gr", "gi")):
                    o = start(name, c)
                    done(pe.matmul(o[:, 0:NT], wbd[k][:, c, :], xc[:, c, :], start=True, stop=True), name, c)
            ada_turned(4)
            proj(12, 13)
            ada_part(5)
            proj(4)
            ada_turned(5)
            proj(5)
            pe.wait_ge(sem("ld_lora"), 48)
            pe.wait_ge(sem("z_done"), 2)
            pe.wait_ge(sem("lora_in"), 2)
            for name, w, m, p0, p1 in (("lw", 0, 12, 0, 64), ("la", 0, 12, 64, 128), ("lg", 1, 13, 0, 128)):
                for q in range(Q):
                    o = start(name, q)
                    done(pe.matmul(o[:, 0:NT], lora[p0:p1, w, P * q:P * q + P], z[p0:p1, m, :],
                                   start=True, stop=True), name, q)
            proj(6, 7)
            ada_part(6)
            ada_part(7)
            ada_turned(6)
            ada_turned(7)
            proj(0, 1, 2, 3)
            pe.wait_ge(sem("kk2_done"), 1)
            for q in range(Q):
                o = start("kn", q)
                done(pe.matmul(o[:, 0:NT], bones, yT[:, q, :], start=True, stop=True), "kn", q)
            ada_part(8)
            proj(8)
            ada_turned(8)
            proj(9, 10, 11)
            ada_part(9)
            pe.wait_ge(sem("consts"), 3)
            pe.wait_ge(sem("consts2"), 5)
            o = start("ssB")
            pe.wait_ge(sem("sqB_done"), 1)
            for c in range(Q):
                mm = pe.matmul(o[:, 0:NT], ones, gi[:, c, :], start=(c == 0), stop=(c == Q - 1))
            done(mm, "ssB")
            ada_part(10)
            ada_turned(9)
            ada_part(11)
            ada_turned(10)
            ada_turned(11)
            pe.wait_ge(sem("smp_done"), 6)
            for k in range(2):
                o = start("smpT", k)
                for j in range(3):
                    mm = turn(o[0:32, P * j:P * j + P], smp[:, 3 * k + j, :, :].rearrange("p q b -> p (q b)"))
                done(mm, "smpT", k)
            o = start("smpB")
            pe.wait_ge(sem("consts2"), 5)
            wait_out(pe, "smpT", 0)
            wait_out(pe, "smpT", 1)
            for k in range(4):
                h = k // 2
                pe.matmul(o[:, 0:320].rearrange("p (v n) -> p v n", v=5), sel4[0:32, k, :],
                          sv[0:32, 0:5, 64 * h:64 * h + 64], start=(k == 0), stop=(k == 3))
            for k in range(4):
                mm = pe.matmul(o[:, 320:352], sel4[0:32, k, :], sv[0:32, 5, 32 * k:32 * k + 32],
                               start=(k == 0), stop=(k == 3))
            done(mm, "smpB")
            pe.wait_ge(sem("rk_done"), Q)
            for q in range(Q):
                o = start("bo", q)
                done(pe.matmul(o[:, 0:NT], bones, cum[:, q, :], start=True, stop=True), "bo", q)

            pe.wait_ge(sem("bm_done"), 4 * Q)
            def head(h):
                return slice(64 * (h % 2), 64 * (h % 2) + 64), h // 2

            def unit(h):
                return 4 * (h % 2) + h // 2

            def tk(t, ks):
                tc = slice(P * t, P * t + P)
                srcs = [lambda q: bm[:, q, tc], lambda q: kap[:, q, tc], lambda q: z[:, 8 + q, tc],
                        lambda q: arp[:, q, t, 0, :]]
                for k in ks:
                    o = start("tk", t, k)
                    for q in range(Q):
                        mm = turn(o[:, P * q:P * q + P], srcs[k](q))
                    done(mm, "tk", t, k)

            def pair_products(t, *ks):
                tc = slice(P * t, P * t + P)
                pairs = {"U": (bm, 0), "L": (None, 0), "Ak": (kap, 0), "Rb": (bm, 1), "Rk": (kap, 1)}
                for k in ks:
                    for g in range(2):
                        o = start(k, t, g)
                        for j in range(4):
                            rows_, q = head(2 * j + g)
                            a, kind = pairs[k]
                            lhs = arp[rows_, q, t, 0, :] if a is None else a[rows_, q, tc]
                            rhs = bm[rows_, q, tc] if a is None else arp[rows_, q, t, kind, :]
                            mm = pe.matmul(o[:, P * j:P * j + P], lhs, rhs, start=True, stop=True)
                        done(mm, k, t, g)

            def systems(t):
                for l in range(1, LEVELS):
                    for g in range(2):
                        o = start("Y", t, g, l)
                        if l == 1:
                            wait_out(pe, "U", t, g)
                            pe.wait_ge(sem("x_init"), 2 * t + g + 1)
                        else:
                            wait_out(pe, "X", t, g, l - 1)
                        for j in range(4):
                            mm = pe.matmul(o[:, P * j:P * j + P], U[:, 4 * g + j, :], X[:, 4 * g + j, :],
                                           start=True, stop=True)
                        done(mm, "Y", t, g, l)
                    if l < LEVELS - 1:
                        for g in range(2):
                            o = start("X", t, g, l)
                            wait_out(pe, "Y", t, g, l)
                            if l == 1:
                                pe.wait_ge(sem("xt_init"), 2 * t + g + 1)
                            else:
                                wait_out(pe, "XT", t, g, l - 1)
                            for j in range(4):
                                mm = pe.matmul(o[:, P * j:P * j + P], XT[:, 4 * g + j, :], Y[:, 4 * g + j, :],
                                               start=True, stop=True)
                            done(mm, "X", t, g, l)
                    for g in range(2):
                        o = start("XT", t, g, l)
                        wait_out(pe, "Y", t, g, l)
                        if l > 1:
                            wait_out(pe, "XT", t, g, l - 1)
                        for j in range(4):
                            mm = pe.matmul(o[:, P * j:P * j + P], Y[:, 4 * g + j, :], XT[:, 4 * g + j, :],
                                           start=True, stop=True)
                        done(mm, "XT", t, g, l)
                for g in range(2):
                    o = start("LV", t, g)
                    wait_out(pe, "Ak", t, g)
                    wait_out(pe, "tk", t, 2)
                    for j in range(4):
                        h = 2 * j + g
                        mm = pe.matmul(o[:, 64 * j:64 * j + 64], Ak[:, 4 * g + j, :], tok[2][:, t, 64 * h:64 * h + 64],
                                       start=True, stop=True)
                    done(mm, "LV", t, g)
                for g in range(2):
                    o = start("Z", t, g)
                    wait_out(pe, "LV", t, g)
                    wait_out(pe, "XT", t, g, LEVELS - 1)
                    for j in range(4):
                        u = 4 * g + j
                        mm = pe.matmul(o[:, 64 * j:64 * j + 64], XT[:, u, :], LV[:, u, :], start=True, stop=True)
                    done(mm, "Z", t, g)
                for g in range(2):
                    o = start("AH", t, g)
                    wait_out(pe, "tk", t, 3)
                    for j in range(4):
                        h = 2 * j + g
                        rows_, q = head(h)
                        mm = pe.matmul(o[rows_, P * q:P * q + P], tok[3][:, t, 64 * h:64 * h + 64],
                                       XT[:, 4 * g + j, :], start=True, stop=True)
                    done(mm, "AH", t, g)

            def sa(c):
                t = c // CPT
                r = slice(CH * (c % CPT), CH * (c % CPT) + CH)
                cc = slice(CH * c, CH * c + CH)
                for g in range(2):
                    o = start("SA", c, g)
                    wait_out(pe, "AH", t, g)
                    if c == 0:
                        pe.wait_ge(sem("vectors_done"), 1)
                    else:
                        pe.wait_ge(sem("state_done"), c)
                    for j in range(4):
                        rows_, q = head(2 * j + g)
                        mm = pe.matmul(o[r, 64 * j:64 * j + 64], ahT[rows_, q, cc], ST[rows_, c, q, :],
                                       start=True, stop=True)
                    done(mm, "SA", c, g)

            def state_update(c):
                t = c // CPT
                r = slice(CH * (c % CPT), CH * (c % CPT) + CH)
                o = start("SU", c)
                wait_out(pe, "tk", t, 0)
                wait_out(pe, "tk", t, 1)
                wait_out(pe, "SA", c, 0)
                wait_out(pe, "SA", c, 1)
                for h in range(H):
                    rows_, q = head(h)
                    hc = slice(64 * h, 64 * h + 64)
                    uc = slice(64 * unit(h), 64 * unit(h) + 64)
                    pe.matmul(o[rows_, 64 * q:64 * q + 64], tok[1][r, t, hc], tok[2][r, t, hc],
                              start=True, stop=False)
                    mm = pe.matmul(o[rows_, 64 * q:64 * q + 64], tok[0][r, t, hc], SA[r, t, uc],
                                   start=False, stop=True)
                done(mm, "SU", c)

            def y_state(t):
                o = start("Y1", t)
                for h in range(H):
                    rows_, q = head(h)
                    for c in range(CPT):
                        r0 = CH * c
                        mm = pe.matmul(o[rows_, P * q + r0:P * q + r0 + CH], ST[rows_, CPT * t + c, q, :],
                                       arp[rows_, q, t, 1, r0:r0 + CH], start=True, stop=True)
                done(mm, "Y1", t)

            def y_chunk(t):
                o = start("Y2", t)
                for k in ("Rb", "Rk"):
                    for g in range(2):
                        wait_out(pe, k, t, g)
                wait_out(pe, "SA", 2 * t + 1, 0)
                wait_out(pe, "SA", 2 * t + 1, 1)
                for h in range(H):
                    rows_, q = head(h)
                    u = unit(h)
                    v = o[rows_, P * q:P * q + P]
                    pe.matmul(v, SA[:, t, 64 * u:64 * u + 64], Rb[:, 8 * t + u, :], start=True, stop=False)
                    mm = pe.matmul(v, tok[2][:, t, 64 * h:64 * h + 64], Rk[:, 8 * t + u, :],
                                   start=False, stop=True)
                done(mm, "Y2", t)

            def head_sums(name, k, src):
                o = start(name, k)
                n = src.shape[2]
                done(pe.matmul(o[:, 0:Q * n].rearrange("p (q n) -> p q n", q=Q), bones, src, start=True, stop=True),
                     name, k)

            def mean(k):
                if k == 2:
                    wait_out(pe, "syT")
                else:
                    wait_out(pe, "Y2", k)
                head_sums("mu", k, yT[:, :, gn_cols[k]])

            def variance(k):
                pe.wait_ge(sem(f"squares{k}"), 1)
                head_sums("va", k, gn_sq[k])

            def x_turned(cs):
                for c in cs:
                    o = start("x2", c)
                    for t in range(3):
                        n = P if t < 2 else NB
                        mm = turn(o[:, P * t:P * t + n], xtok[0:n, t, P * c:P * c + P])
                    done(mm, "x2", c)

            def mixing(name, cs):
                k0 = Q if name == "mB" else 0
                for c in cs:
                    o = start(name, c)
                    for k in range(k0, k0 + Q):
                        mm = pe.matmul(o[:, 0:NT], wout[:, k, P * c:P * c + P], mixT[:, k, :],
                                       start=(k == k0), stop=(k == k0 + Q - 1))
                    done(mm, name, c)

            tk(0, range(4))
            pair_products(0, "U", "L", "Ak", "Rb", "Rk")
            systems(0)
            pe.wait_ge(sem("conv_state"), Q)
            pe.wait_ge(sem("lru_state"), 1)
            for n in range(3):
                o = start("so", n)
                src = so[0].rearrange("p b m -> p (b m)") if n == 0 else so[n]
                done(turn(o[0:nso[n], 0:128], src), "so", n)
            sa(0)
            tk(1, (0, 1))
            state_update(0)
            tk(1, (2, 3))
            pair_products(1, "U")
            sa(1)
            pair_products(1, "L")
            state_update(1)
            pair_products(1, "Ak", "Rb", "Rk")
            systems(1)
            sa(2)
            y_state(0)
            state_update(2)
            y_chunk(0)
            sa(3)
            o = start("syT")
            pe.wait_ge(sem("sample_y"), 2)
            done(turn(o[0:32, 0:128], sv[:, 1, 0:32]), "syT")
            mean(0)
            x_turned(range(0, 4))
            state_update(3)
            mean(2)
            x_turned((4, 5))
            pe.wait_ge(sem("ld_wout"), 16)
            pe.wait_ge(sem("mixB_done"), Q)
            mixing("mB", [0])
            variance(0)
            variance(2)
            o = start("wkv")
            pe.wait_ge(sem("state_done"), NCH)
            for q in range(Q):
                mm = turn(o[0:HN, P * q:P * q + P], ST[:, NCH, q, :])
            done(mm, "wkv")
            y_state(1)
            y_chunk(1)
            x_turned((6, 7))
            mixing("mB", [1])
            mean(1)
            mixing("mB", [2, 3])
            variance(1)
            mixing("mB", range(4, DC))
            pe.wait_ge(sem("mixA_done"), 3)
            mixing("mA", [0])
            o = start("ss2")
            for c in range(DC):
                if c + 1 < DC:
                    mixing("mA", [c + 1])
                pe.wait_ge(sem("sq2_done"), c + 1)
                mm = pe.matmul(o[:, 0:NT], ones, sq2[:, c, :], start=(c == 0), stop=(c == DC - 1))
            done(mm, "ss2")
            pe.wait_ge(sem("ld_router"), 32)
            o = start("lg2")
            for t in range(3):
                n = P if t < 2 else NB
                mm = pe.matmul(o[0:n, E * t:E * t + E], ones[0:1, 0:n], rb[0:1, :], start=True, stop=False)
                for c in range(DC):
                    pe.wait_ge(sem("h2_done" if t < 2 else "h2_samples"), c + 1 if t < 2 else 1)
                    mm = pe.matmul(o[0:n, E * t:E * t + E], h2T[:, c, P * t:P * t + n], rw[:, c, :], start=False,
                                   stop=(c == DC - 1))
            done(mm, "lg2")
            for t in range(3):
                n = P if t < 2 else NB
                for c in range(2):
                    o = start("h2", t, c)
                    for j in range(4):
                        mm = turn(o[0:n, P * j:P * j + P], h2T[:, 4 * c + j, P * t:P * t + n])
                    done(mm, "h2", t, c)
            o = start("rank")
            pe.wait_ge(sem("mask_done"), 1)
            pe.wait_ge(sem("iota_ready"), 1)
            pe.matmul(o[:, 0:E], tri[:, :], msk[:, 0, :], start=True, stop=True)
            pe.matmul(o[:, E:2 * E], ones, msk[:, 0, :], start=True, stop=False)
            pe.matmul(o[:, E:2 * E], tri[:, :], msk[:, 1, :], start=False, stop=True)
            pe.matmul(o[0:NB, 2 * E:3 * E], ones[:, 0:NB], msk[:, 0, :], start=True, stop=False)
            pe.matmul(o[0:NB, 2 * E:3 * E], ones[:, 0:NB], msk[:, 1, :], start=False, stop=False)
            mm = pe.matmul(o[0:NB, 2 * E:3 * E], tri[0:NB, 0:NB], msk[0:NB, 2, :], start=False, stop=True)
            done(mm, "rank")
            o = start("cnt")
            pe.matmul(o[0:1, 0:E], ones[:, 0:1], msk[:, 0, :], start=True, stop=False)
            pe.matmul(o[0:1, 0:E], ones[:, 0:1], msk[:, 1, :], start=False, stop=False)
            done(pe.matmul(o[0:1, 0:E], ones[0:NB, 0:1], msk[0:NB, 2, :], start=False, stop=True), "cnt")
            for c in range(2):
                o = start("g2", c)
                for j in range(4):
                    mm = turn(o[0:NROW, P * j:P * j + P], modT[:, 40 + 4 * c + j, :])
                done(mm, "g2", c)
            assert pos[0] == len(order)

            for b in range(8):
                pe.wait_ge(bank_out[b], taken[b])

            def y_bias():
                pe.wait_ge(sem("gt_copied"), 1)
                pe.wait_ge(sem("ld_bdown"), 16)
                for k in range(4):
                    t, h = k // 2, k % 2
                    if k >= 2:
                        pe.wait_ge(sem("y_started"), k - 1)
                    pe.matmul(ps[6 + k % 2][:, :], gtT[0:E, P * t:P * t + P], bd[0:E, 512 * h:512 * h + 512],
                              start=True, stop=True).then_inc(sem("y_bias"), 1)
                pe.wait_ge(sem("y_started"), 3)
                for h in range(2):
                    mm = pe.matmul(ps[6][64 * h:64 * h + NB, :], gtT[0:E, T:NT], bd[0:E, 512 * h:512 * h + 512],
                                   start=True, stop=True)
                mm.then_inc(sem("y_bias"), 1)

            def gates_turned():
                pe.wait_ge(sem("gatew_done"), 1)
                pe.wait_ge(sem("router_done"), 1)
                turn(ps[7][0:E, 0:128], gatew[:, 0, :])
                turn(ps[7][0:E, 128:256], gatew[:, 1, :])
                turn(ps[7][0:E, 256:NT], gatew[0:NB, 2, :]).then_inc(sem("gt_turned"), 1)

            def gather(n, buf):
                pe.wait_ge(sem("selected"), 4 * n + 4)
                if not isinstance(n, int) or n > 0:
                    pe.wait_ge(sem("x_copied"), n)
                for t in range(3):
                    m = P if t < 2 else NB
                    for h in range(2):
                        mm = pe.matmul(ps[2][64 * h:64 * h + 64, :], Psel[buf][0:m, t, 0:64],
                                       h2tok[0:m, t, 512 * h:512 * h + 512], start=(t == 0), stop=(t == 2))
                mm.then_inc(sem("gathered"), 1)

            def turn_rows(n):
                pe.wait_ge(sem("x_copied"), n + 1)
                if not isinstance(n, int) or n > 0:
                    pe.wait_ge(sem("at_copied"), n)
                for j in range(4):
                    mm = turn(ps[3][:, P * j:P * j + P], Xg[:, P * j:P * j + P])
                mm.then_inc(sem("x_turned"), 1)

            def product(bank_, lhsT, w, bias, buf):
                if bias is not None:
                    for h in range(2):
                        pe.matmul(bank_[64 * h:64 * h + 64, :], selb[buf][0:E, :],
                                  bias[0:E, 512 * h:512 * h + 512], start=True, stop=False)
                for k in range(DC):
                    s0 = P * (k % 4) + 64 * (k // 4)
                    for h in range(2):
                        mm = pe.matmul(bank_[64 * h:64 * h + 64, :], lhsT[:, s0:s0 + 64],
                                       w[:, k, 512 * h:512 * h + 512],
                                       start=(bias is None and k == 0), stop=(k == DC - 1))
                return mm

            def gate_up(n, buf, slot, loaded):
                pe.wait_ge(sem("xt_copied"), n + 1)
                if isinstance(n, int) and n == 0:
                    pe.wait_ge(sem("ld_bias"), 32)
                else:
                    pe.wait_ge(sem("g_read"), n)
                loaded(0)
                product(ps[0], XTg, wslot[slot[0]], bg, buf).then_inc(sem("gate_done"), 1)
                if not isinstance(n, int) or n > 0:
                    pe.wait_ge(sem("u_read"), n)
                loaded(1)
                product(ps[1], XTg, wslot[slot[1]], bu, buf).then_inc(sem("up_done"), 1)

            def turn_act(n):
                pe.wait_ge(sem("act_done2"), n + 1)
                pe.wait_ge(sem("xt_copied"), n + 1)
                for j in range(4):
                    mm = turn(ps[3][:, P * j:P * j + P], a_sb[:, P * j:P * j + P])
                mm.then_inc(sem("act_turned"), 1)

            def turn_places(n, buf):
                if not isinstance(n, int) or n > 0:
                    pe.wait_ge(sem("pt_copied"), 2 * n)
                for t in range(3):
                    m = P if t < 2 else NB
                    mm = turn(ps[4][:, P * t:P * t + m], Psel[buf][0:m, t, :])
                mm.then_inc(sem("pt_turned"), 1)

            def down(n, slot, loaded):
                pe.wait_ge(sem("at_copied"), n + 1)
                if not isinstance(n, int) or n > 0:
                    pe.wait_ge(sem("out_copied"), n)
                loaded(2)
                product(ps[5], aT_sb, wslot[slot[2]], None, 0).then_inc(sem("down_done"), 1)

            def scatter(n):
                pe.wait_ge(sem("out_copied"), n + 1)
                pe.wait_ge(sem("pt_copied"), 2 * n + 2)
                for k in range(4):
                    t, h = k // 2, k % 2
                    if k < 2:
                        if isinstance(n, int) and n == 0:
                            pe.wait_ge(sem("y_started"), 5)
                        else:
                            pe.wait_ge(sem("y_added"), 6 * n)
                    else:
                        pe.wait_ge(sem("y_added"), 6 * n + k - 1)
                    pe.matmul(ps[6 + k % 2][:, :], PTz[h][:, P * t:P * t + P], o_sb[:, :], start=True, stop=True)\
                      .then_inc(sem("scattered"), 1)
                pe.wait_ge(sem("y_added"), 6 * n + 3)
                for h in range(2):
                    mm = pe.matmul(ps[6][64 * h:64 * h + NB, :], PTz[h][:, T:NT], o_sb[:, :], start=True, stop=True)
                mm.then_inc(sem("scattered"), 1)

            def slots_of(r):
                return [(3 * r + t) % 4 for t in range(3)]

            def loaded_of(rounds, r):
                def loaded(t):
                    pe.wait_ge(sem(f"w_loaded{(3 * r + t) % 4}"), 48 * rounds + 16 * ((3 * r + t) // 4 + 1))
                return loaded

            def block_step(n, rounds, r, first=False, last=False):
                gate_up(n, r % 2, slots_of(r), loaded_of(rounds, r))
                if first:
                    gates_turned()
                else:
                    scatter(n - 1)
                if not last:
                    gather(n + 1, (r + 1) % 2)
                turn_act(n)
                turn_places(n, r % 2)
                if not last:
                    turn_rows(n + 1)
                if first:
                    y_bias()
                down(n, slots_of(r), loaded_of(rounds, r))

            gather(0, 0)
            turn_rows(0)
            for r in range(4):
                block_step(r, 0, r, first=(r == 0))
            with pe.Fori(1, E // 4 - 1) as i:
                for r in range(4):
                    block_step(4 * i + r, i, r)
            for r in range(4):
                block_step(E - 4 + r, E // 4 - 1, r, last=(r == 3))
            pe.wait_ge(sem("ld_end"), 32)
            pe.wait_ge(sem("u_read"), E)
            pe.wait_ge(sem("x_copied"), E)
            pe.wait_ge(sem("at_copied"), E)
            pe.wait_ge(sem("pt_copied"), 2 * E)
            for k in range(6):
                t, c = k // 2, k % 2
                n = P if t < 2 else NB
                if k == 5:
                    pe.wait_ge(sem("x1_copied"), 1)
                for j in range(4):
                    mm = turn(ps[k % 5][0:n, P * j:P * j + P], x1o[:, 4 * c + j, P * t:P * t + n])
                mm.then_inc(sem("x1_turned"), 1)
            for k in range(2):
                pe.wait_ge(sem("x1_copied"), k + 2)
                pe.matmul(ps[1 + k][:, :], sel9[0:NROW, 0:P], gate2[0:NROW, 512 * k:512 * k + 512],
                          start=True, stop=True).then_inc(sem("g2_done"), 1)
            pe.wait_ge(sem("x1_copied"), 4)
            for h in range(2):
                mm = pe.matmul(ps[3][64 * h:64 * h + NB, :], sel9[0:NROW, T:NT],
                               gate2[0:NROW, 512 * h:512 * h + 512], start=True, stop=True)
            mm.then_inc(sem("g2_done"), 1)
            scatter(E - 1)
            nreg = pe.alloc_register("pe_block")
            c = pe.alloc_register("pe_over")
            pe.reg_load(c, cnt_i[0:1, (OVER + 1) * E:(OVER + 1) * E + 1])
            with pe.If(pe.snap(c) > 0):
                pe.wait_ge(sem("x1_copied"), 6)
                pe.wait_ge(sem("g2_copied"), 3)
                pe.reg_mov(nreg, E)
                with pe.Fori(1, OVER + 1) as b:
                    with pe.Fori(0, E) as e:
                        pe.reg_load(c, cnt_i[0:1, bass.ds(b * E + e, 1)])
                        with pe.If(pe.snap(c) > 0):
                            n = pe.snap(nreg)

                            def again(t):
                                pe.wait_ge(sem("w_again"), 48 * (n - E) + 48)

                            gather(n, 0)
                            turn_rows(n)
                            gate_up(n, 0, [1, 2, 3], again)
                            turn_act(n)
                            turn_places(n, 0)
                            down(n, [1, 2, 3], again)
                            scatter(n)
                            pe.reg_add(nreg, nreg, 1)
                        pe.nop()
                pe.nop()
            pe.nop()


INPUTS = ["x_prompt", "x_sample", "c_prompt", "c_sample", "state_wkv", "state_shift", "state_conv", "state_lru",
          "w_ada", "b_ada", "norm1_g", "norm2_g", "w_in", "rk_mu", "rk_w0", "rk_w_up", "rk_a0", "rk_a_up",
          "rk_g_up", "rk_k_k", "rk_k_a", "rk_r_k", "rk_lnx_w", "rk_lnx_b", "lru_conv_w", "lru_conv_b",
          "lru_w_r", "lru_b_r", "lru_w_i", "lru_b_i", "lru_lambda", "lru_norm_g", "w_out", "router_w",
          "router_b", "w_gate", "b_gate", "w_up", "b_up", "w_down", "b_down", "final_g"]
OUTPUTS = [("y_prompt", (1, T, D)), ("y_sample", (NB, 1, D)), ("wkv_prompt", (1, 1, H, HN, HN)),
           ("shift_prompt", (1, 1, MA * P)), ("conv_prompt", (1, 1, 3, DA)), ("lru_prompt", (1, 1, DA)),
           ("wkv_sample", (1, NB, H, HN, HN)), ("shift_sample", (1, NB, MA * P)),
           ("conv_sample", (1, NB, 3, DA)), ("lru_sample", (1, NB, DA))]


def kernel(**inputs):
    import numpy as _np
    import concourse.bacc as _bacc
    from concourse import mybir as _mybir
    from concourse.bass_utils import run_bass_kernel_spmd as _run

    nc = _bacc.Bacc("TRN2", target_bir_lowering=False, num_devices=1)
    arrays, ins, outs = {}, {}, {}
    for name in INPUTS:
        a = _np.ascontiguousarray(inputs[name])
        arrays[f"in_{name}_dram"] = a
        ins[name] = nc.dram_tensor(f"in_{name}_dram", a.shape, _mybir.dt.from_np(a.dtype), kind="ExternalInput").ap()
    for name, shape in OUTPUTS:
        outs[name] = nc.dram_tensor(f"out_{name}_dram", shape, _mybir.dt.float32, kind="ExternalOutput").ap()
    build(nc, ins, outs)
    r = _run(nc, [arrays], core_ids=[0])
    return tuple(r.results[0][f"out_{name}_dram"] for name, _ in OUTPUTS)
```

```python
from contextlib import ExitStack

import numpy as np

import concourse.bass as bass
from concourse import mybir
from concourse.alu_op_type import AluOpType as ALU

F32 = mybir.dt.float32
I32 = mybir.dt.int32
ACT = mybir.ActivationFunctionType
AX = mybir.AxisListType.X

P = 128
D = 1024
DC = D // P
T = 256
NB = 8
NT = T + NB
DA = 512
Q = DA // P
HN = 64
H = DA // HN
MA = 14
NROW = NB + 1
EXP_HALF = float(np.exp(-0.5))
CH = 64
LEVELS = CH.bit_length() - 1
CPT = P // CH
NCH = T // CH
E = 32
SLOTS = 64
OVER = 4
NPAR = 94

PARAMS = [("rk_mu", 14), ("rk_w0", 4), ("rk_a0", 4), ("rk_k_k", 4), ("rk_k_a", 4), ("rk_r_k", 4),
          ("rk_lnx_w", 4), ("rk_lnx_b", 4), ("lru_conv_w", 16), ("lru_conv_b", 4), ("lru_b_r", 4),
          ("lru_b_i", 4), ("lru_lambda", 4), ("lru_norm_g", 4), ("norm1_g", 8), ("norm2_g", 8)]
PAT = {}
for _n, _k in PARAMS:
    PAT[_n] = sum(k for _, k in PARAMS[:len(PAT)])

UNITS = [("ada", 512 * j, 512) for j in (0, 2, 1, 3)]
UNITS += [("win", 2304, 512), ("ada", 2048, 512), ("win", 1792, 512), ("ada", 2560, 512), ("win", 1536, 256),
          ("ada", 3072, 512), ("win", 512, 512), ("ada", 3584, 512), ("win", 0, 512), ("ada", 4096, 512),
          ("win", 1024, 512), ("ada", 4608, 512), ("ada", 5120, 512), ("ada", 5632, 512)]
FR = 3


def job_list():
    def ada(*units):
        return [x for j in units for x in ((("ada", j), 1), (("adaT", j), 1))]

    def proj_a(*ms):
        return [(("proj", m), 2) for m in ms]

    def tk(t, *ks):
        return [(("tk", t, k), 1) for k in ks]

    part = lambda j: [(("ada", j), 1)]
    turned = lambda j: [(("adaT", j), 1)]
    proj_b = lambda *ms: [(("proj", m), 1) for m in ms]
    jobs = [(("t", "c"), 1), (("ada", 0), 1)] + [(("xT", c), 1) for c in range(DC)]
    jobs += [(("ada", 2), 1), (("t", "prm"), 1), (("t", "bada"), 1), (("adaT", 0), 1),
             (("adaT", 2), 1)]
    jobs += ada(1, 3) + proj_a(18, 19, 20, 21)
    jobs += [(("t", n), 1) for n in ("shift", "conv", "lru")]
    jobs += part(4) + proj_b(14) + turned(4) + proj_b(15, 16, 17) + part(5)
    for c in range(Q):
        jobs += [(("gr", c), 1), (("gi", c), 1)]
    jobs += turned(5) + proj_a(12, 13) + part(6) + proj_a(4) + turned(6) + proj_a(5)
    jobs += [((k, q), 1) for k in ("lw", "la", "lg") for q in range(Q)]
    jobs += proj_a(6, 7) + part(7) + proj_a(0) + turned(7)
    jobs += [(("kn", q), 1) for q in range(Q)] + proj_a(1, 2) + [(("ssB",), 1)] + proj_a(3)
    jobs += part(8) + proj_a(8) + turned(8) + proj_a(9, 10, 11)
    jobs += part(9) + part(10) + turned(9) + tk(0, 0, 1) + turned(10) + tk(0, 2, 3) + part(11) + turned(11)

    def systems(t):
        jobs = []
        for l in range(LEVELS - 1):
            if l > 0:
                jobs += [(("X", t, g, l), 1) for g in range(2)]
            for g in range(2):
                jobs += [(("XT", t, g, l), 1), (("Y", t, g, l + 1), 1)]
        jobs += [(("XT", t, g, LEVELS - 1), 1) for g in range(2)]
        return jobs + [((k, t, g), 1) for k in ("LV", "Z", "AH") for g in range(2)]

    def pairs(t, *ks):
        return [((k, t, g), 1) for k in ks for g in range(2)]

    def sa(c):
        return [(("SA", c, 0), 1), (("SA", c, 1), 1)]

    jobs += pairs(0, "U", "L", "Ak", "Rb", "Rk")
    jobs += [(("smpT", 0), 1), (("smpT", 1), 1), (("smpB",), 1)] + [(("bo", q), 1) for q in range(Q)]
    jobs += systems(0)
    jobs += [(("so", n), 1) for n in range(3)]
    jobs += sa(0) + tk(1, 0, 1) + [(("SU", 0), 1)] + tk(1, 2, 3)
    jobs += pairs(1, "U") + sa(1) + pairs(1, "L") + [(("SU", 1), 1)] + pairs(1, "Ak", "Rb", "Rk")
    jobs += systems(1)
    x2 = lambda *cs: [(("x2", c), 1) for c in cs]
    mb = lambda *cs: [(("mB", c), 2) for c in cs]
    jobs += sa(2) + [(("Y1", 0), 1), (("SU", 2), 1), (("Y2", 0), 1)] + sa(3) + [(("Y1", 1), 1), (("mu", 0), 1)]
    jobs += [(("Y2", 1), 1), (("syT",), 4)] + x2(0, 1, 2, 3) + [(("mu", 1), 1)] + x2(4, 5, 6, 7)
    jobs += mb(0) + [(("va", 0), 1), (("mu", 2), 1), (("va", 1), 1)] + mb(1) + [(("va", 2), 1)] + mb(2)
    jobs += mb(3) + [(("SU", 3), 1)] + mb(4, 5, 6, 7) + [(("wkv",), 1)]
    jobs += [(("mA", c), 2) for c in range(DC)] + [(("ss2",), 1)]
    jobs += [(("lgT",), 1), (("lg2",), 2)]
    jobs += [(("h2", t, c), 1) for t in range(2) for c in range(2)]
    jobs += [(("rank",), 2), (("cnt",), 1)] + [(("h2", 2, c), 1) for c in range(2)]
    jobs += [(("g2", c), 1) for c in range(2)]
    return jobs


def build(nc, I, O):
    ctx = ExitStack()
    with ctx:
        mem = ctx.enter_context(nc.sbuf_tensor("mem", [P, 53000], F32))
        cnt_i = ctx.enter_context(nc.sbuf_tensor("cnt_i", [1, (OVER + 1) * E + 32], I32))
        ps = [ctx.enter_context(nc.psum_tensor(f"ps{b}", [P, 512], F32)) for b in range(8)]
        x1_dram = nc.dram_tensor("x1_scratch", (P, DC * NT), F32, kind="Internal").ap()
        gate2_dram = nc.dram_tensor("gate2_scratch", (NROW, D), F32, kind="Internal").ap()

        def view(at, *dims):
            n = int(np.prod(dims))
            flat = mem[:, at:at + n]
            if len(dims) == 1:
                return flat
            names = "abcd"[:len(dims)]
            return flat.rearrange(f"p ({' '.join(names)}) -> p {' '.join(names)}",
                                  **{k: v for k, v in zip(names[1:], dims[1:])})

        class Region:

            def __init__(self, at, end):
                self.at, self.end = at, end

            def take(self, *dims):
                v = view(self.at, *dims)
                self.at += int(np.prod(dims))
                assert self.at <= self.end, (self.at, self.end)
                return v

        keep = Region(49600, 53000)
        ident = keep.take(128)
        ones = keep.take(128)
        iota = keep.take(128)
        prm = keep.take(96)
        modT = keep.take(6 * DC, NROW)
        gatew = keep.take(3, E)
        rankb = keep.take(3, (OVER + 1) * E)
        gate2 = keep.take(D)
        tri = keep.take(128)
        small = keep.take(64)
        eps1, epsx = (small[:, k:k + 1] for k in range(2))
        ssq, rstd = small[:, 8:11], small[:, 12:15]
        squares = view(12288, 3, D)
        wslot = [view(8192 * s, DC, D) for s in range(4)]
        moe = Region(32768, 49600)
        x1T = moe.take(DC, NT)
        h2T = moe.take(DC, NT)
        y = view(32768, 2, D)
        y_s = view(32768 + 2 * D, 512)
        h2tok = moe.take(3, D)
        Xg, XTg, g_sb, sg_sb, u_sb, a_sb, aT_sb, o_sb = (moe.take(512) for _ in range(8))
        bg, bu = moe.take(D), moe.take(D)
        Psel = [moe.take(3, 128) for _ in range(2)]
        PTz = [moe.take(NT) for _ in range(2)]
        selb = [moe.take(64) for _ in range(2)]
        bd = view(32768 + 2 * D + 512, D)
        fslot = [view(4096 * s, DC, 512) for s in range(FR)]
        inv = Region(0, 12288)
        U, X, Y, Ak, XT = (inv.take(8, 128) for _ in range(5))
        Rb, Rk = inv.take(16, 128), inv.take(16, 128)
        Stmp = inv.take(2048)
        sv = inv.take(6, 128)
        wout = view(24576, DC, D)
        dead = Region(24576, 32768)
        z = dead.take(MA, NT)
        sigw, cum, aa, kk = (dead.take(Q, NT) for _ in range(4))
        mid = Region(12288, 24576)
        arp = mid.take(Q, 2, 2, 128)
        bm, kap = mid.take(Q, T), mid.take(Q, T)
        hT = mid.take(DC, NT)
        mixT = hT
        W, gg, yT = mid.take(Q, NT), mid.take(Q, NT), mid.take(Q, NT)
        bv = W
        S = mid.take(2048)
        segm = mid.take(NT)
        smp = mid.take(6, Q, NB)
        ar2 = Region(32768, 49600)
        xflat = ar2.take(Q, 292)
        xc, gb, gr, gi, aB = (ar2.take(Q, NT) for _ in range(5))
        xtok = ar2.take(3, D)
        al = Region(32768, 39216)
        tok = [al.take(2, DA) for _ in range(4)]
        ahT = al.take(Q, T)
        ST = al.take(NCH + 1, Q, HN)
        LV = ar2.take(8, HN)
        diag = view(ar2.at - 512, 3, 128)
        bones = ar2.take(128)
        x2 = view(ar2.at, DC, NT)
        m_su, m_iu = ar2.take(128), ar2.take(128)
        mL = [ar2.take(128) for _ in range(LEVELS)]
        sel4 = ar2.take(4, 128)
        svb = ar2.take(352)
        cT = ar2.take(DC, 32)
        assert ar2.at >= 42928 + DC * NT
        SA = view(ar2.at, 2, DA)
        wbd = [ar2.take(Q, 128) for _ in range(2)]
        so = [ar2.take(NROW, MA), ar2.take(108), ar2.take(36)]
        nso = [126, 108, 36]
        badaT, shiftT, h0T = keep.take(48), keep.take(NB, MA), keep.take(NB, Q)
        A1 = ar2.take(DC, NROW)
        omm, omka, sp = ar2.take(MA), ar2.take(Q), ar2.take(8, Q)
        rows = {n: ar2.take(128) for n in ("c", "prm", "bada", "shift", "conv", "lru")}
        nrows = {"c": 72, "prm": NPAR, "bada": 48, "shift": 112, "conv": 96, "lru": 32}
        sorow = [rows["prm"], rows["bada"], rows["shift"]]
        ar2.at = 49600 - 2048
        Z = view(ar2.at, 2, DA)
        lora = ar2.take(2, DA)
        adar = [ar2.take(512) for _ in range(2)]
        fold = keep.take(E)
        gn_sq = [bm.rearrange("p q n -> p (q n)")[:, 512 * k:512 * k + 512].rearrange("p (q n) -> p q n", q=Q)
                 for k in range(2)] + [smp[:, 0, :, :]]
        gn_rs = [kap.rearrange("p q n -> p (q n)")[:, 512 * k:512 * k + 512].rearrange("p (q n) -> p q n", q=Q)
                 for k in range(2)] + [smp[:, 1, :, :]]
        gn_cols = [slice(0, P), slice(P, T), slice(T, NT)]
        late = Region(moe.at, 49600)
        sq2 = x2
        A2 = late.take(DC, NROW)
        rs2 = late.take(NT)
        rw = late.take(DC, E)
        rb = late.take(E)
        lgt = late.take(3, E)
        lbase = late.take(E)
        x1tmp = [late.take(NB) for _ in range(2)]
        late.at = max(late.at, 49600 - 1024)
        wkvo = late.take(Q, 128)
        ex, msk, eq, ce = (late.take(3, E) for _ in range(4))
        top, sc = late.take(3, 8), late.take(3, 8)
        seg = keep.take(3, E)
        sqsum = rs2
        lgs = rs2
        gtT = rs2
        fin = Region(0, 8192)
        x1o = fin.take(DC, NT)
        fing = fin.take(D)
        x1t = fin.take(3, D)
        g2b, g2s = fin.take(D), fin.take(512)
        gt, fsq = view(8192, 3, D), view(8192 + 3 * D, 3, D)
        sems = {}

        def sem(name):
            if name not in sems:
                sems[name] = ctx.enter_context(nc.semaphore(name))
            return sems[name]

        bank_full = [sem(f"bank_full{b}") for b in range(8)]
        bank_out = [sem(f"bank_out{b}") for b in range(8)]
        jobs = job_list()
        where, taken = {}, [0] * 8
        for k, (name, n) in enumerate(jobs):
            before = taken[k % 8]
            taken[k % 8] += n
            where[name] = (k % 8, k // 8 + 1, before, taken[k % 8])

        def bank(*name):
            return ps[where[name][0]]

        def wait_full(eng, *name):
            b, n, _, _ = where[name]
            eng.wait_ge(bank_full[b], n)

        def wait_out(eng, *name):
            b, _, _, n = where[name]
            eng.wait_ge(bank_out[b], n)

        x1_bank = [0, 4, 1, 2, 3, 0]
        bias_bank = [6, 7, 4, 2, 3]

        count = {}

        def signal(eng, ins, name):
            count[name] = count.get(name, 0) + 1
            ins.then_inc(sem(name), 1)
            eng.wait_ge(sem(name), count[name])

        def mark(ins, name):
            count[name] = count.get(name, 0) + 1
            ins.then_inc(sem(name), 1)

        def settle(eng, name):
            eng.wait_ge(sem(name), count[name])

        def ring(n):
            return sem(f"front_loaded{n % FR}"), 16 * (n // FR + 1)

        unit_of = {("ada", c0 // 512): n for n, (what, c0, _) in enumerate(UNITS) if what == "ada"}
        for n, (what, c0, w) in enumerate(UNITS):
            if what == "win":
                unit_of.update({("win", m): n for m in range(c0 // P, (c0 + w) // P)})
        last_job = {}
        for name, _ in jobs:
            if name[0] in ("ada", "proj"):
                last_job[unit_of[("ada" if name[0] == "ada" else "win", name[1])]] = name

        block = ctx.enter_context(nc.Block())

        def vcol(name, k=0):
            return prm[:, PAT[name] + k:PAT[name] + k + 1]

        def mod(i, c, rows_):
            return modT[:, i * DC + c, rows_]

        a_order = [n[1] for n, _ in jobs if n[0] == "proj" and n[1] < MA]

        @block.sync
        def _(sp_):
            def rows_in(dst, src, name):
                sp_.dma_start(dst, src).then_inc(sem(name), 16)

            src = {"ada": I["w_ada"], "win": I["w_in"]}

            def unit_in(n):
                what, c0, w = UNITS[n]
                if n >= FR:
                    wait_full(sp_, *last_job[n - FR])
                sp_.dma_start(fslot[n % FR][:, :, 0:w],
                              src[what][0, :, c0:c0 + w].rearrange("(c p) n -> p c n", p=P))\
                   .then_inc(sem(f"front_loaded{n % FR}"), 16)

            rows_in(rows["c"][0:8, :], I["c_prompt"].rearrange("a (c p) -> (a c) p", p=P), "ld_c")
            rows_in(rows["c"][8:72, :], I["c_sample"].rearrange("a (c p) -> (a c) p", p=P), "ld_c")
            sp_.dma_start(xtok[:, 0:2, :], I["x_prompt"].rearrange("a (t p) d -> p (a t) d", p=P))\
               .then_inc(sem("ld_x"), 16)
            sp_.dma_start(xtok[0:NB, 2, :], I["x_sample"].rearrange("b a d -> (b a) d"))\
               .then_inc(sem("ld_x"), 16)
            unit_in(0)
            rows_in(rows["bada"][0:48, :], I["b_ada"].rearrange("a (c p) -> (a c) p", p=P), "ld_bada")
            unit_in(1)
            a0 = 0
            for name, k in PARAMS:
                vector = I[name]
                flat = {"rk_r_k": "l h n -> (l h n)", "lru_conv_w": "l w d -> (l w d)"}.get(name, "l d -> (l d)")
                sp_.dma_start(rows["prm"][a0:a0 + k, :], vector.rearrange(flat).rearrange("(r p) -> r p", p=P))\
                   .then_inc(sem("ld_prm"), 16)
                a0 += k
            unit_in(2)
            for n in range(FR, len(UNITS)):
                unit_in(n)
            wait_out(sp_, "tk", 1, 3)
            wait_out(sp_, "bo", 3)
            sp_.wait_ge(sem("vectors_done"), 1)
            sp_.dma_start(wout[:, :, :], I["w_out"][0].rearrange("(c p) n -> p c n", p=P))\
               .then_inc(sem("ld_wout"), 16)

            mats = [I["w_gate"], I["w_up"], I["w_down"]]

            def load(e, t, slot, half, signal_sem):
                cs = slice(4 * half, 4 * half + 4)
                sp_.dma_start(wslot[slot][:, cs, :], mats[t][0, bass.ds(e, 1), 512 * half:512 * half + 512, :]
                              .rearrange("a (c p) n -> p (a c) n", p=P)).then_inc(signal_sem, 16)

            def load_both(e, t, slot):
                for half in range(2):
                    load(e, t, slot, half, sem(f"w_loaded{slot}_{half}"))

            for g in range(2):
                wait_out(sp_, "SA", NCH - 1, g)
            sp_.dma_start(rw[:, :, :], I["router_w"][0].rearrange("(c p) n -> p c n", p=P))\
               .then_inc(sem("ld_router"), 16)
            sp_.dma_start(rb[0:1, :], I["router_b"]).then_inc(sem("ld_router"), 16)
            wait_out(sp_, "Y2", 1)
            sp_.wait_ge(sem("sample_y"), 2)
            load_both(0, 0, 0)
            sp_.wait_ge(sem("mixA_done"), 2)
            sp_.wait_ge(sem("mixA0_done"), 1)
            load_both(0, 1, 1)
            wait_full(sp_, "mA", DC - 1)
            sp_.wait_ge(sem("states_out"), 16 * 8)
            load_both(0, 2, 2)
            wait_full(sp_, "ss2")
            sp_.dma_start(bg[0:E, :], I["b_gate"][0]).then_inc(sem("ld_bias"), 16)
            sp_.dma_start(bu[0:E, :], I["b_up"][0]).then_inc(sem("ld_bias"), 16)
            load_both(1, 0, 3)
            sp_.wait_ge(sem("x1_done"), 1)
            sp_.dma_start(x1_dram, x1T.rearrange("p c t -> p (c t)")).then_inc(sem("x1_out"), 16)
            for c in range(2):
                wait_out(sp_, "g2", c)
            sp_.dma_start(gate2_dram, gate2[0:NROW, :]).then_inc(sem("gate2_out"), 16)
            for c in range(2):
                wait_full(sp_, "h2", 2, c)
            sp_.dma_start(bd[0:E, :], I["b_down"][0]).then_inc(sem("ld_bdown"), 16)

            def expert_loads(e, r, first=0):
                for t in range(first, 3):
                    slot = (3 * r + t) % 4
                    name = ("down", "gate", "up")[t]
                    for half in range(2):
                        sp_.wait_ge(sem(name + ("_half", "_done")[half]), e - 1 if t == 0 else e)
                        load(e, t, slot, half, sem(f"w_loaded{slot}_{half}"))

            expert_loads(1, 1, first=1)
            expert_loads(2, 2)
            expert_loads(3, 3)
            with sp_.Fori(1, E // 4) as i:
                for r in range(4):
                    expert_loads(4 * i + r, r)
            sp_.wait_ge(sem("down_done"), E - 1)
            sp_.wait_ge(sem("x1_out"), 16)
            sp_.wait_ge(sem("gate2_out"), 16)
            sp_.dma_start(x1o.rearrange("p c t -> p (c t)"), x1_dram).then_inc(sem("ld_end"), 16)
            sp_.dma_start(g2b[:, :], gate2_dram[0:1, :].broadcast_to([P, D])).then_inc(sem("ld_gate2"), 16)
            for h in range(2):
                sp_.dma_start(g2s[64 * h:64 * h + NB, :], gate2_dram[1:NROW, 512 * h:512 * h + 512])\
                   .then_inc(sem("ld_gate2"), 16)
            sp_.dma_start(fing[:, :], I["final_g"].rearrange("(a d) -> a d", a=1).broadcast_to([P, D]))\
               .then_inc(sem("ld_end"), 16)
            sp_.wait_ge(sem("router_done"), 1)
            n = sp_.alloc_register("sp_block")
            c = sp_.alloc_register("sp_over")
            sp_.reg_load(c, cnt_i[0:1, (OVER + 1) * E:(OVER + 1) * E + 1])
            with sp_.If(sp_.snap(c) > 0):
                sp_.reg_mov(n, E)
                with sp_.Fori(1, OVER + 1) as b:
                    with sp_.Fori(0, E) as e:
                        sp_.reg_load(c, cnt_i[0:1, bass.ds(b * E + e, 1)])
                        with sp_.If(sp_.snap(c) > 0):
                            sp_.wait_ge(sem("down_done"), sp_.snap(n))
                            for t in range(3):
                                for half in range(2):
                                    load(e, t, t + 1, half, sem("w_again"))
                            sp_.reg_add(n, n, 1)
                        sp_.nop()
                sp_.nop()
            sp_.nop()
            for t in range(2):
                sp_.wait_ge(sem("out_ready"), t + 1)
                sp_.dma_start(O["y_prompt"][0, P * t:P * t + P, :], gt[:, t, :]).then_inc(sem("y_out"), 16)
            sp_.wait_ge(sem("out_ready"), 3)
            sp_.dma_start(O["y_sample"].rearrange("b a d -> (b a) d"), gt[0:NB, 2, :])\
               .then_inc(sem("y_out"), 16)
            sp_.wait_ge(sem("y_out"), 48)

        @block.gpsimd
        def _(pool):
            def step(ins, name="pool_done"):
                signal(pool, ins, name)

            def tri_mask(m, cuts):
                step(pool.memset(m, 1.0))
                for v, pattern, base, cm in cuts:
                    step(pool.affine_select(out=v, in_=v, compare_op=ALU.is_ge, fill=0.0, base=base,
                                            pattern=pattern, channel_multiplier=cm))

            step(pool.memset(ident, 0.0))
            step(pool.affine_select(out=ident, in_=ident, compare_op=ALU.not_equal, fill=1.0, base=0,
                                    pattern=[[-1, 128]], channel_multiplier=1), "ident_ready")
            step(pool.memset(ones, 1.0), "consts")
            step(pool.memset(eps1, 1e-6), "consts")
            step(pool.memset(epsx, 64e-5), "consts")
            step(pool.tensor_tensor(fold, ident[:, 0:32], ident[:, 32:64], ALU.add))
            step(pool.tensor_tensor(fold, fold, ident[:, 64:96], ALU.add))
            step(pool.tensor_tensor(fold, fold, ident[:, 96:128], ALU.add), "fold_ready")
            hb = bones.rearrange("p (h n) -> p h n", n=HN)
            tri_mask(bones, [(hb, [[-HN, 2], [0, HN]], 0, 1), (hb, [[HN, 2], [0, HN]], HN - 1, -1)])
            for m, strict in ((m_su, 1), (m_iu, 0)):
                v = m.rearrange("p (c t) -> p c t", t=CH)
                tri_mask(m, [(v, [[-CH, CPT], [0, CH]], 0, 1), (v, [[CH, CPT], [1, CH]], -strict, -1)])
            for l in range(LEVELS):
                b = 1 << l
                v = mL[l].rearrange("p (g h j) -> p g h j", h=2, j=b)
                n = P // (2 * b)
                tri_mask(mL[l], [(v, [[-2 * b, n], [0, 2], [0, b]], -b, 1),
                                 (v, [[2 * b, n], [0, 2], [0, b]], 2 * b - 1, -1),
                                 (v, [[0, n], [-1, 2], [0, b]], 0, 0)])
            step(pool.memset(segm[:, :], 1.0))
            step(pool.memset(segm[:, 0:T:CH], 0.0))
            step(pool.memset(segm[:, T:NT], 0.0), "consts2")
            step(pool.memset(sel4[0:32, :, :], 0.0))
            for k in range(4):
                v = sel4[0:32, k, :].rearrange("p (b q k) -> p b q k", q=Q, k=4)[:, :, :, k]
                step(pool.affine_select(out=v, in_=v, compare_op=ALU.not_equal, fill=1.0, base=0,
                                        pattern=[[-1, NB], [-NB, Q]], channel_multiplier=1), "consts2")
            tri_mask(tri, [(tri, [[1, 128]], -1, -1)])
            step(pool.iota(iota.bitcast(I32), [[0, 2], [1, 64]], base=0, channel_multiplier=0))
            step(pool.tensor_copy(iota, iota.bitcast(I32)), "iota_ready")

            Sv = S.rearrange("p (i j) -> p i j", j=HN)
            Tv = Stmp.rearrange("p (i j) -> p i j", j=HN)
            sh = [P, 32, HN]
            vec = lambda k: svb[:, 64 * k:64 * k + 64].unsqueeze(1).to_broadcast(sh)
            vrow = svb[:, 320:352].unsqueeze(2).to_broadcast(sh)
            red = sv[:, 0, 0:32]
            wait_out(pool, "smpB")
            pool.wait_ge(sem("ld_S"), 16)
            step(pool.tensor_tensor(Tv, Sv, vec(3), ALU.mult), "sample_steps")
            pool.wait_ge(sem("sample_red"), 2)
            step(pool.tensor_tensor(Sv, Sv, vec(2), ALU.mult))
            step(pool.tensor_tensor(Tv, vec(4), red.unsqueeze(2).to_broadcast(sh), ALU.mult))
            step(pool.tensor_tensor(Sv, Sv, Tv, ALU.subtract))
            step(pool.tensor_tensor(Tv, vec(1), vrow, ALU.mult))
            step(pool.tensor_tensor(Sv, Sv, Tv, ALU.add), "sample_state")
            step(pool.tensor_tensor(Tv, Sv, vec(0), ALU.mult), "sample_steps")
            pool.wait_ge(sem("vectors_done"), 1)
            for q in range(Q):
                wait_out(pool, "lg", q)
                step(pool.tensor_scalar(bv[:, q, :], bv[:, q, :], vcol("rk_lnx_b", q), None, ALU.add))
                step(pool.tensor_tensor(bv[:, q, :], bv[:, q, :], gg[:, q, :], ALU.mult))
                step(pool.tensor_scalar(gg[:, q, :], gg[:, q, :], vcol("rk_lnx_w", q), None, ALU.mult), "gates_ready")
            pool.wait_ge(sem("tile0_inverted"), 1)
            v = yT[:, :, gn_cols[0]]
            step(pool.tensor_tensor(v, v, gn_rs[0], ALU.mult))
            step(pool.tensor_tensor(v, v, gg[:, :, gn_cols[0]], ALU.mult))
            step(pool.tensor_tensor(mixT[:, 0:Q, gn_cols[0]], v, bv[:, :, gn_cols[0]], ALU.add), "mixA0_done")
            for g in range(2):
                wait_out(pool, "SA", NCH - 1, g)
            step(pool.memset(seg[:, :, :], 1.0))
            step(pool.memset(seg[:, :, 0:1], 0.0))
            step(pool.memset(lgt[:, 2, :], 0.0), "router_zero")
            for c in range(1, DC - 1):
                pool.wait_ge(sem("sq2_done"), c + 1)
                step(pool.tensor_tensor(sqsum[:, :], sqsum[:, :] if c > 1 else sq2[:, 0, :], sq2[:, c, :], ALU.add),
                     "squares_summed")
            pool.wait_ge(sem("states_out"), 16 * 8)
            step(pool.memset(PTz[0][:, :], 0.0), "ptz_zero")
            step(pool.memset(PTz[1][:, :], 0.0), "ptz_zero")

        @block.scalar
        def _(act):
            def step(ins, name="act_done"):
                signal(act, ins, name)

            def out(ins, *name):
                ins.then_inc(bank_out[where[name][0]], 1)

            act.wait_ge(sem("ld_x"), 32)
            act.wait_ge(sem("consts"), 3)
            for t in range(3):
                n = P if t < 2 else NB
                mark(act.activation(squares[0:n, t, :], xtok[0:n, t, :], ACT.Square, accum_out=ssq[0:n, t:t + 1]),
                     "x_squared")
            settle(act, "x_squared")
            for t in range(3):
                n = P if t < 2 else NB
                mark(act.activation(rstd[0:n, t:t + 1], ssq[0:n, t:t + 1], ACT.Sqrt, bias=eps1[0:n, :],
                                    scale=1.0 / D), "x_root")
            act.wait_ge(sem("ct_zero"), 1)
            wait_full(act, "t", "c")
            out(act.activation(cT[:, :, 0:NROW], bank("t", "c")[:, 0:72].rearrange("p (t c) -> p c t", c=DC),
                               ACT.Silu), "t", "c")

            adas = [n[1] for n, _ in jobs if n[0] == "ada"]

            def ada(j):
                k = adas.index(j)
                wait_full(act, "ada", j)
                if k > 1:
                    wait_full(act, "adaT", adas[k - 2])
                out(act.activation(adar[k % 2][:, :], bank("ada", j)[:, :], ACT.Copy), "ada", j)

            def proj_a(*ms):
                for m in ms:
                    wait_full(act, "proj", m)
                    act.wait_ge(sem("derived"), 1)
                    out(act.activation(so[0][:, :, m], bank("proj", m)[:, T - 1:NT], ACT.Copy), "proj", m)
                    mark(act.activation(z[:, m, :], bank("proj", m)[:, 0:NT], ACT.Copy, scale=omm[:, m:m + 1]),
                         "z_part")

            ada(0)
            for c in range(DC):
                wait_full(act, "xT", c)
                out(act.activation(hT[:, c, :], bank("xT", c)[:, 0:NT], ACT.Copy), "xT", c)
            for j in (2, 1, 3):
                ada(j)
            for name, pat in (("shift", "l b (c p) -> (l b c) p"), ("conv", "l b w (c p) -> (l b w c) p"),
                              ("lru", "l b (c p) -> (l b c) p")):
                act.dma_start(rows[name][0:nrows[name], :], I["state_" + name].rearrange(pat, p=P))\
                   .then_inc(sem("ld_rows"), 16)
            act.dma_start(lora[0:64, 0, :], I["rk_w_up"][0]).then_inc(sem("ld_lora"), 16)
            act.dma_start(lora[64:128, 0, :], I["rk_a_up"][0]).then_inc(sem("ld_lora"), 16)
            act.dma_start(lora[:, 1, :], I["rk_g_up"][0]).then_inc(sem("ld_lora"), 16)
            act.wait_ge(sem("wbd_zero"), 1)
            for k, name in enumerate(("lru_w_r", "lru_w_i")):
                w = I[name][0].rearrange("(q h) c d -> h c q d", h=2)
                act.dma_start(wbd[k][0:64, :, 0:64], w[0]).then_inc(sem("ld_wbd"), 16)
                act.dma_start(wbd[k][64:128, :, 64:128], w[1]).then_inc(sem("ld_wbd"), 16)
            act.dma_start(S[:, :], I["state_wkv"][0].rearrange("b h (s i) j -> (b h s) (i j)", s=2))\
               .then_inc(sem("ld_S"), 16)

            act.wait_ge(sem("xflat_zero"), 1)
            for m in range(18, 22):
                c = m - 18
                wait_full(act, "proj", m)
                out(act.activation(xflat[:, c, 3:3 + T], bank("proj", m)[:, 0:T], ACT.Copy), "proj", m)
                out(act.activation(xflat[:, c, 259:291].rearrange("p (b w) -> p b w", w=4)[:, :, 3],
                                   bank("proj", m)[:, T:NT], ACT.Copy), "proj", m)
            act.wait_ge(sem("sp_one"), 1)
            step(act.activation(sp[:, 1, :], sp[:, 0, :], ACT.Exp, scale=-1.0), "sp_exp")
            ada(4)
            for m in range(14, 18):
                wait_full(act, "proj", m)
                out(act.activation(gb[:, m - 14, :], bank("proj", m)[:, 0:NT], ACT.Gelu_apprx_tanh),
                    "proj", m)
            ada(5)
            for c in range(Q):
                wait_full(act, "gr", c)
                out(act.activation(gr[:, c, :], bank("gr", c)[:, 0:NT], ACT.Sigmoid, bias=vcol("lru_b_r", c)),
                    "gr", c)
                wait_full(act, "gi", c)
                out(act.activation(gi[:, c, :], bank("gi", c)[:, 0:NT], ACT.Sigmoid, bias=vcol("lru_b_i", c)),
                    "gi", c)
            proj_a(12, 13)
            act.wait_ge(sem("sp_done"), 1)
            for c in range(Q):
                wait_out(act, "gr", c)
                mark(act.activation(aB[:, c, :], gr[:, c, :], ACT.Exp, scale=sp[:, 3, c:c + 1]), "lru_a")
            settle(act, "lru_a")
            ada(6)
            for c in range(Q):
                mark(act.activation(gr[:, c, :], gr[:, c, :], ACT.Tanh, scale=sp[:, 2, c:c + 1]), "lru_th")
            act.wait_ge(sem("z_done"), 2)
            mark(act.activation(z[0:64, 12, :], z[0:64, 12, :], ACT.Tanh), "lora_in")
            mark(act.activation(z[:, 13, :], z[:, 13, :], ACT.Sigmoid), "lora_in")
            proj_a(4, 5)
            for q in range(Q):
                wait_full(act, "lw", q)
                out(act.activation(sigw[:, q, :], bank("lw", q)[:, 0:NT], ACT.Sigmoid, bias=vcol("rk_w0", q)),
                    "lw", q)
            for q in range(Q):
                wait_full(act, "la", q)
                out(act.activation(aa[:, q, :], bank("la", q)[:, 0:NT], ACT.Sigmoid, bias=vcol("rk_a0", q)),
                    "la", q)
            for q in range(Q):
                wait_full(act, "lg", q)
                out(act.activation(gg[:, q, :], bank("lg", q)[:, 0:NT], ACT.Copy), "lg", q)
            proj_a(6, 7)
            act.wait_ge(sem("lru_b2"), 1)
            step(act.activation(gr[:, :, :], gr[:, :, :], ACT.Sqrt), "lru_root")
            ada(7)
            proj_a(0)
            act.wait_ge(sem("cum_done"), Q + 1)
            step(act.activation(W[:, :, :], cum[:, :, :], ACT.Exp, scale=-EXP_HALF), "decays")
            mark(act.activation(cum[:, :, :], cum[:, :, :], ACT.Exp, scale=EXP_HALF), "decays")
            mark(act.activation(sigw[:, :, :], sigw[:, :, :], ACT.Exp, scale=-EXP_HALF), "decays")
            for q in range(Q):
                wait_full(act, "kn", q)
                act.wait_ge(sem("kk2_done"), 1)
                out(act.activation(yT[:, q, :], bank("kn", q)[:, 0:NT], ACT.Sqrt), "kn", q)
            proj_a(1, 2)
            wait_full(act, "ssB")
            out(act.activation(gr[:, 0, :], bank("ssB")[:, 0:NT], ACT.Sqrt, bias=eps1, scale=1.0 / DA), "ssB")
            proj_a(3)
            ada(8)
            proj_a(8, 9, 10, 11)
            ada(9)
            ada(10)

            def tk_copies(t, ks):
                for k in ks:
                    wait_full(act, "tk", t, k)
                    out(act.activation(tok[k][:, t, :], bank("tk", t, k)[:, :], ACT.Copy), "tk", t, k)

            def u_copies(t):
                for g in range(2):
                    wait_full(act, "U", t, g)
                    out(act.activation(U[:, 4 * g:4 * g + 4, :].rearrange("p u n -> p (u n)"),
                                       bank("U", t, g)[:, :], ACT.Copy), "U", t, g)

            def xt_copies(t):
                for l in range(LEVELS - 1):
                    for g in range(2):
                        wait_full(act, "XT", t, g, l)
                        out(act.activation(XT[:, 4 * g:4 * g + 4, :].rearrange("p u n -> p (u n)"),
                                           bank("XT", t, g, l)[:, :], ACT.Copy), "XT", t, g, l)

            def system_copies(t):
                xt_copies(t)
                for k in ("LV", "Z", "AH"):
                    for g in range(2):
                        wait_full(act, k, t, g)
                        b = bank(k, t, g)
                        if k == "LV":
                            dst, b = LV[:, 4 * g:4 * g + 4, :].rearrange("p u n -> p (u n)"), b[:, 0:256]
                        elif k == "Z":
                            dst, b = Z[:, t, 256 * g:256 * g + 256], b[:, 0:256]
                        else:
                            rows_ = slice(64 * g, 64 * g + 64)
                            dst, b = ahT[rows_, :, P * t:P * t + P], b[rows_, :].rearrange("p (q n) -> p q n", q=Q)
                        out(act.activation(dst, b, ACT.Copy), k, t, g)

            def y1_copy(t):
                wait_full(act, "Y1", t)
                out(act.activation(yT[:, :, P * t:P * t + P],
                                   bank("Y1", t)[:, :].rearrange("p (q n) -> p q n", q=Q), ACT.Copy), "Y1", t)

            def x2_copies(cs):
                for c in cs:
                    wait_full(act, "x2", c)
                    out(act.activation(x2[:, c, :], bank("x2", c)[:, 0:NT], ACT.Copy), "x2", c)

            def root(k):
                wait_full(act, "va", k)
                n = gn_cols[k].stop - gn_cols[k].start
                out(act.activation(gn_rs[k], bank("va", k)[:, 0:Q * n].rearrange("p (q n) -> p q n", q=Q),
                                   ACT.Sqrt, bias=epsx, scale=1.0 / HN), "va", k)

            def state(dst, src):
                act.dma_start(dst, src).then_inc(sem("states_out"), 16)

            wait_full(act, "proj", 11)
            act.wait_ge(sem("normB_done"), Q)
            mark(act.activation(mixT[:, Q:2 * Q, :], xc[:, :, :], ACT.Copy), "mixB_done")
            settle(act, "mixB_done")
            tk_copies(0, range(4))
            ada(11)
            u_copies(0)
            for k in range(2):
                wait_full(act, "smpT", k)
                out(act.activation(sv[0:32, 3 * k:3 * k + 3, :].rearrange("p k n -> p (k n)"),
                                   bank("smpT", k)[0:32, 0:384], ACT.Copy), "smpT", k)
            wait_full(act, "smpB")
            out(act.activation(svb[:, :], bank("smpB")[:, 0:352], ACT.Copy), "smpB")
            system_copies(0)
            for n in range(3):
                wait_full(act, "so", n)
                out(act.activation(sorow[n][0:nso[n], :], bank("so", n)[0:nso[n], 0:128], ACT.Copy), "so", n)
            tk_copies(1, range(4))
            u_copies(1)
            for n in range(3):
                wait_out(act, "so", n)
            state(O["shift_prompt"].rearrange("a b (m p) -> (a b m) p", p=P), sorow[0][0:14, :])
            state(O["shift_sample"].rearrange("a b (m p) -> (a b m) p", p=P), sorow[0][14:126, :])
            state(O["conv_prompt"].rearrange("a b w (c p) -> (a b w c) p", p=P), sorow[1][0:12, :])
            state(O["conv_sample"].rearrange("a b w (c p) -> (a b w c) p", p=P), sorow[1][12:108, :])
            state(O["lru_prompt"].rearrange("a b (c p) -> (a b c) p", p=P), sorow[2][0:4, :])
            state(O["lru_sample"].rearrange("a b (c p) -> (a b c) p", p=P), sorow[2][4:36, :])
            system_copies(1)
            y1_copy(0)
            y1_copy(1)
            act.wait_ge(sem("sample_y"), 2)
            for g in range(2):
                wait_out(act, "XT", 1, g, LEVELS - 1)
            x2_copies(range(DC))
            root(0)
            root(1)
            root(2)
            act.wait_ge(sem("sample_state"), 1)
            state(O["wkv_sample"][0].rearrange("b h (s i) j -> (b h s) (i j)", s=2), S[:, :])
            wait_full(act, "wkv")
            out(act.activation(wkvo[0:HN, :, :].rearrange("p q n -> p (q n)"), bank("wkv")[0:HN, :], ACT.Copy),
                "wkv")
            wait_out(act, "wkv")
            state(O["wkv_prompt"].rearrange("a b h i j -> i (a b h) j"),
                  wkvo[0:HN, :, :].rearrange("p q (t j) -> p (q t) j", t=2))
            wait_full(act, "ss2")
            out(act.activation(rs2[:, :], bank("ss2")[:, 0:NT], ACT.Sqrt, bias=eps1, scale=1.0 / D), "ss2")
            for c in range(DC):
                act.wait_ge(sem("h2_scaled"), c + 1)
                mark(act.activation(h2T[:, c, 0:T], h2T[:, c, 0:T], ACT.Identity, bias=mod(3, c, slice(0, 1))),
                     "h2_done")
            wait_full(act, "lgT")
            out(act.activation(lgs[:, :], bank("lgT")[:, 0:NT], ACT.Copy), "lgT")
            for t in range(3):
                for c in range(2):
                    n = P if t < 2 else NB
                    if (t, c) == (0, 0):
                        act.wait_ge(sem("gates_in"), 1)
                        mark(act.activation(ex[:, :, :], ex[:, :, :], ACT.Exp), "gates_exp")
                    wait_full(act, "h2", t, c)
                    out(act.activation(h2tok[0:n, t, 512 * c:512 * c + 512], bank("h2", t, c)[0:n, :], ACT.Copy),
                        "h2", t, c)
            for c in range(2):
                wait_full(act, "g2", c)
                out(act.activation(gate2[0:NROW, 512 * c:512 * c + 512], bank("g2", c)[0:NROW, :], ACT.Copy),
                    "g2", c)

            def x_copy(n):
                act.wait_ge(sem("gathered"), n + 1)
                act.activation(Xg[:, :], ps[2][:, :], ACT.Copy).then_inc(sem("x_copied"), 1)

            def xt_copy(n):
                act.wait_ge(sem("x_turned"), n + 1)
                act.activation(XTg[:, :], ps[3][:, :], ACT.Copy).then_inc(sem("xt_copied"), 1)

            def sigmoid(n):
                act.wait_ge(sem("g_read"), n + 1)
                if not isinstance(n, int) or n > 0:
                    act.wait_ge(sem("glu_done"), n)
                act.activation(sg_sb[:, :], g_sb[:, :], ACT.Sigmoid, scale=1.702).then_inc(sem("sig_done"), 1)

            def at_copy(n):
                act.wait_ge(sem("act_turned"), n + 1)
                act.activation(aT_sb[:, :], ps[3][:, :], ACT.Copy).then_inc(sem("at_copied"), 1)

            def pt_copy(n):
                act.wait_ge(sem("pt_turned"), n + 1)
                act.activation(PTz[0][0:64, :], ps[4][0:64, 0:NT], ACT.Copy).then_inc(sem("pt_copied"), 1)
                act.activation(PTz[1][64:128, :], ps[4][64:128, 0:NT], ACT.Copy).then_inc(sem("pt_copied"), 1)

            def out_copy(n):
                act.wait_ge(sem("down_done"), n + 1)
                act.activation(o_sb[:, :], ps[5][:, :], ACT.Copy).then_inc(sem("out_copied"), 1)

            def block_step(n, last=False):
                sigmoid(n)
                if not last:
                    x_copy(n + 1)
                at_copy(n)
                pt_copy(n)
                if not last:
                    xt_copy(n + 1)
                out_copy(n)

            act.wait_ge(sem("ptz_zero"), 2)
            x_copy(0)
            xt_copy(0)
            for r in range(4):
                block_step(r)
            with act.Fori(1, E // 4 - 1) as i:
                for r in range(4):
                    block_step(4 * i + r)
            for r in range(4):
                block_step(E - 4 + r, last=(r == 3))
            for k in range(6):
                t, c = k // 2, k % 2
                n = P if t < 2 else NB
                act.wait_ge(sem("x1_turned"), k + 1)
                act.activation(x1t[0:n, t, 512 * c:512 * c + 512], ps[x1_bank[k]][0:n, :], ACT.Copy)\
                   .then_inc(sem("x1_copied"), 1)
            n = act.alloc_register("act_block")
            c = act.alloc_register("act_over")
            act.wait_ge(sem("router_done"), 1)
            act.reg_load(c, cnt_i[0:1, (OVER + 1) * E:(OVER + 1) * E + 1])
            with act.If(act.snap(c) > 0):
                act.reg_mov(n, E)
                with act.Fori(1, OVER + 1) as b:
                    with act.Fori(0, E) as e:
                        act.reg_load(c, cnt_i[0:1, bass.ds(b * E + e, 1)])
                        with act.If(act.snap(c) > 0):
                            k = act.snap(n)
                            x_copy(k)
                            xt_copy(k)
                            block_step(k, last=True)
                            act.reg_add(n, n, 1)
                        act.nop()
                act.nop()
            act.nop()
            for t in range(3):
                n = P if t < 2 else NB
                act.wait_ge(sem("x3_ready"), t + 1)
                act.activation(fsq[0:n, t, :], gt[0:n, t, :], ACT.Square, accum_out=ssq[0:n, t:t + 1])\
                   .then_inc(sem("ss3_done"), 1)
                act.wait_ge(sem("ss3_done"), t + 1)
                act.activation(rstd[0:n, t:t + 1], ssq[0:n, t:t + 1], ACT.Sqrt, bias=eps1[0:n, :],
                               scale=1.0 / D).then_inc(sem("root3"), 1)
            act.wait_ge(sem("states_out"), 16 * 8)

        @block.vector
        def _(dve):
            def step(ins, name="lanes_done"):
                signal(dve, ins, name)

            def out(ins, *name):
                ins.then_inc(bank_out[where[name][0]], 1)

            def tt(o, a, b, op, name="lanes_done"):
                step(dve.tensor_tensor(o, a, b, op), name)

            def ts(o, a, s1, s2, op0, op1=ALU.bypass, name="lanes_done"):
                step(dve.tensor_scalar(o, a, s1, s2, op0, op1), name)

            def stt(o, a, s, b, op0, op1, name="lanes_done"):
                step(dve.scalar_tensor_tensor(out=o, in0=a, scalar=s, in1=b, op0=op0, op1=op1), name)

            step(dve.memset(cT[:, :, :], 0.0), "ct_zero")
            step(dve.memset(wbd[0][:, :, :], 0.0))
            step(dve.memset(wbd[1][:, :, :], 0.0), "wbd_zero")
            step(dve.memset(xflat[:, :, :], 0.0), "xflat_zero")
            step(dve.memset(cnt_i[:, :], 0), "count_zero")
            dve.wait_ge(sem("ident_ready"), 1)
            dve.wait_ge(sem("x_root"), 3)
            for t in range(3):
                n = P if t < 2 else NB
                step(dve.reciprocal(rstd[0:n, t:t + 1], rstd[0:n, t:t + 1]))
                ts(diag[0:n, t, 0:n], ident[0:n, 0:n], rstd[0:n, t:t + 1], None, ALU.mult, name="diag_ready")

            def column_vectors(name, dst):
                wait_full(dve, "t", name)
                src = bank("t", name)[:, 0:nrows[name]]
                if name == "conv":
                    dst = xflat[:, :, 259:291].rearrange("p c (b w) -> p c b w", w=4)
                    src = src.rearrange("p (b w c) -> p c b w", w=3, c=Q)
                    for c in range(Q):
                        ins = dve.tensor_copy(dst[:, c, :, 0:3], src[:, c, :, :])
                        if c < Q - 1:
                            step(ins)
                    out(ins, "t", name)
                else:
                    out(dve.tensor_copy(dst, src), "t", name)
                wait_out(dve, "t", name)

            column_vectors("prm", prm[:, 0:NPAR])
            column_vectors("bada", badaT[:, :])

            def adaT(j):
                wait_full(dve, "adaT", j)
                out(dve.tensor_tensor(modT[:, 4 * j:4 * j + 4, :],
                                      bank("adaT", j)[:, 0:64].rearrange("p (g r) -> p g r", g=4)[:, :, 0:NROW],
                                      badaT[:, 4 * j:4 * j + 4].unsqueeze(2).to_broadcast([P, 4, NROW]),
                                      ALU.add), "adaT", j)
                wait_out(dve, "adaT", j)

            def gains(A, scale, norm, cs):
                ts(A[:, cs, :], modT[:, scale * DC + cs.start:scale * DC + cs.stop, :], 1.0, None, ALU.add)
                g_ = prm[:, PAT[norm] + cs.start:PAT[norm] + cs.stop]
                tt(A[:, cs, :], A[:, cs, :], g_.unsqueeze(2).to_broadcast([P, cs.stop - cs.start, NROW]), ALU.mult)

            def affine(v, A, shift, cs, name):
                tt(v[:, cs, T:NT], v[:, cs, T:NT], A[:, cs, 1:NROW], ALU.mult)
                tt(v[:, cs, T:NT], v[:, cs, T:NT], modT[:, shift * DC + cs.start:shift * DC + cs.stop, 1:NROW],
                   ALU.add)
                for c in range(cs.start, cs.stop):
                    mark(dve.tensor_scalar(v[:, c, 0:T], v[:, c, 0:T], A[:, c, 0:1], mod(shift, c, slice(0, 1)),
                                           ALU.mult, ALU.add), name)

            for c0, js in ((0, (0, 2)), (4, (1, 3))):
                cs = slice(c0, c0 + 4)
                for j in js:
                    adaT(j)
                for c in range(c0, c0 + 4):
                    wait_out(dve, "xT", c)
                gains(A1, 1, "norm1_g", cs)
                affine(hT, A1, 0, cs, "h_done")
            ts(omm[:, :], prm[:, 0:MA], -1.0, 1.0, ALU.mult, ALU.add, name="derived")
            ka = prm[:, PAT["rk_k_a"]:PAT["rk_k_a"] + Q]
            ts(omka[:, :], ka, -1.0, 1.0, ALU.mult, ALU.add)
            lam = prm[:, PAT["lru_lambda"]:PAT["lru_lambda"] + Q]
            ts(sp[:, 4, :], lam, -1.0, None, ALU.mult)
            tt(sp[:, 0, :], sp[:, 4, :], lam, ALU.max, name="sp_one")
            column_vectors("shift", shiftT.rearrange("p b m -> p (b m)"))
            column_vectors("conv", None)
            column_vectors("lru", h0T.rearrange("p b c -> p (b c)"))

            dve.wait_ge(sem("sp_exp"), 1)
            e_, s_, s2_, q_ = (sp[:, k, :] for k in (1, 5, 6, 7))
            ts(q_, e_, 2.0, None, ALU.add)
            step(dve.reciprocal(q_, q_))
            tt(s_, e_, q_, ALU.mult)
            tt(s2_, s_, s_, ALU.mult)
            ts(q_, s2_, 1.0 / 17, None, ALU.mult)
            for k in (15, 13, 11, 9, 7, 5, 3):
                stt(q_, q_, 1.0 / k, s2_, ALU.add, ALU.mult)
            stt(q_, q_, 1.0, s_, ALU.add, ALU.mult)
            ts(sp[:, 4, :], sp[:, 4, :], 0.0, None, ALU.max)
            stt(q_, q_, 2.0, sp[:, 4, :], ALU.mult, ALU.add)
            ts(sp[:, 2, :], q_, 8.0, None, ALU.mult)
            ts(sp[:, 3, :], q_, -8.0, None, ALU.mult, name="sp_done")

            adaT(4)
            cw = lambda j, c: vcol("lru_conv_w", 4 * j + c)
            for c in range(Q):
                wait_out(dve, "proj", 18 + c)
                wait_out(dve, "t", "conv")
                tmp = aB.rearrange("p c n -> p (c n)")[:, 0:288]
                ts(tmp, xflat[:, c, 0:288], cw(0, c), vcol("lru_conv_b", c), ALU.mult, ALU.add)
                stt(tmp, xflat[:, c, 1:289], cw(1, c), tmp, ALU.mult, ALU.add)
                stt(tmp, xflat[:, c, 2:290], cw(2, c), tmp, ALU.mult, ALU.add)
                stt(xc[:, c, 0:T], xflat[:, c, 3:259], cw(3, c), tmp[:, 0:T], ALU.mult, ALU.add)
                smp_x = xflat[:, c, 259:291].rearrange("p (b w) -> p b w", w=4)[:, :, 3]
                smp_t = aB.rearrange("p c n -> p (c n)")[:, 259:291].rearrange("p (b w) -> p b w", w=4)[:, :, 0]
                stt(xc[:, c, T:NT], smp_x, cw(3, c), smp_t, ALU.mult, ALU.add, name="conv_done")
            for c in range(Q):
                step(dve.tensor_copy(so[1][:, 0:12].rearrange("p (w c) -> p c w", c=Q)[:, c, :],
                                     xflat[:, c, 256:259]))
                step(dve.tensor_copy(so[1][:, 12:108].rearrange("p (b w c) -> p c b w", c=Q, w=3)[:, c, :, :],
                                     xflat[:, c, 259:291].rearrange("p (b w) -> p b w", w=4)[:, :, 1:4]), "conv_state")

            def mix_shift(*ms):
                for m in ms:
                    wait_full(dve, "proj", m)
                    dve.wait_ge(sem("z_part"), a_order.index(m) + 1)
                    out(dve.scalar_tensor_tensor(out=z[:, m, 1:T], in0=bank("proj", m)[:, 0:T - 1],
                                                 scalar=vcol("rk_mu", m), in1=z[:, m, 1:T],
                                                 op0=ALU.mult, op1=ALU.add), "proj", m)
                    mark(dve.scalar_tensor_tensor(out=z[:, m, T:NT], in0=shiftT[:, :, m], scalar=vcol("rk_mu", m),
                                                  in1=z[:, m, T:NT], op0=ALU.mult, op1=ALU.add), "z_done")

            def z_ready(*ms):
                for m in ms:
                    wait_out(dve, "proj", m)
                dve.wait_ge(sem("z_done"), max(a_order.index(m) for m in ms) + 1)

            adaT(5)
            mix_shift(12, 13)
            mix_shift(4)
            adaT(6)
            mix_shift(5)
            dve.wait_ge(sem("lru_a"), Q)
            dve.wait_ge(sem("lru_th"), Q)
            for c in range(Q):
                wait_out(dve, "gi", c)
            tt(gi[:, :, :], gi[:, :, :], xc[:, :, :], ALU.mult)
            tt(xc[:, :, :], aB[:, :, :], aB[:, :, :], ALU.mult)
            stt(gr[:, :, :], xc[:, :, :], 1.0, gr[:, :, :], ALU.add, ALU.mult, name="lru_b2")
            dve.wait_ge(sem("consts2"), 1)
            for q in range(Q):
                wait_out(dve, "lw", q)
                mark(dve.tensor_tensor_scan(cum[:, q, :], segm[:, :], sigw[:, q, :], 0.0, ALU.mult, ALU.add),
                     "cum_done")
            settle(dve, "cum_done")
            tt(sigw[:, :, :], cum[:, :, :], sigw[:, :, :], ALU.subtract, name="cum_done")
            mix_shift(6, 7)
            z_ready(4, 5, 6, 7)
            for q in range(Q):
                mark(dve.tensor_scalar(kk[:, q, :], z[:, 4 + q, :], vcol("rk_k_k", q), None, ALU.mult), "kk_done")
            settle(dve, "kk_done")
            tt(yT[:, :, :], kk[:, :, :], kk[:, :, :], ALU.mult, name="kk2_done")
            dve.wait_ge(sem("lru_root"), 1)
            tt(gi[:, :, :], gi[:, :, :], gr[:, :, :], ALU.mult)
            for c in range(Q):
                mark(dve.tensor_tensor_scan(xc[:, c, 0:T], aB[:, c, 0:T], gi[:, c, 0:T], 0.0, ALU.mult, ALU.add),
                     "lanes_done")
            h0 = h0T.rearrange("p b c -> p c b")
            tt(xc[:, :, T:NT], aB[:, :, T:NT], h0, ALU.mult)
            tt(xc[:, :, T:NT], xc[:, :, T:NT], gi[:, :, T:NT], ALU.add)
            step(dve.tensor_copy(so[2][:, 0:4].unsqueeze(2), xc[:, :, T - 1:T]))
            step(dve.tensor_copy(so[2][:, 4:36].rearrange("p (b c) -> p c b", c=Q), xc[:, :, T:NT]), "lru_state")
            for c in range(Q):
                wait_out(dve, "proj", 14 + c)
            tt(xc[:, :, :], xc[:, :, :], gb[:, :, :], ALU.mult)
            tt(gi[:, :, :], xc[:, :, :], xc[:, :, :], ALU.mult, name="sqB_done")
            mix_shift(0)
            adaT(7)

            zk = z[:, 4:8, :]
            for q in range(Q):
                wait_out(dve, "la", q)
            arp_flat = arp.rearrange("p q t k n -> p (q t k n)")
            fq = [arp_flat[:, 512 * q:512 * q + NT] for q in range(Q)]
            for q in range(Q):
                mark(dve.tensor_scalar(fq[q], aa[:, q, :], vcol("rk_k_a", q), omka[:, q:q + 1], ALU.mult, ALU.add),
                     "lanes_done")
            settle(dve, "lanes_done")
            for q in range(Q):
                mark(dve.tensor_tensor(z[:, 4 + q, :], z[:, 4 + q, :], fq[q], ALU.mult), "lanes_done")
            for q in range(Q):
                wait_out(dve, "kn", q)
            ts(yT[:, :, :], yT[:, :, :], 1e-12, None, ALU.max)
            step(dve.reciprocal(yT[:, :, :], yT[:, :, :]))
            tt(kk[:, :, :], kk[:, :, :], yT[:, :, :], ALU.mult)
            tt(aa[:, :, :], kk[:, :, :], aa[:, :, :], ALU.mult)
            mix_shift(1, 2)
            wait_out(dve, "ssB")
            step(dve.reciprocal(gr[:, 0, :], gr[:, 0, :]))
            for c in range(Q):
                mark(dve.scalar_tensor_tensor(out=xc[:, c, :], in0=xc[:, c, :], scalar=vcol("lru_norm_g", c),
                                              in1=gr[:, 0, :], op0=ALU.mult, op1=ALU.mult), "normB_done")
            mix_shift(3)
            dve.wait_ge(sem("decays"), 3)
            z_ready(0, 1, 2, 3)
            zr, zv = z[:, 0:4, :], z[:, 8:12, :]
            two = lambda v: v.rearrange("p (t n) -> p t n", t=2)
            for q in range(Q):
                if q == 2:
                    mix_shift(8)
                    adaT(8)
                for ins in (
                        dve.scalar_tensor_tensor(out=bm[:, q, :], in0=aa[:, q, 0:T], scalar=-1.0,
                                                 in1=cum[:, q, 0:T], op0=ALU.mult, op1=ALU.mult),
                        dve.tensor_tensor(kap[:, q, :], z[:, 4 + q, 0:T], cum[:, q, 0:T], ALU.mult),
                        dve.tensor_tensor(arp[:, q, :, 0, :], two(kk[:, q, 0:T]), two(sigw[:, q, 0:T]), ALU.mult),
                        dve.tensor_tensor(arp[:, q, :, 1, :], two(z[:, q, 0:T]), two(W[:, q, 0:T]), ALU.mult)):
                    mark(ins, "bm_done")
            settle(dve, "bm_done")
            mix_shift(9, 10, 11)
            z_ready(8, 9, 10, 11)
            adaT(9)
            for q in range(Q):
                mark(dve.scalar_tensor_tensor(out=cum[:, q, :], in0=z[:, q, :], scalar=vcol("rk_r_k", q),
                                              in1=z[:, 4 + q, :], op0=ALU.mult, op1=ALU.mult), "rk_done")
            for k, src in enumerate((zr, zk, W, kk, aa, zv)):
                mark(dve.tensor_copy(smp[:, k, :, :], src[:, :, T:NT]), "smp_done")
            wend = sp[:, 0:8, :].rearrange("p a b -> p (a b)")[:, 0:Q * NCH].rearrange("p (q c) -> p q c", q=Q)
            step(dve.tensor_copy(wend, W[:, :, CH - 1:T:CH]))
            adaT(10)
            adaT(11)
            wait_out(dve, "tk", 0, 3)
            step(dve.memset(ST[:, 0, :, :], 0.0))

            four = lambda m: m.unsqueeze(1).to_broadcast([P, 4, 128])
            grp = lambda b: b[:, :].rearrange("p (u n) -> p u n", u=4)

            def l_masks(t):
                for g in range(2):
                    u = slice(4 * g, 4 * g + 4)
                    wait_full(dve, "L", t, g)
                    out(dve.tensor_tensor(X[:, u, :], grp(bank("L", t, g)), four(mL[0]), ALU.mult), "L", t, g)
                for g in range(2):
                    u = slice(4 * g, 4 * g + 4)
                    wait_out(dve, "L", t, g)
                    tt(X[:, u, :], X[:, u, :], four(ident), ALU.add, name="x_init")

            def pair_masks(t):
                for k, dst, m, n0 in (("Ak", Ak, m_su, 0), ("Rb", Rb, m_iu, 8 * t), ("Rk", Rk, m_iu, 8 * t)):
                    for g in range(2):
                        wait_full(dve, k, t, g)
                        out(dve.tensor_tensor(dst[:, n0 + 4 * g:n0 + 4 * g + 4, :], grp(bank(k, t, g)), four(m),
                                              ALU.mult), k, t, g)

            def level(t, l):
                for g in range(2):
                    u = slice(4 * g, 4 * g + 4)
                    wait_full(dve, "Y", t, g, l)
                    out(dve.tensor_tensor(Y[:, u, :], grp(bank("Y", t, g, l)), four(mL[l]), ALU.mult),
                        "Y", t, g, l)
                k, dst = ("X", X) if l < LEVELS - 1 else ("XT", XT)
                for g in range(2):
                    u = slice(4 * g, 4 * g + 4)
                    wait_full(dve, k, t, g, l)
                    if k == "XT" or l > 1:
                        wait_out(dve, k, t, g, l - 1)
                    out(dve.tensor_tensor(dst[:, u, :], grp(bank(k, t, g, l)), dst[:, u, :], ALU.add),
                        k, t, g, l)

            def sa_sum(c):
                t, r = c // CPT, slice(CH * (c % CPT), CH * (c % CPT) + CH)
                for g in range(2):
                    gc = slice(256 * g, 256 * g + 256)
                    wait_full(dve, "SA", c, g)
                    wait_out(dve, "Z", t, g)
                    out(dve.tensor_tensor(SA[r, t, gc], bank("SA", c, g)[r, 0:256], Z[r, t, gc], ALU.add),
                        "SA", c, g)

            def state_sum(c):
                wait_full(dve, "SU", c)
                b = bank("SU", c)[:, 0:Q * HN].rearrange("p (q n) -> p q n", q=Q)
                out(dve.tensor_tensor(ST[:, c + 1, :, :], b, ST[:, c, :, :], ALU.add), "SU", c)
                wait_out(dve, "SU", c)
                tt(ST[:, c + 1, :, :], ST[:, c + 1, :, :], wend[:, :, c].unsqueeze(2).to_broadcast([P, Q, HN]),
                   ALU.mult, name="state_done")

            def y_sum(t):
                wait_full(dve, "Y2", t)
                wait_out(dve, "Y1", t)
                yt = yT[:, :, P * t:P * t + P]
                out(dve.tensor_tensor(yt, bank("Y2", t)[:, :].rearrange("p (q n) -> p q n", q=Q), yt, ALU.add),
                    "Y2", t)

            def centre(k):
                n = gn_cols[k].stop - gn_cols[k].start
                wait_full(dve, "mu", k)
                v = yT[:, :, gn_cols[k]]
                out(dve.scalar_tensor_tensor(out=v, in0=bank("mu", k)[:, 0:Q * n].rearrange("p (q n) -> p q n", q=Q),
                                             scalar=-1.0 / HN, in1=v, op0=ALU.mult, op1=ALU.add), "mu", k)
                wait_out(dve, "mu", k)
                tt(gn_sq[k], v, v, ALU.mult, name=f"squares{k}")

            def inverted(k, name):
                wait_out(dve, "va", k)
                step(dve.reciprocal(gn_rs[k], gn_rs[k]), name)

            def gated(k):
                v = yT[:, :, gn_cols[k]]
                tt(v, v, gn_rs[k], ALU.mult)
                dve.wait_ge(sem("gates_ready"), Q)
                tt(v, v, gg[:, :, gn_cols[k]], ALU.mult)
                tt(mixT[:, 0:Q, gn_cols[k]], v, bv[:, :, gn_cols[k]], ALU.add, name="mixA_done")

            def mixing(k, cs, dst, base):
                for c in cs:
                    wait_full(dve, k, c)
                    if k == "mB":
                        wait_out(dve, "x2", c)
                    b = bank(k, c)
                    out(dve.scalar_tensor_tensor(out=dst[:, c, 0:T], in0=b[:, 0:T], scalar=mod(2, c, slice(0, 1)),
                                                 in1=base[:, c, 0:T], op0=ALU.mult, op1=ALU.add), k, c)
                    tmp = x1tmp[c % 2]
                    out(dve.tensor_tensor(tmp, b[:, T:NT], mod(2, c, slice(1, NROW)), ALU.mult), k, c)
                    wait_out(dve, k, c)
                    tt(dst[:, c, T:NT], base[:, c, T:NT], tmp, ALU.add, name=k + "_added")

            def key_sums(row, half, name):
                Tv = Stmp.rearrange("p (i j) -> p i j", j=HN)
                hs = slice(16 * half, 16 * half + 16)
                mark(dve.tensor_reduce(sv[:, row, hs], Tv[:, hs, :], AX, ALU.add), name)

            l_masks(0)
            pair_masks(0)
            for q in range(Q):
                wait_full(dve, "bo", q)
                out(dve.tensor_tensor(bv[:, q, :], bank("bo", q)[:, 0:NT], z[:, 8 + q, :], ALU.mult), "bo", q)
            for q in range(Q):
                wait_out(dve, "bo", q)
            step(dve.memset(small[:, 42:43], 0.0), "vectors_done")
            for l in range(1, LEVELS):
                level(0, l)
                if l in (3, 4):
                    dve.wait_ge(sem("sample_steps"), 1)
                    key_sums(0, l - 3, "sample_red")
            sa_sum(0)
            state_sum(0)
            sa_sum(1)
            l_masks(1)
            state_sum(1)
            pair_masks(1)
            for l in range(1, LEVELS):
                level(1, l)
                if l in (3, 4):
                    dve.wait_ge(sem("sample_steps"), 2)
                    key_sums(1, l - 3, "sample_y")
            sa_sum(2)
            state_sum(2)
            y_sum(0)
            wait_out(dve, "Y2", 0)
            sa_sum(3)
            centre(0)
            y_sum(1)
            wait_full(dve, "syT")
            b = bank("syT")[0:32, 0:128].rearrange("p (b q k) -> p k q b", q=Q, k=4)
            for k in range(4):
                out(dve.tensor_copy(yT[32 * k:32 * k + 32, :, T:NT], b[:, k, :, :]), "syT")
            wait_out(dve, "Y2", 1)
            wait_out(dve, "syT")
            centre(1)
            centre(2)
            mixing("mB", [0], x2, x2)
            inverted(1, "lanes_done")
            mixing("mB", [1], x2, x2)
            inverted(0, "tile0_inverted")
            gated(1)
            mixing("mB", [2], x2, x2)
            inverted(2, "lanes_done")
            gated(2)
            mixing("mB", [3], x2, x2)
            state_sum(3)
            mixing("mB", range(4, DC), x2, x2)
            gains(A2, 4, "norm2_g", slice(0, DC))
            for c in range(DC):
                mixing("mA", [c], x1T, x2)
                mark(dve.tensor_tensor(sq2[:, c, :], x1T[:, c, :], x1T[:, c, :], ALU.mult), "sq2_done")
                mark(dve.tensor_scalar(h2T[:, c, 0:T], x1T[:, c, 0:T], A2[:, c, 0:1], None, ALU.mult), "x1_gained")
            step(dve.memset(lbase[0:1, 0:1], 0.0), "x1_done")
            tt(h2T[:, :, T:NT], x1T[:, :, T:NT], A2[:, :, 1:NROW], ALU.mult, name="x1_gained")
            wait_out(dve, "ss2")
            step(dve.reciprocal(rs2[:, :], rs2[:, :]))
            tt(h2T[:, :, T:NT], h2T[:, :, T:NT], rs2[:, T:NT].unsqueeze(1).to_broadcast([P, DC, NB]), ALU.mult)
            tt(h2T[:, :, T:NT], h2T[:, :, T:NT], modT[:, 3 * DC:4 * DC, 1:NROW], ALU.add, name="h2_samples")
            for c in range(DC):
                mark(dve.tensor_tensor(h2T[:, c, 0:T], h2T[:, c, 0:T], rs2[:, 0:T], ALU.mult), "h2_scaled")

            dve.wait_ge(sem("iota_ready"), 1)
            dve.wait_ge(sem("router_zero"), 1)
            wait_full(dve, "lg2")
            b = bank("lg2")[:, 0:96].rearrange("p (t e) -> p t e", t=3)
            out(dve.tensor_copy(lgt[:, 0:2, :], b[:, 0:2, :]), "lg2")
            out(dve.tensor_copy(lgt[0:NB, 2, :], b[0:NB, 2, :]), "lg2")
            wait_out(dve, "lg2")
            for t in range(3):
                mark(dve.max(top[:, t, :], lgt[:, t, :]), "top_done")
            settle(dve, "top_done")
            over = lambda v: v.to_broadcast([P, 3, E])
            mark(dve.tensor_tensor(ex[:, :, :], lgt[:, :, :], over(top[:, :, 0:1]), ALU.subtract), "gates_in")
            mark(dve.tensor_tensor(eq[:, :, :], lgt[:, :, :], over(top[:, :, 3:4]), ALU.is_equal), "lanes_done")
            tt(msk[:, :, :], lgt[:, :, :], over(top[:, :, 3:4]), ALU.is_gt)
            mark(dve.tensor_reduce(sc[:, :, 0:1], msk[:, :, :], AX, ALU.add), "lanes_done")
            flat = lambda v: v.rearrange("p t e -> p (t e)")
            step(dve.tensor_tensor_scan(flat(ce), flat(seg), flat(eq), 0.0, ALU.mult, ALU.add))
            tt(ce[:, :, :], ce[:, :, :], over(sc[:, :, 0:1]), ALU.add)
            stt(ce[:, :, :], ce[:, :, :], 4.0, eq[:, :, :], ALU.is_le, ALU.mult)
            tt(msk[:, :, :], msk[:, :, :], ce[:, :, :], ALU.add, name="mask_done")
            dve.wait_ge(sem("gates_exp"), 1)
            tt(ex[:, :, :], ex[:, :, :], msk[:, :, :], ALU.mult)
            step(dve.tensor_reduce(sc[:, :, 1:2], ex[:, :, :], AX, ALU.add))
            step(dve.reciprocal(sc[:, :, 1:2], sc[:, :, 1:2]))
            tt(gatew[:, :, :], ex[:, :, :], over(sc[:, :, 1:2]), ALU.mult, name="gatew_done")
            wait_full(dve, "rank")
            b = bank("rank")[:, 0:96].rearrange("p (t e) -> p t e", t=3)
            out(dve.scalar_tensor_tensor(out=lgt[:, 0:2, :], in0=b[:, 0:2, :], scalar=1.0, in1=msk[:, 0:2, :],
                                         op0=ALU.add, op1=ALU.mult), "rank")
            out(dve.scalar_tensor_tensor(out=lgt[0:NB, 2, :], in0=b[0:NB, 2, :], scalar=1.0,
                                         in1=msk[0:NB, 2, :], op0=ALU.add, op1=ALU.mult), "rank")
            wait_out(dve, "rank")

            def places(k):
                mark(dve.tensor_scalar(rankb[:, :, E * k:E * k + E], lgt[:, :, :], -1.0 - SLOTS * k, None, ALU.add),
                     "places_done")

            def counts():
                step(dve.tensor_copy(gatew[64:72, 2, :], gatew[0:8, 2, :]), "gatew_done")
                for k in range(1, OVER + 1):
                    places(k)
                for k in range(OVER + 1):
                    ts(cnt_i[0:1, E * k:E * k + E], lbase[0:1, :], float(-SLOTS * k), 0.0, ALU.add, ALU.max)
                step(dve.tensor_reduce(cnt_i[0:1, (OVER + 1) * E:(OVER + 1) * E + 1], cnt_i[0:1, E:2 * E], AX,
                                       ALU.max), "router_done")

            places(0)
            wait_full(dve, "cnt")
            out(dve.tensor_copy(lbase[0:1, :], bank("cnt")[0:1, 0:E]), "cnt")
            wait_out(dve, "cnt")
            settle(dve, "places_done")

            def select(n, k, e, buf, turned):
                if turned is not None:
                    dve.wait_ge(sem("pt_turned"), turned)
                    dve.wait_ge(sem("up_done"), turned)
                for t in range(3):
                    m = P if t < 2 else NB
                    dve.tensor_scalar(Psel[buf][0:m, t, :], iota[0:m, :], rankb[0:m, t, bass.ds(k, 1)], None,
                                      ALU.is_equal).then_inc(sem("selected"), 1)
                dve.tensor_scalar(selb[buf][0:E, :], ones[0:E, 0:64], ident[0:E, bass.ds(e, 1)], None,
                                  ALU.mult).then_inc(sem("selected"), 1)

            def glu_g(n):
                dve.wait_ge(sem("gate_done"), n + 1)
                if not isinstance(n, int) or n > 0:
                    dve.wait_ge(sem("act_ready"), n)
                dve.tensor_scalar(g_sb[:, :], ps[0][:, :], 7.0, None, ALU.min).then_inc(sem("g_read"), 1)

            def glu_u(n):
                dve.wait_ge(sem("up_done"), n + 1)
                dve.tensor_scalar(u_sb[:, :], ps[1][:, :], 7.0, -7.0, ALU.min, ALU.max).then_inc(sem("u_read"), 1)
                dve.wait_ge(sem("sig_done"), n + 1)
                dve.tensor_tensor(g_sb[:, :], g_sb[:, :], sg_sb[:, :], ALU.mult).then_inc(sem("glu_done"), 1)
                dve.wait_ge(sem("glu_done"), n + 1)
                dve.wait_ge(sem("u_read"), n + 1)
                if not isinstance(n, int) or n > 0:
                    dve.wait_ge(sem("act_turned"), n)
                dve.scalar_tensor_tensor(out=a_sb[:, :], in0=u_sb[:, :], scalar=1.0, in1=g_sb[:, :],
                                         op0=ALU.add, op1=ALU.mult).then_inc(sem("act_ready"), 1)

            def add_out(n, e):
                if not isinstance(n, int) or n > 0:
                    dve.wait_ge(sem("y_added"), 6 * n)
                for k in range(4):
                    t, h = k // 2, k % 2
                    dve.wait_ge(sem("scattered"), 5 * n + k + 1)
                    v = y[:, t, 512 * h:512 * h + 512]
                    dve.scalar_tensor_tensor(out=v, in0=ps[6 + k % 2][:, :], scalar=gatew[:, t, bass.ds(e, 1)],
                                             in1=v, op0=ALU.mult, op1=ALU.add).then_inc(sem("y_added"), 1)
                dve.wait_ge(sem("scattered"), 5 * n + 5)
                for p0 in (0, 64):
                    v = y_s[p0:p0 + NB, :]
                    dve.scalar_tensor_tensor(out=v, in0=ps[6][p0:p0 + NB, :],
                                             scalar=gatew[p0:p0 + NB, 2, bass.ds(e, 1)], in1=v,
                                             op0=ALU.mult, op1=ALU.add).then_inc(sem("y_added"), 1)

            def y_start():
                dve.wait_ge(sem("gt_turned"), 1)
                step(dve.tensor_copy(gtT[0:E, :], ps[7][0:E, 0:NT]), "gt_copied")
                dve.wait_ge(sem("x1_out"), 16)
                for k in range(5):
                    dve.wait_ge(sem("y_bias"), k + 1)
                    if k < 4:
                        step(dve.tensor_copy(y[:, k // 2, 512 * (k % 2):512 * (k % 2) + 512],
                                             ps[bias_bank[k]][:, :]), "y_started")
                    else:
                        step(dve.tensor_copy(y_s[0:NB, :], ps[bias_bank[4]][0:NB, :]))
                        step(dve.tensor_copy(y_s[64:64 + NB, :], ps[bias_bank[4]][64:64 + NB, :]), "y_started")

            select(0, 0, 0, 0, None)
            counts()
            for n in range(4):
                glu_g(n)
                select(n + 1, n + 1, n + 1, (n + 1) % 2, n if n > 0 else None)
                glu_u(n)
                if n > 0:
                    add_out(n - 1, n - 1)
                else:
                    y_start()
            with dve.Fori(1, E // 4 - 1) as i:
                for r in range(4):
                    n = 4 * i + r
                    glu_g(n)
                    select(n + 1, n + 1, n + 1, (r + 1) % 2, n)
                    glu_u(n)
                    add_out(n - 1, n - 1)
            for r in range(4):
                n = E - 4 + r
                glu_g(n)
                if r < 3:
                    select(n + 1, n + 1, n + 1, (r + 1) % 2, n)
                glu_u(n)
                add_out(n - 1, n - 1)
            add_out(E - 1, E - 1)
            nreg = dve.alloc_register("dve_block")
            c = dve.alloc_register("dve_over")
            dve.reg_mov(nreg, E)
            dve.reg_load(c, cnt_i[0:1, (OVER + 1) * E:(OVER + 1) * E + 1])
            with dve.If(dve.snap(c) > 0):
                with dve.Fori(1, OVER + 1) as b:
                    with dve.Fori(0, E) as e:
                        dve.reg_load(c, cnt_i[0:1, bass.ds(b * E + e, 1)])
                        with dve.If(dve.snap(c) > 0):
                            n = dve.snap(nreg)
                            select(n, b * E + e, e, 0, n)
                            glu_g(n)
                            glu_u(n)
                            add_out(n, e)
                            dve.reg_add(nreg, nreg, 1)
                        dve.nop()
                dve.nop()
            dve.nop()
            dve.wait_ge(sem("x1_copied"), 6)
            dve.wait_ge(sem("ld_gate2"), 48)
            dve.wait_ge(sem("y_added"), dve.snap(nreg) * 6)
            for t in range(2):
                tt(gt[:, t, :], g2b[:, :], y[:, t, :], ALU.mult)
                tt(gt[:, t, :], gt[:, t, :], x1t[:, t, :], ALU.add, name="x3_ready")
            for h in range(2):
                p0, cs = 64 * h, slice(512 * h, 512 * h + 512)
                tt(g_sb[p0:p0 + NB, :], g2s[p0:p0 + NB, :], y_s[p0:p0 + NB, :], ALU.mult)
            step(dve.tensor_copy(u_sb[0:NB, :], g_sb[64:64 + NB, :]))
            for h in range(2):
                cs = slice(512 * h, 512 * h + 512)
                mark(dve.tensor_tensor(gt[0:NB, 2, cs], (u_sb if h else g_sb)[0:NB, :], x1t[0:NB, 2, cs], ALU.add),
                     "x3_samples")
            settle(dve, "x3_samples")
            step(dve.memset(small[:, 41:42], 0.0), "x3_ready")
            dve.wait_ge(sem("ld_end"), 32)
            for t in range(3):
                n = P if t < 2 else NB
                dve.wait_ge(sem("root3"), t + 1)
                step(dve.reciprocal(rstd[0:n, t:t + 1], rstd[0:n, t:t + 1]))
                stt(gt[0:n, t, :], gt[0:n, t, :], rstd[0:n, t:t + 1], fing[0:n, :], ALU.mult, ALU.mult,
                    name="out_ready")

        @block.tensor
        def _(pe):
            order = [n for n, _ in jobs]
            pos = [0]

            def start(*name):
                assert order[pos[0]] == name, (order[pos[0]], name)
                pos[0] += 1
                b, _, before, _ = where[name]
                if before:
                    pe.wait_ge(bank_out[b], before)
                return ps[b]

            def done(ins, *name):
                ins.then_inc(bank_full[where[name][0]], 1)

            def turn(dst, src):
                return pe.transpose(dst, src, ident[0:src.shape[0], 0:src.shape[0]])

            def rows_turned(name):
                o = start("t", name)
                done(turn(o[:, 0:nrows[name]], rows[name][0:nrows[name], :]), "t", name)

            pe.wait_ge(sem("ident_ready"), 1)
            pe.wait_ge(sem("ld_c"), 32)
            rows_turned("c")
            adas = [n[1] for n, _ in jobs if n[0] == "ada"]

            def ada_part(j):
                n = unit_of[("ada", j)]
                w = fslot[n % FR]
                o = start("ada", j)
                pe.wait_ge(*ring(n))
                wait_out(pe, "t", "c")
                for c in range(2):
                    for g in range(4):
                        mm = pe.matmul(o[32 * g:32 * g + 32, :], cT[:, 2 * g + c, :], w[:, 2 * g + c, :],
                                       start=(c == 0), stop=(c == 1))
                done(mm, "ada", j)

            def ada_turned(j):
                o = start("adaT", j)
                wait_out(pe, "ada", j)
                pe.wait_ge(sem("fold_ready"), 1)
                for g in range(4):
                    mm = pe.matmul(o[:, 16 * g:16 * g + 16], adar[adas.index(j) % 2][:, P * g:P * g + P], fold[:, 0:16],
                                   start=True, stop=True)
                done(mm, "adaT", j)

            def ada(*js):
                for j in js:
                    ada_part(j)
                    ada_turned(j)

            def proj(*ms):
                for m in ms:
                    o = start("proj", m)
                    n = unit_of[("win", m)]
                    pe.wait_ge(*ring(n))
                    w = fslot[n % FR]
                    c0 = P * m - UNITS[n][1]
                    for c in range(DC):
                        if m == 18:
                            pe.wait_ge(sem("h_done"), c + 1)
                        mm = pe.matmul(o[:, 0:NT], w[:, c, c0:c0 + P], hT[:, c, :], start=(c == 0),
                                       stop=(c == DC - 1))
                    done(mm, "proj", m)

            ada_part(0)
            pe.wait_ge(sem("diag_ready"), 3)
            for c in range(DC):
                o = start("xT", c)
                for t in range(3):
                    n = P if t < 2 else NB
                    mm = pe.matmul(o[:, P * t:P * t + n], xtok[0:n, t, P * c:P * c + P], diag[0:n, t, 0:n],
                                   start=True, stop=True)
                done(mm, "xT", c)
            ada_part(2)
            pe.wait_ge(sem("ld_prm"), 16 * len(PARAMS))
            rows_turned("prm")
            pe.wait_ge(sem("ld_bada"), 16)
            rows_turned("bada")
            ada_turned(0)
            ada_turned(2)
            ada(1, 3)
            proj(18, 19, 20, 21)
            pe.wait_ge(sem("ld_rows"), 16 * 3)
            for name in ("shift", "conv", "lru"):
                rows_turned(name)
            ada_part(4)
            proj(14)
            ada_turned(4)
            proj(15, 16, 17)
            ada_part(5)
            pe.wait_ge(sem("ld_wbd"), 64)
            for c in range(Q):
                pe.wait_ge(sem("conv_done"), c + 1)
                for k, name in enumerate(("gr", "gi")):
                    o = start(name, c)
                    done(pe.matmul(o[:, 0:NT], wbd[k][:, c, :], xc[:, c, :], start=True, stop=True), name, c)
            ada_turned(5)
            proj(12, 13)
            ada_part(6)
            proj(4)
            ada_turned(6)
            proj(5)
            pe.wait_ge(sem("ld_lora"), 48)
            pe.wait_ge(sem("z_done"), 2)
            pe.wait_ge(sem("lora_in"), 2)
            for name, w, m, p0, p1 in (("lw", 0, 12, 0, 64), ("la", 0, 12, 64, 128), ("lg", 1, 13, 0, 128)):
                for q in range(Q):
                    o = start(name, q)
                    done(pe.matmul(o[:, 0:NT], lora[p0:p1, w, P * q:P * q + P], z[p0:p1, m, :],
                                   start=True, stop=True), name, q)
            proj(6, 7)
            ada_part(7)
            proj(0)
            ada_turned(7)
            pe.wait_ge(sem("kk2_done"), 1)
            for q in range(Q):
                o = start("kn", q)
                done(pe.matmul(o[:, 0:NT], bones, yT[:, q, :], start=True, stop=True), "kn", q)
            proj(1, 2)
            pe.wait_ge(sem("consts"), 3)
            pe.wait_ge(sem("consts2"), 5)
            o = start("ssB")
            pe.wait_ge(sem("sqB_done"), 1)
            for c in range(Q):
                mm = pe.matmul(o[:, 0:NT], ones, gi[:, c, :], start=(c == 0), stop=(c == Q - 1))
            done(mm, "ssB")
            proj(3)
            ada_part(8)
            proj(8)
            ada_turned(8)
            proj(9, 10, 11)
            ada_part(9)
            pe.wait_ge(sem("bm_done"), 4 * Q)

            def head(h):
                return slice(64 * (h % 2), 64 * (h % 2) + 64), h // 2

            def unit(h):
                return 4 * (h % 2) + h // 2

            def tk(t, ks):
                tc = slice(P * t, P * t + P)
                srcs = [lambda q: bm[:, q, tc], lambda q: kap[:, q, tc], lambda q: z[:, 8 + q, tc],
                        lambda q: arp[:, q, t, 0, :]]
                for k in ks:
                    o = start("tk", t, k)
                    if k == 2:
                        pe.wait_ge(sem("z_done"), MA)
                    for q in range(Q):
                        mm = turn(o[:, P * q:P * q + P], srcs[k](q))
                    done(mm, "tk", t, k)

            def pair_products(t, *ks):
                tc = slice(P * t, P * t + P)
                pairs = {"U": (bm, 0), "L": (None, 0), "Ak": (kap, 0), "Rb": (bm, 1), "Rk": (kap, 1)}
                for k in ks:
                    for g in range(2):
                        o = start(k, t, g)
                        for j in range(4):
                            rows_, q = head(2 * j + g)
                            a, kind = pairs[k]
                            lhs = arp[rows_, q, t, 0, :] if a is None else a[rows_, q, tc]
                            rhs = bm[rows_, q, tc] if a is None else arp[rows_, q, t, kind, :]
                            mm = pe.matmul(o[:, P * j:P * j + P], lhs, rhs, start=True, stop=True)
                        done(mm, k, t, g)

            def systems(t):
                fours = lambda o, lhs, rhs, g: [
                    pe.matmul(o[:, P * j:P * j + P], lhs[:, 4 * g + j, :], rhs[:, 4 * g + j, :],
                              start=True, stop=True) for j in range(4)][-1]
                for l in range(LEVELS - 1):
                    if l > 0:
                        for g in range(2):
                            o = start("X", t, g, l)
                            wait_out(pe, "Y", t, g, l)
                            wait_out(pe, "XT", t, g, l - 1)
                            done(fours(o, XT, Y, g), "X", t, g, l)
                    for g in range(2):
                        o = start("XT", t, g, l)
                        if l == 0:
                            pe.wait_ge(sem("x_init"), 2 * t + g + 1)
                        else:
                            wait_out(pe, "X", t, g, l)
                        for j in range(4):
                            mm = turn(o[:, P * j:P * j + P], X[:, 4 * g + j, :])
                        done(mm, "XT", t, g, l)
                        o = start("Y", t, g, l + 1)
                        if l == 0:
                            wait_out(pe, "U", t, g)
                        done(fours(o, U, X, g), "Y", t, g, l + 1)
                for g in range(2):
                    o = start("XT", t, g, LEVELS - 1)
                    wait_out(pe, "Y", t, g, LEVELS - 1)
                    wait_out(pe, "XT", t, g, LEVELS - 2)
                    done(fours(o, Y, XT, g), "XT", t, g, LEVELS - 1)
                for g in range(2):
                    o = start("LV", t, g)
                    wait_out(pe, "Ak", t, g)
                    wait_out(pe, "tk", t, 2)
                    for j in range(4):
                        h = 2 * j + g
                        mm = pe.matmul(o[:, 64 * j:64 * j + 64], Ak[:, 4 * g + j, :], tok[2][:, t, 64 * h:64 * h + 64],
                                       start=True, stop=True)
                    done(mm, "LV", t, g)
                for g in range(2):
                    o = start("Z", t, g)
                    wait_out(pe, "LV", t, g)
                    wait_out(pe, "XT", t, g, LEVELS - 1)
                    for j in range(4):
                        u = 4 * g + j
                        mm = pe.matmul(o[:, 64 * j:64 * j + 64], XT[:, u, :], LV[:, u, :], start=True, stop=True)
                    done(mm, "Z", t, g)
                for g in range(2):
                    o = start("AH", t, g)
                    wait_out(pe, "tk", t, 3)
                    for j in range(4):
                        h = 2 * j + g
                        rows_, q = head(h)
                        mm = pe.matmul(o[rows_, P * q:P * q + P], tok[3][:, t, 64 * h:64 * h + 64],
                                       XT[:, 4 * g + j, :], start=True, stop=True)
                    done(mm, "AH", t, g)

            def sa(c):
                t = c // CPT
                r = slice(CH * (c % CPT), CH * (c % CPT) + CH)
                cc = slice(CH * c, CH * c + CH)
                for g in range(2):
                    o = start("SA", c, g)
                    wait_out(pe, "AH", t, g)
                    if c == 0:
                        pe.wait_ge(sem("vectors_done"), 1)
                    else:
                        pe.wait_ge(sem("state_done"), c)
                    for j in range(4):
                        rows_, q = head(2 * j + g)
                        mm = pe.matmul(o[r, 64 * j:64 * j + 64], ahT[rows_, q, cc], ST[rows_, c, q, :],
                                       start=True, stop=True)
                    done(mm, "SA", c, g)

            def state_update(c):
                t = c // CPT
                r = slice(CH * (c % CPT), CH * (c % CPT) + CH)
                o = start("SU", c)
                wait_out(pe, "tk", t, 0)
                wait_out(pe, "tk", t, 1)
                wait_out(pe, "SA", c, 0)
                wait_out(pe, "SA", c, 1)
                for h in range(H):
                    rows_, q = head(h)
                    hc = slice(64 * h, 64 * h + 64)
                    uc = slice(64 * unit(h), 64 * unit(h) + 64)
                    pe.matmul(o[rows_, 64 * q:64 * q + 64], tok[1][r, t, hc], tok[2][r, t, hc],
                              start=True, stop=False)
                    mm = pe.matmul(o[rows_, 64 * q:64 * q + 64], tok[0][r, t, hc], SA[r, t, uc],
                                   start=False, stop=True)
                done(mm, "SU", c)

            def y_state(t):
                o = start("Y1", t)
                for h in range(H):
                    rows_, q = head(h)
                    for c in range(CPT):
                        r0 = CH * c
                        mm = pe.matmul(o[rows_, P * q + r0:P * q + r0 + CH], ST[rows_, CPT * t + c, q, :],
                                       arp[rows_, q, t, 1, r0:r0 + CH], start=True, stop=True)
                done(mm, "Y1", t)

            def y_chunk(t):
                o = start("Y2", t)
                for k in ("Rb", "Rk"):
                    for g in range(2):
                        wait_out(pe, k, t, g)
                wait_out(pe, "SA", 2 * t + 1, 0)
                wait_out(pe, "SA", 2 * t + 1, 1)
                for h in range(H):
                    rows_, q = head(h)
                    u = unit(h)
                    v = o[rows_, P * q:P * q + P]
                    pe.matmul(v, SA[:, t, 64 * u:64 * u + 64], Rb[:, 8 * t + u, :], start=True, stop=False)
                    mm = pe.matmul(v, tok[2][:, t, 64 * h:64 * h + 64], Rk[:, 8 * t + u, :],
                                   start=False, stop=True)
                done(mm, "Y2", t)

            def head_sums(name, k, src):
                o = start(name, k)
                n = src.shape[2]
                done(pe.matmul(o[:, 0:Q * n].rearrange("p (q n) -> p q n", q=Q), bones, src, start=True, stop=True),
                     name, k)

            def mean(k):
                if k == 2:
                    wait_out(pe, "syT")
                else:
                    wait_out(pe, "Y2", k)
                head_sums("mu", k, yT[:, :, gn_cols[k]])

            def variance(k):
                pe.wait_ge(sem(f"squares{k}"), 1)
                head_sums("va", k, gn_sq[k])

            def x_turned(cs):
                for c in cs:
                    o = start("x2", c)
                    for t in range(3):
                        n = P if t < 2 else NB
                        mm = turn(o[:, P * t:P * t + n], xtok[0:n, t, P * c:P * c + P])
                    done(mm, "x2", c)

            def mixing(name, cs):
                k0 = Q if name == "mB" else 0
                for c in cs:
                    o = start(name, c)
                    for k in range(k0, k0 + Q):
                        mm = pe.matmul(o[:, 0:NT], wout[:, k, P * c:P * c + P], mixT[:, k, :],
                                       start=(k == k0), stop=(k == k0 + Q - 1))
                    done(mm, name, c)

            ada_part(10)
            ada_turned(9)
            tk(0, (0, 1))
            ada_turned(10)
            tk(0, (2, 3))
            ada_part(11)
            ada_turned(11)
            pair_products(0, "U", "L", "Ak", "Rb", "Rk")
            pe.wait_ge(sem("smp_done"), 6)
            for k in range(2):
                o = start("smpT", k)
                for j in range(3):
                    mm = turn(o[0:32, P * j:P * j + P], smp[:, 3 * k + j, :, :].rearrange("p q b -> p (q b)"))
                done(mm, "smpT", k)
            o = start("smpB")
            pe.wait_ge(sem("consts2"), 5)
            wait_out(pe, "smpT", 0)
            wait_out(pe, "smpT", 1)
            for k in range(4):
                h = k // 2
                pe.matmul(o[:, 0:320].rearrange("p (v n) -> p v n", v=5), sel4[0:32, k, :],
                          sv[0:32, 0:5, 64 * h:64 * h + 64], start=(k == 0), stop=(k == 3))
            for k in range(4):
                mm = pe.matmul(o[:, 320:352], sel4[0:32, k, :], sv[0:32, 5, 32 * k:32 * k + 32],
                               start=(k == 0), stop=(k == 3))
            done(mm, "smpB")
            pe.wait_ge(sem("rk_done"), Q)
            for q in range(Q):
                o = start("bo", q)
                done(pe.matmul(o[:, 0:NT], bones, cum[:, q, :], start=True, stop=True), "bo", q)

            systems(0)
            pe.wait_ge(sem("conv_state"), Q)
            pe.wait_ge(sem("lru_state"), 1)
            for n in range(3):
                o = start("so", n)
                src = so[0].rearrange("p b m -> p (b m)") if n == 0 else so[n]
                done(turn(o[0:nso[n], 0:128], src), "so", n)
            sa(0)
            tk(1, (0, 1))
            state_update(0)
            tk(1, (2, 3))
            pair_products(1, "U")
            sa(1)
            pair_products(1, "L")
            state_update(1)
            pair_products(1, "Ak", "Rb", "Rk")
            systems(1)
            sa(2)
            y_state(0)
            state_update(2)
            y_chunk(0)
            sa(3)
            y_state(1)
            mean(0)
            y_chunk(1)
            o = start("syT")
            pe.wait_ge(sem("sample_y"), 2)
            done(turn(o[0:32, 0:128], sv[:, 1, 0:32]), "syT")
            x_turned(range(0, 4))
            mean(1)
            x_turned(range(4, DC))
            pe.wait_ge(sem("ld_wout"), 16)
            pe.wait_ge(sem("mixB_done"), 1)
            mixing("mB", [0])
            variance(0)
            mean(2)
            variance(1)
            mixing("mB", [1])
            variance(2)
            mixing("mB", [2, 3])
            state_update(3)
            mixing("mB", range(4, DC))
            o = start("wkv")
            pe.wait_ge(sem("state_done"), NCH)
            for q in range(Q):
                mm = turn(o[0:HN, P * q:P * q + P], ST[:, NCH, q, :])
            done(mm, "wkv")
            pe.wait_ge(sem("mixA0_done"), 1)
            pe.wait_ge(sem("mixA_done"), 2)
            mixing("mA", range(DC))
            o = start("ss2")
            pe.wait_ge(sem("squares_summed"), DC - 2)
            pe.matmul(o[:, 0:NT], ones, sqsum[:, :], start=True, stop=False)
            pe.wait_ge(sem("sq2_done"), DC)
            done(pe.matmul(o[:, 0:NT], ones, sq2[:, DC - 1, :], start=False, stop=True), "ss2")
            pe.wait_ge(sem("ld_router"), 32)
            o = start("lgT")
            pe.wait_ge(sem("h2_samples"), 1)
            for c in range(DC):
                g = c % 4
                pe.wait_ge(sem("h2_done"), c + 1)
                mm = pe.matmul(o[32 * g:32 * g + 32, 0:NT], rw[:, c, :], h2T[:, c, :], start=(c < 4), stop=(c >= 4))
            done(mm, "lgT")
            o = start("lg2")
            wait_out(pe, "lgT")
            for t in range(3):
                n = P if t < 2 else NB
                pe.matmul(o[0:n, E * t:E * t + E], ones[0:1, 0:n], rb[0:1, :], start=True, stop=False)
                mm = pe.matmul(o[0:n, E * t:E * t + E], lgs[:, P * t:P * t + n], fold, start=False, stop=True)
            done(mm, "lg2")

            def h2_turned(ts_):
                for t in ts_:
                    n = P if t < 2 else NB
                    for c in range(2):
                        o = start("h2", t, c)
                        for j in range(4):
                            mm = turn(o[0:n, P * j:P * j + P], h2T[:, 4 * c + j, P * t:P * t + n])
                        done(mm, "h2", t, c)

            h2_turned((0, 1))
            o = start("rank")
            pe.wait_ge(sem("mask_done"), 1)
            pe.wait_ge(sem("iota_ready"), 1)
            pe.matmul(o[:, 0:E], tri[:, :], msk[:, 0, :], start=True, stop=True)
            pe.matmul(o[:, E:2 * E], ones, msk[:, 0, :], start=True, stop=False)
            pe.matmul(o[:, E:2 * E], tri[:, :], msk[:, 1, :], start=False, stop=True)
            pe.matmul(o[0:NB, 2 * E:3 * E], ones[:, 0:NB], msk[:, 0, :], start=True, stop=False)
            pe.matmul(o[0:NB, 2 * E:3 * E], ones[:, 0:NB], msk[:, 1, :], start=False, stop=False)
            mm = pe.matmul(o[0:NB, 2 * E:3 * E], tri[0:NB, 0:NB], msk[0:NB, 2, :], start=False, stop=True)
            done(mm, "rank")
            o = start("cnt")
            pe.matmul(o[0:1, 0:E], ones[:, 0:1], msk[:, 0, :], start=True, stop=False)
            pe.matmul(o[0:1, 0:E], ones[:, 0:1], msk[:, 1, :], start=False, stop=False)
            done(pe.matmul(o[0:1, 0:E], ones[0:NB, 0:1], msk[0:NB, 2, :], start=False, stop=True), "cnt")
            h2_turned((2,))
            for c in range(2):
                o = start("g2", c)
                for j in range(4):
                    mm = turn(o[0:NROW, P * j:P * j + P], modT[:, 40 + 4 * c + j, :])
                done(mm, "g2", c)
            assert pos[0] == len(order)

            for b in range(8):
                pe.wait_ge(bank_out[b], taken[b])

            def y_bias():
                pe.wait_ge(sem("gt_copied"), 1)
                pe.wait_ge(sem("ld_bdown"), 16)
                pe.wait_ge(sem("x_copied"), 2)
                pe.wait_ge(sem("xt_copied"), 2)
                pe.wait_ge(sem("pt_copied"), 2)
                for k in range(4):
                    t, h = k // 2, k % 2
                    pe.matmul(ps[bias_bank[k]][:, :], gtT[0:E, P * t:P * t + P], bd[0:E, 512 * h:512 * h + 512],
                              start=True, stop=True).then_inc(sem("y_bias"), 1)
                for h in range(2):
                    mm = pe.matmul(ps[bias_bank[4]][64 * h:64 * h + NB, :], gtT[0:E, T:NT], bd[0:E, 512 * h:512 * h + 512],
                                   start=True, stop=True)
                mm.then_inc(sem("y_bias"), 1)

            def gates_turned():
                pe.wait_ge(sem("gatew_done"), 1)
                pe.wait_ge(sem("router_done"), 1)
                turn(ps[7][0:E, 0:128], gatew[:, 0, :])
                turn(ps[7][0:E, 128:256], gatew[:, 1, :])
                turn(ps[7][0:E, 256:NT], gatew[0:NB, 2, :]).then_inc(sem("gt_turned"), 1)

            def gather(n, buf):
                pe.wait_ge(sem("selected"), 4 * n + 4)
                if not isinstance(n, int) or n > 0:
                    pe.wait_ge(sem("x_copied"), n)
                for t in range(3):
                    m = P if t < 2 else NB
                    for h in range(2):
                        mm = pe.matmul(ps[2][64 * h:64 * h + 64, :], Psel[buf][0:m, t, 0:64],
                                       h2tok[0:m, t, 512 * h:512 * h + 512], start=(t == 0), stop=(t == 2))
                mm.then_inc(sem("gathered"), 1)

            def turn_rows(n):
                pe.wait_ge(sem("x_copied"), n + 1)
                if not isinstance(n, int) or n > 0:
                    pe.wait_ge(sem("at_copied"), n)
                for j in range(4):
                    mm = turn(ps[3][:, P * j:P * j + P], Xg[:, P * j:P * j + P])
                mm.then_inc(sem("x_turned"), 1)

            def product(bank_, lhsT, w, bias, buf, name, loaded, t):
                if bias is not None:
                    for h in range(2):
                        pe.matmul(bank_[64 * h:64 * h + 64, :], selb[buf][0:E, :],
                                  bias[0:E, 512 * h:512 * h + 512], start=True, stop=False)
                for k in range(DC):
                    if k % 4 == 0:
                        loaded(t, k // 4)
                    s0 = P * (k % 4) + 64 * (k // 4)
                    for h in range(2):
                        mm = pe.matmul(bank_[64 * h:64 * h + 64, :], lhsT[:, s0:s0 + 64],
                                       w[:, k, 512 * h:512 * h + 512],
                                       start=(bias is None and k == 0), stop=(k == DC - 1))
                    if k == 3:
                        mm.then_inc(sem(name + "_half"), 1)
                mm.then_inc(sem(name + "_done"), 1)

            def gate_up(n, buf, slot, loaded):
                pe.wait_ge(sem("xt_copied"), n + 1)
                if isinstance(n, int) and n == 0:
                    pe.wait_ge(sem("ld_bias"), 32)
                else:
                    pe.wait_ge(sem("g_read"), n)
                product(ps[0], XTg, wslot[slot[0]], bg, buf, "gate", loaded, 0)
                if not isinstance(n, int) or n > 0:
                    pe.wait_ge(sem("u_read"), n)
                product(ps[1], XTg, wslot[slot[1]], bu, buf, "up", loaded, 1)

            def turn_act(n):
                pe.wait_ge(sem("act_ready"), n + 1)
                pe.wait_ge(sem("xt_copied"), n + 1)
                for j in range(4):
                    mm = turn(ps[3][:, P * j:P * j + P], a_sb[:, P * j:P * j + P])
                mm.then_inc(sem("act_turned"), 1)

            def turn_places(n, buf):
                if not isinstance(n, int) or n > 0:
                    pe.wait_ge(sem("pt_copied"), 2 * n)
                for t in range(3):
                    m = P if t < 2 else NB
                    mm = turn(ps[4][:, P * t:P * t + m], Psel[buf][0:m, t, :])
                mm.then_inc(sem("pt_turned"), 1)

            def down(n, slot, loaded):
                pe.wait_ge(sem("at_copied"), n + 1)
                if not isinstance(n, int) or n > 0:
                    pe.wait_ge(sem("out_copied"), n)
                product(ps[5], aT_sb, wslot[slot[2]], None, 0, "down", loaded, 2)

            def scatter(n, between=lambda k: None):
                pe.wait_ge(sem("out_copied"), n + 1)
                pe.wait_ge(sem("pt_copied"), 2 * n + 2)
                for k in range(4):
                    t, h = k // 2, k % 2
                    if k < 2:
                        if isinstance(n, int) and n == 0:
                            pe.wait_ge(sem("y_started"), 5)
                        else:
                            pe.wait_ge(sem("y_added"), 6 * n)
                    else:
                        pe.wait_ge(sem("y_added"), 6 * n + k - 1)
                    pe.matmul(ps[6 + k % 2][:, :], PTz[h][:, P * t:P * t + P], o_sb[:, :], start=True, stop=True)\
                      .then_inc(sem("scattered"), 1)
                    between(k)
                pe.wait_ge(sem("y_added"), 6 * n + 3)
                for h in range(2):
                    mm = pe.matmul(ps[6][64 * h:64 * h + NB, :], PTz[h][:, T:NT], o_sb[:, :], start=True, stop=True)
                mm.then_inc(sem("scattered"), 1)

            def slots_of(r):
                return [(3 * r + t) % 4 for t in range(3)]

            def loaded_of(rounds, r):
                def loaded(t, half):
                    pe.wait_ge(sem(f"w_loaded{(3 * r + t) % 4}_{half}"), 48 * rounds + 16 * ((3 * r + t) // 4 + 1))
                return loaded

            def block_step(n, rounds, r, first=False, last=False):
                gate_up(n, r % 2, slots_of(r), loaded_of(rounds, r))
                if first:
                    gates_turned()
                elif last:
                    scatter(n - 1, between=lambda k: turn_act(n) if k == 1 else None)
                else:
                    scatter(n - 1)
                if not last:
                    gather(n + 1, (r + 1) % 2)
                    turn_act(n)
                turn_places(n, r % 2)
                if not last:
                    turn_rows(n + 1)
                down(n, slots_of(r), loaded_of(rounds, r))
                if first:
                    y_bias()

            gather(0, 0)
            turn_rows(0)
            for r in range(4):
                block_step(r, 0, r, first=(r == 0))
            with pe.Fori(1, E // 4 - 1) as i:
                for r in range(4):
                    block_step(4 * i + r, i, r)
            for r in range(4):
                block_step(E - 4 + r, E // 4 - 1, r, last=(r == 3))
            pe.wait_ge(sem("ld_end"), 32)
            pe.wait_ge(sem("u_read"), E)
            pe.wait_ge(sem("x_copied"), E)
            pe.wait_ge(sem("at_copied"), E)
            pe.wait_ge(sem("pt_copied"), 2 * E)

            def x1_turned(k):
                t, c = k // 2, k % 2
                n = P if t < 2 else NB
                if k >= 5:
                    pe.wait_ge(sem("x1_copied"), k - 4)
                for j in range(4):
                    mm = turn(ps[x1_bank[k]][0:n, P * j:P * j + P], x1o[:, 4 * c + j, P * t:P * t + n])
                mm.then_inc(sem("x1_turned"), 1)

            scatter(E - 1, between=x1_turned)
            x1_turned(4)
            x1_turned(5)
            nreg = pe.alloc_register("pe_block")
            c = pe.alloc_register("pe_over")
            pe.wait_ge(sem("router_done"), 1)
            pe.reg_load(c, cnt_i[0:1, (OVER + 1) * E:(OVER + 1) * E + 1])
            with pe.If(pe.snap(c) > 0):
                pe.wait_ge(sem("x1_copied"), 6)
                pe.reg_mov(nreg, E)
                with pe.Fori(1, OVER + 1) as b:
                    with pe.Fori(0, E) as e:
                        pe.reg_load(c, cnt_i[0:1, bass.ds(b * E + e, 1)])
                        with pe.If(pe.snap(c) > 0):
                            n = pe.snap(nreg)

                            def again(t, half):
                                pe.wait_ge(sem("w_again"), 96 * (n - E) + 96)

                            gather(n, 0)
                            turn_rows(n)
                            gate_up(n, 0, [1, 2, 3], again)
                            turn_act(n)
                            turn_places(n, 0)
                            down(n, [1, 2, 3], again)
                            scatter(n)
                            pe.reg_add(nreg, nreg, 1)
                        pe.nop()
                pe.nop()
            pe.nop()


INPUTS = ["x_prompt", "x_sample", "c_prompt", "c_sample", "state_wkv", "state_shift", "state_conv", "state_lru",
          "w_ada", "b_ada", "norm1_g", "norm2_g", "w_in", "rk_mu", "rk_w0", "rk_w_up", "rk_a0", "rk_a_up",
          "rk_g_up", "rk_k_k", "rk_k_a", "rk_r_k", "rk_lnx_w", "rk_lnx_b", "lru_conv_w", "lru_conv_b",
          "lru_w_r", "lru_b_r", "lru_w_i", "lru_b_i", "lru_lambda", "lru_norm_g", "w_out", "router_w",
          "router_b", "w_gate", "b_gate", "w_up", "b_up", "w_down", "b_down", "final_g"]
OUTPUTS = [("y_prompt", (1, T, D)), ("y_sample", (NB, 1, D)), ("wkv_prompt", (1, 1, H, HN, HN)),
           ("shift_prompt", (1, 1, MA * P)), ("conv_prompt", (1, 1, 3, DA)), ("lru_prompt", (1, 1, DA)),
           ("wkv_sample", (1, NB, H, HN, HN)), ("shift_sample", (1, NB, MA * P)),
           ("conv_sample", (1, NB, 3, DA)), ("lru_sample", (1, NB, DA))]


def kernel(**inputs):
    import numpy as _np
    import concourse.bacc as _bacc
    from concourse import mybir as _mybir
    from concourse.bass_utils import run_bass_kernel_spmd as _run

    nc = _bacc.Bacc("TRN2", target_bir_lowering=False, num_devices=1)
    arrays, ins, outs = {}, {}, {}
    for name in INPUTS:
        a = _np.ascontiguousarray(inputs[name])
        arrays[f"in_{name}_dram"] = a
        ins[name] = nc.dram_tensor(f"in_{name}_dram", a.shape, _mybir.dt.from_np(a.dtype), kind="ExternalInput").ap()
    for name, shape in OUTPUTS:
        outs[name] = nc.dram_tensor(f"out_{name}_dram", shape, _mybir.dt.float32, kind="ExternalOutput").ap()
    build(nc, ins, outs)
    r = _run(nc, [arrays], core_ids=[0])
    return tuple(r.results[0][f"out_{name}_dram"] for name, _ in OUTPUTS)
```
